# Optimizing a Trainium2 kernel written in Bass

```python
import jax, jax.numpy as jnp
from jax import lax
import numpy as np

D_MODEL = 1024
BATCH = 1
SEQ = 256
DEPTH = 1

SSM_EXPAND = 2
SSM_D_INNER = SSM_EXPAND * D_MODEL
SSM_HEAD_DIM = 64
SSM_HEADS = SSM_D_INNER // SSM_HEAD_DIM
SSM_GROUPS = 4
SSM_STATE = 128
SSM_CONV = 4
SSM_CHUNK = 128
SSM_CONV_DIM = SSM_D_INNER + 2 * SSM_GROUPS * SSM_STATE
ATT_HEADS = 16
ATT_HEAD_DIM = 64
ATT_WIDTH = ATT_HEADS * ATT_HEAD_DIM
IDX_HEADS = 8
IDX_HEAD_DIM = 64
TOPK_MAX = 256
Q_BLOCK = 128
NEG_INF = -1e30
MEM_LEN = 256
X_HEADS = 4
X_HEAD_DIM = D_MODEL // X_HEADS
MOE_GROUPS = 4
MOE_EXPERTS_PER_GROUP = 8
MOE_EXPERTS = MOE_GROUPS * MOE_EXPERTS_PER_GROUP
MOE_TOPK = 2
MOE_HIDDEN = 512
EPS = 1e-6

IN_SPLIT_SIZES = (SSM_D_INNER, SSM_CONV_DIM, SSM_HEADS,
                  ATT_WIDTH, ATT_HEAD_DIM, ATT_HEAD_DIM,
                  IDX_HEADS * IDX_HEAD_DIM, IDX_HEAD_DIM, IDX_HEADS,
                  D_MODEL, D_MODEL)
D_IN_PROJ = sum(IN_SPLIT_SIZES)

kernel_name = "hybrid_ssd_dsa_hmoe_block"

def _split_points():
    pts, acc = [], 0
    for s in IN_SPLIT_SIZES[:-1]:
        acc += s
        pts.append(acc)
    return pts

def rms_norm(x, g):
    xf = x.astype(jnp.float32)
    y = xf * lax.rsqrt(jnp.mean(xf * xf, axis=-1, keepdims=True) + EPS)
    return (y * g.astype(jnp.float32)).astype(x.dtype)

def causal_dwconv(x, w, bias):
    k = w.shape[1]
    xp = jnp.pad(x, ((0, 0), (k - 1, 0), (0, 0)))
    rhs = jnp.transpose(w)[:, None, :].astype(x.dtype)
    y = lax.conv_general_dilated(xp, rhs, window_strides=(1,), padding='VALID',
                                 dimension_numbers=('NWC', 'WIO', 'NWC'),
                                 feature_group_count=x.shape[-1])
    return y + bias.astype(x.dtype)

def ssd_chunked(xh, dt, a, bm, cm):
    b, l, h, p = xh.shape
    g, n = bm.shape[2], bm.shape[3]
    kh = h // g
    c = l // SSM_CHUNK
    q = SSM_CHUNK
    x = xh.reshape(b, c, q, g, kh, p)
    dt = dt.reshape(b, c, q, g, kh)
    bc = bm.reshape(b, c, q, g, n)
    cc = cm.reshape(b, c, q, g, n)
    a_cs = jnp.cumsum(dt * a.reshape(g, kh), axis=2)
    xdt = x * dt[..., None]
    seg = a_cs[:, :, :, None] - a_cs[:, :, None, :]
    causal = jnp.tril(jnp.ones((q, q), dtype=bool))[:, :, None, None]
    lmat = jnp.exp(jnp.where(causal, seg, -jnp.inf))
    cb = jnp.einsum('bctgn,bcsgn->bctsg', cc, bc)
    y_diag = jnp.einsum('bctsg,bctsgk,bcsgkp->bctgkp', cb, lmat, xdt)
    decay_states = jnp.exp(a_cs[:, :, -1:] - a_cs)
    states = jnp.einsum('bcsgn,bcsgk,bcsgkp->bcgkpn', bc, decay_states, xdt)
    chunk_decay = jnp.exp(a_cs[:, :, -1])

    def step(hprev, inp):
        st, dec = inp
        return hprev * dec[..., None, None] + st, hprev

    h0 = jnp.zeros((b, g, kh, p, n), jnp.float32)
    _, states_in = lax.scan(step, h0, (jnp.moveaxis(states, 1, 0), jnp.moveaxis(chunk_decay, 1, 0)))
    states_in = jnp.moveaxis(states_in, 0, 1)
    y_off = jnp.einsum('bctgn,bcgkpn,bctgk->bctgkp', cc, states_in, jnp.exp(a_cs))
    return (y_diag + y_off).reshape(b, l, h, p)

def ssm_branch(z, xbc, dt_raw, conv_w, conv_b, dt_bias, a_log, d_skip, ssm_norm):
    b, l, _ = z.shape
    xbc = jax.nn.silu(causal_dwconv(xbc, conv_w, conv_b))
    xs, bm, cm = jnp.split(xbc, [SSM_D_INNER, SSM_D_INNER + SSM_GROUPS * SSM_STATE], axis=-1)
    xh = xs.reshape(b, l, SSM_HEADS, SSM_HEAD_DIM).astype(jnp.float32)
    bm = bm.reshape(b, l, SSM_GROUPS, SSM_STATE).astype(jnp.float32)
    cm = cm.reshape(b, l, SSM_GROUPS, SSM_STATE).astype(jnp.float32)
    dt = jax.nn.softplus(dt_raw.astype(jnp.float32) + dt_bias.astype(jnp.float32))
    a = -jnp.exp(a_log.astype(jnp.float32))
    y = ssd_chunked(xh, dt, a, bm, cm) + d_skip.astype(jnp.float32)[:, None] * xh
    y = y.reshape(b, l, SSM_D_INNER).astype(z.dtype)
    return rms_norm(y * jax.nn.silu(z), ssm_norm)

def dsa_branch(q, k, v, qi, ki, wi):
    b, l, _ = q.shape
    topk = min(TOPK_MAX, l // 4)
    nb = l // Q_BLOCK
    q = q.reshape(b, nb, Q_BLOCK, ATT_HEADS, ATT_HEAD_DIM)
    qi = qi.reshape(b, nb, Q_BLOCK, IDX_HEADS, IDX_HEAD_DIM).astype(jnp.float32)
    wi = wi.reshape(b, nb, Q_BLOCK, IDX_HEADS).astype(jnp.float32) * (IDX_HEADS ** -0.5 * IDX_HEAD_DIM ** -0.5)
    kif = ki.astype(jnp.float32)
    slopes = jnp.exp2(-8.0 * jnp.arange(1, ATT_HEADS + 1, dtype=jnp.float32) / ATT_HEADS)
    spos = jnp.arange(l)
    gather = jax.vmap(lambda arr, ix: arr[ix])

    def block(args):
        blk, qb, qib, wib = args
        tpos = blk * Q_BLOCK + jnp.arange(Q_BLOCK)
        rel = jax.nn.relu(jnp.einsum('bthd,bsd->bths', qib, kif))
        iscore = jnp.einsum('bths,bth->bts', rel, wib)
        iscore = jnp.where(spos[None, None, :] <= tpos[None, :, None], iscore, NEG_INF)
        _, idx = lax.top_k(iscore, topk)
        ksel = gather(k, idx)
        vsel = gather(v, idx)
        s = jnp.einsum('bthd,btkd->bthk', qb, ksel).astype(jnp.float32) * (ATT_HEAD_DIM ** -0.5)
        dist = (tpos[None, :, None] - idx).astype(jnp.float32)
        s = s - slopes[:, None] * dist[:, :, None, :]
        valid = (idx <= tpos[None, :, None])[:, :, None, :]
        s = jnp.where(valid, s, -jnp.inf)
        p = jax.nn.softmax(s, axis=-1).astype(v.dtype)
        return jnp.einsum('bthk,btkd->bthd', p, vsel)

    xs = (jnp.arange(nb), jnp.moveaxis(q, 1, 0), jnp.moveaxis(qi, 1, 0), jnp.moveaxis(wi, 1, 0))
    o = lax.map(block, xs)
    return jnp.moveaxis(o, 0, 1).reshape(b, l, ATT_WIDTH)

def cross_attention(hn, mn, w_xq, w_xkv, w_xo):
    b, l, _ = hn.shape
    m = mn.shape[1]
    q = (hn @ w_xq).reshape(b, l, X_HEADS, X_HEAD_DIM)
    kv = (mn @ w_xkv).reshape(b, m, 2, X_HEADS, X_HEAD_DIM)
    k, v = kv[:, :, 0], kv[:, :, 1]
    s = jnp.einsum('blhd,bmhd->bhlm', q, k).astype(jnp.float32) * (X_HEAD_DIM ** -0.5)
    p = jax.nn.softmax(s, axis=-1).astype(v.dtype)
    o = jnp.einsum('bhlm,bmhd->blhd', p, v).reshape(b, l, D_MODEL)
    return o @ w_xo

def hierarchical_moe(hn, w_rg, b_rg, w_re, b_re, w_e_gate, w_e_up, w_e_down):
    b, l, d = hn.shape
    t = hn.reshape(b * l, d)
    glog = (t @ w_rg).astype(jnp.float32) + b_rg.astype(jnp.float32)
    gprob = jax.nn.softmax(glog, axis=-1)
    g_sel = jnp.argmax(gprob, axis=-1)
    pg = jnp.max(gprob, axis=-1)
    elog = ((t @ w_re).astype(jnp.float32) + b_re.astype(jnp.float32)).reshape(-1, MOE_GROUPS, MOE_EXPERTS_PER_GROUP)
    elog_g = jnp.take_along_axis(elog, g_sel[:, None, None], axis=1)[:, 0, :]
    eprob = jax.nn.softmax(elog_g, axis=-1)
    topv, topi = lax.top_k(eprob, MOE_TOPK)
    wts = pg[:, None] * topv / jnp.sum(topv, axis=-1, keepdims=True)
    gid = g_sel[:, None] * MOE_EXPERTS_PER_GROUP + topi
    comb = jnp.sum(jax.nn.one_hot(gid, MOE_EXPERTS, dtype=jnp.float32) * wts[..., None], axis=1).astype(t.dtype)
    out = jnp.zeros_like(t)
    for e in range(MOE_EXPERTS):
        hid = jax.nn.silu(t @ w_e_gate[e]) * (t @ w_e_up[e])
        out = out + comb[:, e:e + 1] * (hid @ w_e_down[e])
    return out.reshape(b, l, d)

def hybrid_layer(x, mem, norm_mix, w_in, conv_w, conv_b, dt_bias, a_log, d_skip, ssm_norm,
                 w_ssm_out, w_att_out, w_mix_out, norm_x, norm_mem, w_xq, w_xkv, w_xo,
                 norm_moe, w_rg, b_rg, w_re, b_re, w_e_gate, w_e_up, w_e_down):
    u = rms_norm(x, norm_mix)
    proj = u @ w_in
    z, xbc, dt_raw, q, k, v, qi, ki, wi, g_ssm, g_att = jnp.split(proj, _split_points(), axis=-1)
    y_ssm = ssm_branch(z, xbc, dt_raw, conv_w, conv_b, dt_bias, a_log, d_skip, ssm_norm) @ w_ssm_out
    y_att = dsa_branch(q, k, v, qi, ki, wi) @ w_att_out
    mix = jax.nn.sigmoid(g_ssm) * y_ssm + jax.nn.sigmoid(g_att) * y_att
    x = x + mix @ w_mix_out
    x = x + cross_attention(rms_norm(x, norm_x), rms_norm(mem, norm_mem), w_xq, w_xkv, w_xo)
    x = x + hierarchical_moe(rms_norm(x, norm_moe), w_rg, b_rg, w_re, b_re, w_e_gate, w_e_up, w_e_down)
    return x

def setup_inputs(seed: int = 0) -> dict:
    key = jax.random.key(seed)
    ks = jax.random.split(key, 32)
    f32 = jnp.float32
    L = DEPTH

    def w(k, shape, fan_in):
        return jax.random.normal(k, shape, f32) * (fan_in ** -0.5)

    def gain(k, shape):
        return 1.0 + 0.02 * jax.random.normal(k, shape, f32)

    def small(k, shape, s=0.01):
        return s * jax.random.normal(k, shape, f32)

    u = jax.random.uniform(ks[7], (L, SSM_HEADS), f32)
    dt0 = jnp.exp(u * (np.log(0.1) - np.log(0.001)) + np.log(0.001)).astype(f32)
    dt_bias = dt0 + jnp.log(-jnp.expm1(-dt0))
    return {
        "x": jax.random.normal(ks[0], (BATCH, SEQ, D_MODEL), f32),
        "mem": jax.random.normal(ks[1], (BATCH, MEM_LEN, D_MODEL), f32),
        "norm_mix": gain(ks[2], (L, D_MODEL)),
        "w_in": w(ks[3], (L, D_MODEL, D_IN_PROJ), D_MODEL),
        "conv_w": w(ks[4], (L, SSM_CONV_DIM, SSM_CONV), SSM_CONV),
        "conv_b": small(ks[5], (L, SSM_CONV_DIM), 0.02),
        "dt_bias": dt_bias,
        "a_log": jnp.log(jax.random.uniform(ks[8], (L, SSM_HEADS), f32, 1.0, 16.0)),
        "d_skip": gain(ks[9], (L, SSM_HEADS)),
        "ssm_norm": gain(ks[10], (L, SSM_D_INNER)),
        "w_ssm_out": w(ks[11], (L, SSM_D_INNER, D_MODEL), SSM_D_INNER),
        "w_att_out": w(ks[12], (L, ATT_WIDTH, D_MODEL), ATT_WIDTH),
        "w_mix_out": w(ks[13], (L, D_MODEL, D_MODEL), D_MODEL),
        "norm_x": gain(ks[14], (L, D_MODEL)),
        "norm_mem": gain(ks[15], (L, D_MODEL)),
        "w_xq": w(ks[16], (L, D_MODEL, D_MODEL), D_MODEL),
        "w_xkv": w(ks[17], (L, D_MODEL, 2 * D_MODEL), D_MODEL),
        "w_xo": w(ks[18], (L, D_MODEL, D_MODEL), D_MODEL),
        "norm_moe": gain(ks[19], (L, D_MODEL)),
        "w_rg": w(ks[20], (L, D_MODEL, MOE_GROUPS), D_MODEL),
        "b_rg": small(ks[21], (L, MOE_GROUPS)),
        "w_re": w(ks[22], (L, D_MODEL, MOE_EXPERTS), D_MODEL),
        "b_re": small(ks[23], (L, MOE_EXPERTS)),
        "w_e_gate": w(ks[24], (L, MOE_EXPERTS, D_MODEL, MOE_HIDDEN), D_MODEL),
        "w_e_up": w(ks[25], (L, MOE_EXPERTS, D_MODEL, MOE_HIDDEN), D_MODEL),
        "w_e_down": w(ks[26], (L, MOE_EXPERTS, MOE_HIDDEN, D_MODEL), MOE_HIDDEN),
        "norm_final": gain(ks[27], (D_MODEL,)),
    }

def reference(x, mem, norm_mix, w_in, conv_w, conv_b, dt_bias, a_log, d_skip, ssm_norm,
              w_ssm_out, w_att_out, w_mix_out, norm_x, norm_mem, w_xq, w_xkv, w_xo,
              norm_moe, w_rg, b_rg, w_re, b_re, w_e_gate, w_e_up, w_e_down, norm_final):
    h = x
    for i in range(DEPTH):
        h = hybrid_layer(h, mem, norm_mix[i], w_in[i], conv_w[i], conv_b[i], dt_bias[i], a_log[i],
                         d_skip[i], ssm_norm[i], w_ssm_out[i], w_att_out[i], w_mix_out[i],
                         norm_x[i], norm_mem[i], w_xq[i], w_xkv[i], w_xo[i], norm_moe[i],
                         w_rg[i], b_rg[i], w_re[i], b_re[i], w_e_gate[i], w_e_up[i], w_e_down[i])
    return rms_norm(h, norm_final)


_drawn_inputs = setup_inputs


def setup_inputs(seed=0):
    import zlib

    import numpy as np

    out = dict(_drawn_inputs(seed))
    spreads = {}
    factors = {'d_skip': 3.249,
     'ssm_norm': 2.702,
     'norm_x': 8.0,
     'norm_mem': 4.717,
     'b_rg': 54.096,
     'b_re': 29.76,
     'norm_final': 9.703,
     'norm_moe': 7.197}
    for name, (base, spread) in spreads.items():
        noise = np.random.default_rng([zlib.crc32(name.encode()), seed]).standard_normal(out[name].shape)
        drawn = base * np.exp(spread * noise) if base else spread * noise
        out[name] = __import__('jax').numpy.asarray(drawn.astype(out[name].dtype))
    for name, factor in factors.items():
        out[name] = (out[name] * factor).astype(out[name].dtype)
    return out
```

```python
import concourse.bass as bass
from concourse import mybir
from contextlib import ExitStack

F32 = mybir.dt.float32
I32 = mybir.dt.int32
ACT = mybir.ActivationFunctionType
ALU = mybir.AluOpType
AXX = mybir.AxisListType.X

P = 128
SEQ, D = 256, 1024
NT = SEQ // P
KT = D // P
EPS = 1e-6
D_INNER, N_STATE, N_GROUPS, SSM_HEADS, HEAD = 2048, 128, 4, 32, 64
CONV_K = 4
ATT_HEADS, IDX_HEADS, TOPK = 16, 8, 64
X_HEADS = 4
EXPERTS, GROUPS, PER_GROUP, HID = 32, 4, 8, 512
CAP = 64
PAIRS = EXPERTS // 2
MAX_PASSES = SEQ // CAP
NEG = -1e30
TAKEN = -3e38
UNIT = 4096
RING = 4
MOE_RING = 6

C_Z, C_XS, C_B, C_C = 0, 2048, 4096, 4608
C_DT, C_Q, C_K, C_V, C_QI, C_KI, C_WI, C_GS, C_GA = 5120, 5152, 6176, 6240, 6304, 6816, 6880, 6888, 7912
SM_K, SM_V, SM_KI, SM_WI, SM_DT, SM_W = 0, 64, 128, 192, 200, 232
TM_W = SM_W - SM_V


def hybrid_block(nc, x, mem, norm_mix, w_in, conv_w, conv_b, dt_bias, a_log, d_skip, ssm_norm,
                 w_ssm_out, w_att_out, w_mix_out, norm_x, norm_mem, w_xq, w_xkv, w_xo, norm_moe,
                 w_rg, b_rg, w_re, b_re, w_e_gate, w_e_up, w_e_down, norm_final, out):
    ctx = ExitStack()
    with ctx:
        def sb(name, shape, dt=F32):
            return ctx.enter_context(nc.sbuf_tensor(name, shape, dt))

        def sem(name):
            return ctx.enter_context(nc.semaphore(name))

        ctx.enter_context(nc.allow_non_contiguous_dma(reason="a few small parameter vectors"))

        ring = sb("ring", [P, RING, UNIT])
        zs = sb("zs", [P, 16, SEQ])
        gates = sb("gates", [P, 16, SEQ])
        xdt = sb("xdt", [P, NT, D_INNER])
        ysT = sb("ysT", [P, 16, SEQ])
        bc = sb("bc", [P, 8, SEQ])
        cbm = sb("cbm", [P, N_GROUPS, 384])
        xres = sb("xres", [P, NT, D])
        uT = sb("uT", [P, KT, SEQ])
        qT = sb("qT", [P, 8, SEQ])
        qiT = sb("qiT", [P, 4, SEQ])
        kz = sb("kz", [P, 2, SEQ])
        kiz = sb("kiz", [P, 2, SEQ])
        small_tm = sb("small_tm", [P, NT, TM_W])
        isc = sb("isc", [P, 384])
        selm = sb("selm", [P, 384])
        dist = sb("dist", [P, 384])
        caus = sb("caus", [P, 384])
        work = sb("work", [P, 12, 384])
        ident = sb("ident", [P, P])
        tri = sb("tri", [P, P])
        ones = sb("ones", [P, P])
        iota64 = sb("iota64", [P, CAP])
        prm = sb("prm", [P, 512])
        wr = sb("wr", [P, KT, 36])
        st = sb("st", [P, 480])

        slot = [ring[:, s, :] for s in range(RING)]
        moe_slot = slot + [zs[:, :, :].rearrange("p a b -> p (a b)"), gates[:, :, :].rearrange("p a b -> p (a b)")]
        flat_xdt = xdt[:, :, :].rearrange("p a b -> p (a b)")
        flat_ys = ysT[:, :, :].rearrange("p a b -> p (a b)")
        flat_bc = bc[:, :, :].rearrange("p a b -> p (a b)")
        flat_work = work[:, :, :].rearrange("p a b -> p (a b)")
        flat_qi = qiT[:, :, :].rearrange("p a b -> p (a b)")
        xn0 = flat_xdt[:, 0:2048].rearrange("p (i d) -> p i d", i=NT)
        memx = flat_bc[:, :].rearrange("p (i d) -> p i d", i=NT)
        memn = flat_ys[:, 2048:4096].rearrange("p (i d) -> p i d", i=NT)
        memT = flat_ys[:, 0:2048].rearrange("p (k t) -> p k t", k=KT)
        kxT = flat_xdt[:, 0:2048].rearrange("p (k t) -> p k t", k=KT)
        vx = flat_xdt[:, 2048:4096].rearrange("p (i d) -> p i d", i=NT)
        xn1 = memn
        hxT = memT
        qxT = bc
        xn2 = memn
        tT = memT
        raw = flat_work[:, 0:3 * 260].rearrange("p (n w) -> p n w", n=3)
        cacc = flat_work[:, 780:780 + 512].rearrange("p (n w) -> p n w", n=2)
        rel = flat_work[:, 1536:1536 + 1536].rearrange("p (n w) -> p n w", n=2)
        prob = work[:, 0:4, :]
        probT = work[:, 4:6, :]
        albi = flat_qi[:, 0:768].rearrange("p (h w) -> p h w", h=2)
        seg = work[:, 0:4, :]
        mdec = work[:, 4:8, :]
        ysq = flat_work[:, 3072:3072 + 512].rearrange("p (n w) -> p n w", n=2)
        pX = flat_work[:, 0:2048].rearrange("p (n w) -> p n w", n=4)
        pXT = flat_work[:, 2048:3072].rearrange("p (n w) -> p n w", n=2)
        rs_bc = flat_work[:, 3584:3584 + 256]

        cw = prm[:, 0:96].rearrange("p (k b) -> p k b", k=CONV_K)
        cbias = prm[:, 96:120]
        sgain = prm[:, 120:136]
        g_mix, g_mem, g_x, g_moe = (prm[:, 136 + 8 * i:144 + 8 * i] for i in range(4))
        dskip = prm[:, 168:184]
        dtb = prm[:, 184:216]
        alog = prm[:, 216:248]
        brt = prm[:, 248:284]
        rev4 = prm[:, 284:288]
        rev32 = prm[:, 288:320]
        dt = prm[:, 320:384].rearrange("p (i h) -> p i h", i=NT)
        dA = prm[:, 384:448].rearrange("p (i h) -> p i h", i=NT)
        flat_cb = cbm[:, :, :].rearrange("p a b -> p (a b)")
        cwrow = flat_cb[0:24, 0:512]
        prow = flat_cb[0:40, 768:896]
        sel2 = sb("sel2", [2, P])
        drow = sb("drow", [2, 16])
        n_it = sb("n_it", [P, 2], I32)
        pos_all = sb("pos_all", [P, NT, MAX_PASSES * EXPERTS + 2])
        comb_all = flat_bc[:, 0:NT * (MAX_PASSES * EXPERTS + 2)].rearrange("p (i n) -> p i n", i=NT)
        bias3 = pos_all[:, 0, 0:96].rearrange("p (k h) -> p k h", k=3)

        xg = flat_xdt[:, 0:1024].rearrange("p (k j) -> p k j", k=KT)
        yj = flat_xdt[:, 1024:2048]
        hs = flat_xdt[:, 2048:2560]
        hh = flat_xdt[:, 2560:3072]
        hT = flat_xdt[:, 3072:3584].rearrange("p (k j) -> p k j", k=4)
        S = flat_work[:, 0:256].rearrange("p (i a j) -> p i a j", i=NT, a=2)
        Sw = flat_work[:, 256:512].rearrange("p (i a j) -> p i a j", i=NT, a=2)
        SwT = flat_work[:, 512:768].rearrange("p (i t) -> p i t", i=NT)
        gain_f = flat_work[:, 1024:2048]
        junk = flat_xdt[:, 0:2048].rearrange("p (n w) -> p n w", n=4)
        rt = flat_work[:, 3072:4096]
        outb = uT[:, :, :].rearrange("p a b -> p (a b)").rearrange("p (i d) -> p i d", i=NT)

        bank = [ctx.enter_context(nc.psum_tensor(f"bank{i}", [P, 512], F32)) for i in range(8)]
        acc_bank = [[bank[0], bank[1]], [bank[6], bank[7]]]

        landed = [sem(f"landed{s}") for s in range(RING)]
        moe_landed = [sem(f"moe_landed{s}") for s in range(MOE_RING)]
        x_in = sem("x_in")
        mem_in = sem("mem_in")
        prm_in = sem("prm_in")
        gainf_in = sem("gainf_in")
        consts = sem("consts")
        pool_chain = sem("pool_chain")
        act_chain = sem("act_chain")
        dve_chain = sem("dve_chain")
        ssq_done = sem("ssq_done")
        ms_ready = sem("ms_ready")
        rstd_done = sem("rstd_done")
        xn_ready = sem("xn_ready")
        tr_ready = sem("tr_ready")
        tr_evac = sem("tr_evac")
        prm_tr = sem("prm_tr")
        prm_ready = sem("prm_ready")
        proj_ready = sem("proj_ready")
        evac_act = sem("evac_act")
        evac_dve = sem("evac_dve")
        dt_exp_in, dt_exp, dt_ready = sem("dt_exp_in"), sem("dt_exp"), sem("dt_ready")
        idx_ready, idx_relu, idx_used = sem("idx_ready"), sem("idx_relu"), sem("idx_used")
        conv_done, conv_silu = sem("conv_done"), sem("conv_silu")
        cb_ready, cb_done = sem("cb_ready"), sem("cb_done")
        acs_ready, acs_done = sem("acs_ready"), sem("acs_done")
        xt_ready, xdt_done = sem("xt_ready"), sem("xdt_done")
        mask_ready = sem("mask_ready")
        albi_ready, sc_ready, sc_used, mx_ready, exp_done, pn_ready = (
            sem(n) for n in ("albi_ready", "sc_ready", "sc_used", "mx_ready", "exp_done", "pn_ready"))
        rcp_ready = sem("rcp_ready")
        pt_ready, pt_evac, pv_ready, pv_evac = (sem(n) for n in ("pt_ready", "pt_evac", "pv_ready", "pv_evac"))
        zsilu, gsig = sem("zsilu"), sem("gsig")
        r_ready, seg_ready, dec_ready, m_ready, y_ready, y_used = (
            sem(n) for n in ("r_ready", "seg_ready", "dec_ready", "m_ready", "y_ready", "y_used"))
        yg_ready, sq_ready, ssq_mm, yfin = sem("yg_ready"), sem("sq_ready"), sem("ssq_mm"), sem("yfin")
        gn_ms, gn_rstd = sem("gn_ms"), sem("gn_rstd")
        xs_ready, xmx_ready, xexp_done, xpn_ready, xpt_ready, xpt_evac, xo_ready, xo_evac = (
            sem(n) for n in ("xs_ready", "xmx_ready", "xexp_done", "xpn_ready", "xpt_ready", "xpt_evac",
                             "xo_ready", "xo_evac"))
        rl_ready, rexp_in, rexp_done, rmask, rpos = (
            sem(n) for n in ("rl_ready", "rexp_in", "rexp_done", "rmask", "rpos"))
        route_ready = sem("route_ready")
        m_sel, m_gath, m_xg, m_silu, m_h, m_tr, m_ht, m_st, m_y0, m_y1, m_sw = (
            sem("moe_" + n) for n in ("sel", "gathered", "xg", "silu", "h", "transposed", "hT", "swT", "y_act", "y_dve", "sw"))
        gate_used, up_used, down_used = sem("gate_used"), sem("up_used"), sem("down_used")
        moe_done, f_ssq, f_ms, f_rstd, f_out, stored = (
            sem(n) for n in ("moe_done", "f_ssq", "f_ms", "f_rstd", "f_out", "stored"))

        steps = (["k", "ki", "tm0", "tm1"] + [f"qi{b}" for b in range(4)] + [f"bc{b}" for b in range(8)]
                 + [f"xs{b}" for b in range(16)] + [f"q{b}" for b in range(8)] + [f"z{b}" for b in range(16)]
                 + [f"g{b}" for b in range(16)] + [f"kx{b}" for b in range(8)]
                 + [f"vx{c}{i}" for c in range(2) for i in range(NT)]
                 + [f"ao{b}" for b in range(8)] + [f"so{b}" for b in range(8)]
                 + [f"mo{c}{i}" for c in range(2) for i in range(NT)] + [f"qx{b}" for b in range(8)]
                 + [f"xo{c}{i}" for c in range(2) for i in range(NT)])
        STEP = {s: n for n, s in enumerate(steps)}
        by_dve = [s[:2] in ("ao", "so", "mo", "xo") for s in steps]

        def wait_evac(eng, name_or_n):
            n = STEP[name_or_n] if isinstance(name_or_n, str) else name_or_n
            if by_dve[n]:
                eng.wait_ge(evac_dve, sum(by_dve[:n + 1]))
            else:
                eng.wait_ge(evac_act, n + 1 - sum(by_dve[:n + 1]))

        def cols(w, c0, n):
            return w[0, :, c0:c0 + n].rearrange("(p t) n -> p t n", t=KT)

        units = [("small", None), ("qi", [cols(w_in, C_QI, 512)])]
        units += [(f"bc{j}", [cols(w_in, C_B + 512 * j, 512)]) for j in range(2)]
        units += [(f"xs{j}", [cols(w_in, C_XS + 512 * j, 512)]) for j in range(4)]
        units += [(f"q{j}", [cols(w_in, C_Q + 512 * j, 512)]) for j in range(2)]
        units += [(f"z{j}", [cols(w_in, C_Z + 512 * j, 512)]) for j in range(4)]
        units += [(f"g{j}", [cols(w_in, C_GS + 512 * j, 512)]) for j in range(4)]
        units += [(f"kv{j}", [cols(w_xkv, 512 * j, 512)]) for j in range(4)]
        units += [(f"ao{j}", [w_att_out[0, :, 512 * j:512 * j + 512].rearrange("(t p) n -> p t n", p=P)])
                  for j in range(2)]
        units += [(f"so{j}", [w_ssm_out[0, :, 256 * j:256 * j + 256].rearrange("(t p) n -> p t n", p=P)])
                  for j in range(4)]
        units += [(f"mo{j}", [w_mix_out[0, :, 512 * j:512 * j + 512].rearrange("(t p) n -> p t n", p=P)])
                  for j in range(2)]
        units += [(f"xq{j}", [cols(w_xq, 512 * j, 512)]) for j in range(2)]
        units += [(f"xo{j}", [w_xo[0, :, 512 * j:512 * j + 512].rearrange("(t p) n -> p t n", p=P)])
                  for j in range(2)]
        UN = {u: n for n, (u, _) in enumerate(units)}
        LAST_STEP = {"small": "tm1", "qi": "qi3"}
        for kind, per in (("bc", 4), ("xs", 4), ("q", 4), ("z", 4), ("g", 4), ("ao", 4), ("so", 2), ("xq", 4)):
            for j in range(8):
                LAST_STEP[f"{kind}{j}"] = ("qx" if kind == "xq" else kind) + str(per * j + per - 1)
        for j in range(2):
            LAST_STEP.update({f"kv{j}": f"kx{4 * j + 3}", f"kv{j + 2}": f"vx{j}1", f"mo{j}": f"mo{j}1",
                              f"xo{j}": f"xo{j}1"})
        SMALL_PARTS = [(SM_K, C_K, 128), (SM_KI, C_KI, 72), (SM_DT, C_DT, 32)]

        def unit_view(name, k):
            return slot[UN[name] % RING].rearrange("p (t n) -> p t n", t=k)

        small_w = slot[0][:, 0:KT * SM_W].rearrange("p (t n) -> p t n", t=KT)
        n_small_dma = len(SMALL_PARTS)

        def landed_value(n):
            return 16 * (n // RING + 1) + (16 * (n_small_dma - 1) if n % RING == 0 else 0)

        def wait_used(eng, n):
            eng.wait_ge(proj_ready, STEP[LAST_STEP[units[n][0]]] + 1)

        block = ctx.enter_context(nc.Block())

        @block.sync
        def _(sp):
            for i in range(NT):
                sp.dma_start(xres[:, i, :], x[0, P * i:P * i + P, :]).then_inc(x_in, 16)
            for n, (name, src) in enumerate(units):
                if n >= RING:
                    wait_used(sp, n - RING)
                if name == "small":
                    for d0, s0, w in SMALL_PARTS:
                        sp.dma_start(small_w[:, :, d0:d0 + w], cols(w_in, s0, w)).then_inc(landed[0], 16)
                else:
                    dst = slot[n % RING].rearrange("p (t n) -> p t n", t=src[0].shape[1])
                    sp.dma_start(dst, src[0]).then_inc(landed[n % RING], 16)
                if name == "kv3":
                    sp.wait_ge(cb_done, N_GROUPS)
                    for i in range(NT):
                        sp.dma_start(memx[:, i, :], mem[0, P * i:P * i + P, :]).then_inc(mem_in, 16)

            def load_experts(pair, first):
                for k, (w, used) in enumerate(((w_e_gate, gate_used), (w_e_up, up_used), (w_e_down, down_used))):
                    for a in range(2):
                        s = 2 * k + a
                        if first:
                            if s < RING:
                                wait_used(sp, max(n for n in range(len(units)) if n % RING == s))
                            elif s == RING:
                                wait_used(sp, UN["so3"])
                            else:
                                wait_evac(sp, "so7")
                        elif a == 0:
                            sp.wait_ge(used, pair[1])
                        e = 2 * pair[0] + a
                        t = HID * D // P // w.shape[3]
                        src = w[0:1, bass.ds(e, 1), :, :].rearrange("o e (p t) n -> p (o e t) n", p=P)
                        sp.dma_start(moe_slot[s].rearrange("p (t n) -> p t n", t=t), src)\
                            .then_inc(moe_landed[s], 16)

            load_experts((0, 0), True)
            with sp.Fori(1, PAIRS) as i:
                load_experts((i, i), False)
            sp.wait_ge(route_ready, 1)
            n_pass = sp.value_load(n_it[0:1, 1:2], min_val=1, max_val=MAX_PASSES)
            with sp.If(n_pass > 1):
                with sp.Fori(1, n_pass) as r:
                    with sp.Fori(0, PAIRS) as i:
                        load_experts((i, r * PAIRS + i), False)
            for i in range(NT):
                sp.wait_ge(f_out, i + 1)
                sp.dma_start(out[0, P * i:P * i + P, :], outb[:, i, :]).then_inc(stored, 16)
            sp.wait_ge(stored, 16 * NT)

        @block.gpsimd
        def _(pool):
            chain = [0]

            def link(ins):
                chain[0] += 1
                ins.then_inc(pool_chain, 1)
                pool.wait_ge(pool_chain, chain[0])

            link(nc.gpsimd.memset(ident[:, :], 0.0))
            link(nc.gpsimd.affine_select(out=ident[:, :], in_=ident[:, :], compare_op=ALU.not_equal, fill=1.0,
                                         base=0, pattern=[[-1, P]], channel_multiplier=1))
            link(nc.gpsimd.memset(ones[:, :], 1.0))
            link(nc.gpsimd.affine_select(out=tri[:, :], in_=ones[:, :], compare_op=ALU.is_ge, fill=0.0,
                                         base=0, pattern=[[1, P]], channel_multiplier=-1))
            link(nc.gpsimd.affine_select(out=sel2[:, :], in_=ones[0:2, :], compare_op=ALU.is_ge, fill=0.0,
                                         base=0, pattern=[[1, P]], channel_multiplier=-64))
            link(nc.gpsimd.affine_select(out=sel2[:, :], in_=sel2[:, :], compare_op=ALU.is_ge, fill=0.0,
                                         base=63, pattern=[[-1, P]], channel_multiplier=64))
            for d in (kz, kiz):
                link(nc.gpsimd.memset(d[0:64, 1, :], 0.0))
                link(nc.gpsimd.memset(d[64:128, 0, :], 0.0))
            for n in range(3):
                link(nc.gpsimd.memset(raw[:, n, 0:3], 0.0))
            nc.gpsimd.memset(st[:, :], 0.0).then_inc(consts, 1)
            link(nc.gpsimd.iota(dist[:, 0:128], pattern=[[-1, 128]], base=0, channel_multiplier=1,
                                allow_small_or_imprecise_dtypes=True))
            link(nc.gpsimd.iota(dist[:, 128:384], pattern=[[-1, 256]], base=128, channel_multiplier=1,
                                allow_small_or_imprecise_dtypes=True))
            link(nc.gpsimd.iota(iota64[:, :], pattern=[[1, CAP]], base=0, channel_multiplier=0,
                                allow_small_or_imprecise_dtypes=True))
            link(nc.gpsimd.iota(rev4, pattern=[[-1, GROUPS]], base=GROUPS, channel_multiplier=0,
                                allow_small_or_imprecise_dtypes=True))
            link(nc.gpsimd.iota(rev32, pattern=[[-1, EXPERTS]], base=EXPERTS, channel_multiplier=0,
                                allow_small_or_imprecise_dtypes=True))
            link(nc.gpsimd.memset(caus[:, :], 0.0))
            nc.gpsimd.affine_select(out=caus[:, 0:128], in_=caus[:, 0:128], compare_op=ALU.is_ge, fill=NEG,
                                    base=0, pattern=[[-1, 128]], channel_multiplier=1)
            nc.gpsimd.affine_select(out=caus[:, 128:384], in_=caus[:, 128:384], compare_op=ALU.is_ge, fill=NEG,
                                    base=128, pattern=[[-1, 256]], channel_multiplier=1).then_inc(consts, 1)

            def albi_tile(h):
                if h >= 2:
                    pool.wait_ge(sc_used, h - 1)
                slope = 2.0 ** (-8.0 * (h + 1) / ATT_HEADS)
                link(nc.gpsimd.tensor_scalar(albi[:, h % 2, :], dist[:, :], -slope, None, ALU.mult))
                nc.gpsimd.tensor_tensor(albi[:, h % 2, :], albi[:, h % 2, :], selm[:, :], ALU.add)\
                    .then_inc(albi_ready, 1)

            def normalise(h):
                pool.wait_ge(rcp_ready, h // 2 + 1)
                pb = prob[:, 2 * (h // 2 % 2) + h % 2, :]
                for i, (a, b) in enumerate(((0, 128), (128, 384))):
                    k = 96 + 4 * (h // 2 % 2) + 2 * (h % 2) + i
                    last = nc.gpsimd.tensor_scalar(pb[:, a:b], pb[:, a:b], st[:, k:k + 1], None, ALU.mult)
                last.then_inc(pn_ready, 1)

            pool.wait_ge(consts, 2)
            pool.wait_ge(mask_ready, 1)
            pool.wait_ge(idx_ready, 4)
            albi_tile(0)
            albi_tile(1)
            for b in range(ATT_HEADS // 2):
                if b + 1 < ATT_HEADS // 2:
                    albi_tile(2 * b + 2)
                    albi_tile(2 * b + 3)
                normalise(2 * b)
                normalise(2 * b + 1)

            def gate_y(b):
                pool.wait_ge(y_used, b + 1)
                if b == 0:
                    pool.wait_ge(zsilu, 1)
                nc.gpsimd.tensor_tensor(ysT[:, b, :], ysT[:, b, :], zs[:, b, :], ALU.mult).then_inc(yg_ready, 1)
                pool.wait_ge(yg_ready, b + 1)
                nc.gpsimd.tensor_scalar(zs[:, b, :], ysT[:, b, :], sgain[:, b:b + 1], None, ALU.mult)\
                    .then_inc(yfin, 1)

            pool.wait_ge(cb_done, N_GROUPS)
            pool.wait_ge(prm_ready, 2)
            for b in range(SSM_HEADS // 2):
                for a in range(2):
                    h = 2 * b + a
                    pool.wait_ge(dec_ready, h + 1)
                    if b >= 2:
                        pool.wait_ge(y_ready, b - 1)
                    nc.gpsimd.tensor_tensor(mdec[:, 2 * (b % 2) + a, :], seg[:, 2 * (b % 2) + a, :],
                                            cbm[:, h // 8, :], ALU.mult).then_inc(m_ready, 1)
                if b >= 1:
                    gate_y(b - 1)
            gate_y(SSM_HEADS // 2 - 1)

        @block.scalar
        def _(act):
            chain = [0]

            def link(ins):
                chain[0] += 1
                ins.then_inc(act_chain, 1)
                act.wait_ge(act_chain, chain[0])

            act.dma_start(prow[0:24, :], conv_b[0, :].rearrange("(b p) -> b p", p=P)).then_inc(prm_in, 16)
            act.dma_start(prow[24:40, :], ssm_norm[0, :].rearrange("(b p) -> b p", p=P)).then_inc(prm_in, 16)
            act.dma_start(cwrow, conv_w[0, :, :].rearrange("(b q) k -> b (q k)", q=P))\
                .then_inc(prm_in, 16)
            for d, s in ((g_mix, norm_mix), (g_mem, norm_mem), (g_x, norm_x), (g_moe, norm_moe)):
                act.dma_start(d, s[0, :].rearrange("(p t) -> p t", t=KT)).then_inc(prm_in, 16)
            act.dma_start(drow[:, :], d_skip[0, :].rearrange("(b a) -> a b", a=2)).then_inc(prm_in, 16)
            act.dma_start(dtb, dt_bias[0:1, :].to_broadcast([P, SSM_HEADS])).then_inc(prm_in, 16)
            act.dma_start(alog, a_log[0:1, :].to_broadcast([P, SSM_HEADS])).then_inc(prm_in, 16)
            act.dma_start(brt[:, 0:4], b_rg[0:1, :].to_broadcast([P, GROUPS])).then_inc(prm_in, 16)
            act.dma_start(brt[:, 4:36], b_re[0:1, :].to_broadcast([P, EXPERTS])).then_inc(prm_in, 16)
            act.dma_start(wr[:, :, 0:4], w_rg[0, :, :].rearrange("(p t) n -> p t n", t=KT)).then_inc(prm_in, 16)
            act.dma_start(wr[:, :, 4:36], w_re[0, :, :].rearrange("(p t) n -> p t n", t=KT)).then_inc(prm_in, 16)

            def norm_stats(n, src, junk_to):
                for i in range(NT):
                    last = nc.scalar.activation(junk_to[:, i, :], src[:, i, :], ACT.Square,
                                                accum_out=st[:, 4 * n + i:4 * n + i + 1])
                last.then_inc(ssq_done, 1)
                act.wait_ge(ms_ready, n + 1)
                nc.scalar.activation(st[:, 4 * n + 2:4 * n + 4], st[:, 4 * n + 2:4 * n + 4], ACT.Sqrt)\
                    .then_inc(rstd_done, 1)

            def evac(name, dst, scale=1.0, src=None):
                n = STEP[name]
                act.wait_ge(proj_ready, n + 1)
                src = bank[n % 2][:, 0:SEQ] if src is None else src
                nc.scalar.activation(dst, src, ACT.Copy, scale=scale).then_inc(evac_act, 1)

            act.wait_ge(x_in, 32)
            act.wait_ge(consts, 1)
            norm_stats(0, xres, xn0)

            for name, d in (("k", kz), ("ki", kiz)):
                n = STEP[name]
                act.wait_ge(proj_ready, n + 1)
                nc.scalar.activation(d[0:64, 0, :], bank[n % 2][0:64, 0:SEQ], ACT.Copy)
                nc.scalar.activation(d[64:128, 1, :], bank[n % 2][64:128, 0:SEQ], ACT.Copy).then_inc(evac_act, 1)
            for i in range(NT):
                n = STEP[f"tm{i}"]
                evac(f"tm{i}", small_tm[:, i, :], src=bank[n % 2][:, 0:TM_W])
            act.wait_ge(prm_in, 16 * 14)
            nc.scalar.activation(alog, alog, ACT.Exp)
            act.wait_ge(dt_exp_in, 1)
            nc.scalar.activation(st[:, 160:224], st[:, 160:224], ACT.Exp).then_inc(dt_exp, 1)

            def relu(b):
                act.wait_ge(idx_ready, b + 1)
                if b >= 2:
                    act.wait_ge(idx_used, b - 1)
                nc.scalar.activation(rel[:, b % 2, 0:256], bank[4][:, 0:256], ACT.Relu)
                nc.scalar.activation(rel[:, b % 2, 256:768], bank[5][:, :], ACT.Relu).then_inc(idx_relu, 1)

            for b in range(4):
                evac(f"qi{b}", qiT[:, b, :])
                if b >= 1:
                    relu(b - 1)
            relu(3)

            xbc = [f"bc{b}" for b in range(8)] + [f"xs{b}" for b in range(16)]

            def conv_out(n):
                act.wait_ge(conv_done, n + 1)
                dst = bc[:, n, :] if n < 8 else ysT[:, n - 8, :]
                nc.scalar.activation(dst, cacc[:, n % 2, :], ACT.Silu).then_inc(conv_silu, 1)

            for n, name in enumerate(xbc):
                if n >= 3:
                    act.wait_ge(conv_done, n - 2)
                evac(name, raw[:, n % 3, 3:259])
                if n >= 1:
                    conv_out(n - 1)
            conv_out(23)

            for b in range(8):
                evac(f"q{b}", qT[:, b, :], scale=HEAD ** -0.5)

            for b in range(8):
                evac(f"z{2 * b}", zs[:, 2 * b, :])
                act.wait_ge(mx_ready, b + 1)
                if b >= 2:
                    act.wait_ge(pt_ready, 2 * (b - 1))
                for a in range(2):
                    for i, (lo, hi) in enumerate(((0, 128), (128, 384))):
                        k = 2 * a + i
                        pb = prob[:, 2 * (b % 2) + a, lo:hi]
                        last = nc.scalar.activation(pb, pb, ACT.Exp, bias=st[:, 72 + 4 * (b % 2) + k:73 + 4 * (b % 2) + k],
                                                    accum_out=st[:, 80 + 4 * (b % 2) + k:81 + 4 * (b % 2) + k])
                last.then_inc(exp_done, 1)
                if b >= 1:
                    act.wait_ge(pv_ready, b)
                    nc.scalar.activation(qT[:, b - 1, :], bank[6 + (b - 1) % 2][:, 0:SEQ], ACT.Copy)\
                        .then_inc(pv_evac, 1)
                evac(f"z{2 * b + 1}", zs[:, 2 * b + 1, :])
            act.wait_ge(pv_ready, 8)
            nc.scalar.activation(qT[:, 7, :], bank[7][:, 0:SEQ], ACT.Copy).then_inc(pv_evac, 1)
            link(nc.scalar.activation(st[:, 470:471], st[:, 471:472], ACT.Copy))
            wait_evac(act, "z15")
            nc.scalar.activation(zs[:, :, :], zs[:, :, :], ACT.Silu).then_inc(zsilu, 1)

            def square_y(b):
                act.wait_ge(yg_ready, b + 1)
                if b >= 2:
                    act.wait_ge(ssq_mm, b - 1)
                nc.scalar.activation(ysq[:, b % 2, :], ysT[:, b, :], ACT.Square).then_inc(sq_ready, 1)

            for b in range(16):
                for a in range(2):
                    h = 2 * b + a
                    act.wait_ge(seg_ready, h + 1)
                    sg = seg[:, 2 * (b % 2) + a, :]
                    nc.scalar.activation(sg, sg, ACT.Exp).then_inc(dec_ready, 1)
                evac(f"g{b}", gates[:, b, :])
                if b >= 2:
                    square_y(b - 2)
            square_y(14)
            square_y(15)
            wait_evac(act, "g15")
            nc.scalar.activation(gates[:, :, :], gates[:, :, :], ACT.Sigmoid).then_inc(gsig, 1)

            act.wait_ge(gn_ms, 1)
            nc.scalar.activation(rs_bc, rs_bc, ACT.Sqrt).then_inc(gn_rstd, 1)
            act.wait_ge(mem_in, 32)
            act.wait_ge(yfin, 16)
            norm_stats(1, memx, memn)
            for b in range(8):
                evac(f"kx{b}", kxT[:, b, :])
            for c in range(2):
                for i in range(NT):
                    n = STEP[f"vx{c}{i}"]
                    evac(f"vx{c}{i}", vx[:, i, 512 * c:512 * c + 512], src=bank[n % 2][:, :])

            wait_evac(act, "mo11")
            norm_stats(2, xres, xn1)
            for b in range(8):
                evac(f"qx{b}", qxT[:, b, :], scale=(D // X_HEADS) ** -0.5)
            for h in range(X_HEADS):
                for i in range(NT):
                    n = NT * h + i
                    act.wait_ge(xmx_ready, n + 1)
                    if h >= 2:
                        act.wait_ge(xpt_ready, h - 1)
                    nc.scalar.activation(pX[:, 2 * (h % 2) + i, 0:256], bank[4 + i][:, 0:256], ACT.Exp,
                                         bias=st[:, 104 + n:105 + n],
                                         accum_out=st[:, 112 + n:113 + n]).then_inc(xexp_done, 1)
                if h >= 1:
                    for c in range(2):
                        act.wait_ge(xo_ready, 2 * (h - 1) + c + 1)
                        nc.scalar.activation(qT[:, 2 * (h - 1) + c, :], bank[6 + c][:, 0:SEQ], ACT.Copy)\
                            .then_inc(xo_evac, 1)
            for c in range(2):
                act.wait_ge(xo_ready, 2 * (X_HEADS - 1) + c + 1)
                nc.scalar.activation(qT[:, 2 * (X_HEADS - 1) + c, :], bank[6 + c][:, 0:SEQ], ACT.Copy)\
                    .then_inc(xo_evac, 1)
            wait_evac(act, "xo11")
            norm_stats(3, xres, xn2)
            act.wait_ge(rexp_in, 1)
            nc.scalar.activation(rt[:, 80:88], rt[:, 80:88], ACT.Exp).then_inc(rexp_done, 1)
            act.wait_ge(rexp_in, 2)
            nc.scalar.activation(rt[:, 96:98], rt[:, 96:98], ACT.Exp).then_inc(rexp_done, 1)
            act.wait_ge(xpt_ready, X_HEADS)
            act.dma_start(gain_f, norm_final.rearrange("(o d) -> o d", o=1).to_broadcast([P, D]))\
                .then_inc(gainf_in, 16)

            act.wait_ge(route_ready, 1)
            n_iter = act.value_load(n_it[0:1, 0:1], min_val=PAIRS, max_val=PAIRS * MAX_PASSES)
            with act.Fori(0, n_iter) as i:
                act.wait_ge(up_used, i + 1)
                nc.scalar.activation(hs, bank[4][:, :], ACT.Silu).then_inc(m_silu, 1)
                act.wait_ge(down_used, i + 1)
                nc.scalar.activation(yj[:, 0:512], bank[2][:, :], ACT.Copy).then_inc(m_y0, 1)
            act.wait_ge(moe_done, 1)
            for i in range(NT):
                for c in range(2):
                    last = nc.scalar.activation(junk[:, 2 * i + c, :], acc_bank[i][c][:, :], ACT.Square,
                                                accum_out=st[:, 128 + 2 * i + c:129 + 2 * i + c])
            last.then_inc(f_ssq, 1)
            act.wait_ge(f_ms, 1)
            nc.scalar.activation(st[:, 136:138], st[:, 136:138], ACT.Sqrt).then_inc(f_rstd, 1)

        @block.vector
        def _(dve):
            chain = [0]

            def link(ins):
                chain[0] += 1
                ins.then_inc(dve_chain, 1)
                dve.wait_ge(dve_chain, chain[0])

            tt, ts_, stt = nc.vector.tensor_tensor, nc.vector.tensor_scalar, nc.vector.scalar_tensor_tensor
            group = [0]

            def norm_apply(n, src, dst, gain, dstT):
                dve.wait_ge(ssq_done, n + 1)
                c = 4 * n
                link(ts_(st[:, c + 2:c + 4], st[:, c:c + 2], 1.0 / D, EPS, ALU.mult, ALU.add))
                nc.vector.reciprocal(st[:, c + 2:c + 4], st[:, c + 2:c + 4]).then_inc(ms_ready, 1)
                dve.wait_ge(rstd_done, n + 1)
                for i in range(NT):
                    ts_(dst[:, i, :], src[:, i, :], st[:, c + 2 + i:c + 3 + i], None, ALU.mult).then_inc(xn_ready, 1)
                for i in range(NT):
                    for q in range(2):
                        g = group[0]
                        dve.wait_ge(tr_ready, g + 1)
                        ps = bank[2 + g % 2][:, :].rearrange("p (k t) -> p k t", k=4)
                        gb = gain[:, 4 * q:4 * q + 4].unsqueeze(2).to_broadcast([P, 4, P])
                        tt(dstT[:, 4 * q:4 * q + 4, P * i:P * i + P], ps, gb, ALU.mult).then_inc(tr_evac, 1)
                        group[0] += 1

            dve.wait_ge(consts, 1)
            dve.wait_ge(prm_in, 16 * 14)
            norm_apply(0, xres, xn0, g_mix, uT)

            dve.wait_ge(prm_tr, 1)
            nc.vector.tensor_copy(prm[:, 0:136], bank[4][:, 0:136]).then_inc(prm_ready, 1)
            nc.vector.tensor_copy(dskip, bank[5][:, 0:16]).then_inc(prm_ready, 1)

            wait_evac(dve, "tm1")
            r = st[:, 224:288].rearrange("p (i h) -> p i h", i=NT)
            e1 = st[:, 160:224].rearrange("p (i h) -> p i h", i=NT)
            e2 = st[:, 288:352].rearrange("p (i h) -> p i h", i=NT)
            z2 = st[:, 352:416].rearrange("p (i h) -> p i h", i=NT)
            hb = dtb.unsqueeze(1).to_broadcast([P, NT, SSM_HEADS])
            link(tt(r, small_tm[:, :, SM_DT - SM_V:SM_DT - SM_V + SSM_HEADS], hb, ALU.add))
            link(ts_(dt, r, 0.0, None, ALU.max))
            stt(e1, dt, -2.0, r, ALU.mult, ALU.add).then_inc(dt_exp_in, 1)
            dve.wait_ge(dt_exp_in, 1)
            dve.wait_ge(dt_exp, 1)
            link(ts_(e1, e1, 0.0, None, ALU.add) if False else ts_(e2, e1, 2.0, None, ALU.add))
            link(nc.vector.reciprocal(e2, e2))
            link(tt(e1, e1, e2, ALU.mult))
            link(tt(z2, e1, e1, ALU.mult))
            link(ts_(e2, z2, 1.0 / 19, None, ALU.mult))
            for k in (17, 15, 13, 11, 9, 7, 5, 3):
                link(stt(e2, e2, 1.0 / k, z2, ALU.add, ALU.mult))
            link(stt(e2, e2, 1.0, e1, ALU.add, ALU.mult))
            link(stt(dt, e2, 2.0, dt, ALU.mult, ALU.add))
            stt(dA, dt, -1.0, alog.unsqueeze(1).to_broadcast([P, NT, SSM_HEADS]), ALU.mult, ALU.mult)\
                .then_inc(dt_ready, 1)
            link(ts_(small_tm[:, :, SM_WI - SM_V:SM_WI - SM_V + 8], small_tm[:, :, SM_WI - SM_V:SM_WI - SM_V + 8],
                     IDX_HEADS ** -0.5 * HEAD ** -0.5, None, ALU.mult))

            for b in range(4):
                dve.wait_ge(idx_relu, b + 1)
                for a in range(2):
                    h = 2 * b + a
                    for i, (lo, hi) in enumerate(((0, 128), (128, 384))):
                        w = hi - lo
                        src = rel[:, b % 2, 128 * a:128 * a + 128] if i == 0 else \
                            rel[:, b % 2, 256 + 256 * a:512 + 256 * a]
                        wi = small_tm[:, i, SM_WI - SM_V + h:SM_WI - SM_V + h + 1]
                        if h == 0:
                            link(ts_(isc[:, lo:hi], src, wi, None, ALU.mult))
                        elif h < 7 or i == 0:
                            link(stt(isc[:, lo:hi], src, wi, isc[:, lo:hi], ALU.mult, ALU.add))
                        else:
                            link(stt(isc[:, lo:hi], src, wi, isc[:, lo:hi], ALU.mult, ALU.add))
                nc.vector.tensor_copy(st[:, 472:473], st[:, 473:474]).then_inc(idx_used, 1)
            dve.wait_ge(consts, 2)
            link(stt(selm[:, :], caus[:, :], 0.0, isc[:, :], ALU.is_ge, ALU.mult))
            link(tt(isc[:, :], selm[:, :], caus[:, :], ALU.add))

            def topk_round(i):
                lo, hi = ((0, 128), (128, 384))[i]
                m8 = st[:, 416 + 8 * i:424 + 8 * i]
                link(nc.vector.max(out=m8, in_=isc[:, lo:hi]))
                link(nc.vector.match_replace(out=isc[:, lo:hi], in_to_replace=m8, in_values=isc[:, lo:hi],
                                             imm_value=TAKEN))

            def decay_and_cb():
                for g in range(N_GROUPS):
                    dve.wait_ge(cb_ready, g + 1)
                    ps = bank[4 + g % 2]
                    tt(cbm[:, g, 0:128], ps[:, 0:128], tri[:, :], ALU.mult)
                    nc.vector.tensor_copy(cbm[:, g, 128:256], ps[:, 128:256])
                    tt(cbm[:, g, 256:384], ps[:, 256:384], tri[:, :], ALU.mult).then_inc(cb_done, 1)
                dve.wait_ge(acs_ready, 1)
                ts_(bias3[:, 0, :], bank[6][:, 0:32], -1.0, None, ALU.mult)
                ts_(bias3[:, 2, :], bank[6][:, 32:64], -1.0, None, ALU.mult)
                nc.vector.tensor_copy(bias3[:, 1, :], bank[6][:, 64:96]).then_inc(acs_done, 1)
                dve.wait_ge(acs_done, 1)
                tt(bias3[:, 1, :], bias3[:, 1, :], bias3[:, 0, :], ALU.add).then_inc(acs_done, 1)

            dve.wait_ge(prm_ready, 2)
            for n in range(24):
                wait_evac(dve, STEP["bc0"] + n)
                if n >= 2:
                    dve.wait_ge(conv_silu, n - 1)
                rb, cbuf = raw[:, n % 3, :], cacc[:, n % 2, :]
                ch = n + 16 if n < 8 else n - 8
                link(ts_(cbuf, rb[:, 3:259], cw[:, 3, ch:ch + 1], cbias[:, ch:ch + 1], ALU.mult, ALU.add))
                for k in (2, 1):
                    link(stt(cbuf, rb[:, k:k + 256], cw[:, k, ch:ch + 1], cbuf, ALU.mult, ALU.add))
                stt(cbuf, rb[:, 0:256], cw[:, 0, ch:ch + 1], cbuf, ALU.mult, ALU.add).then_inc(conv_done, 1)
                if n < 2 * TOPK // 8:
                    topk_round(n % 2)
                if n == 15:
                    decay_and_cb()
            link(ts_(selm[:, :], isc[:, :], TAKEN, -1.0, ALU.is_equal, ALU.add))
            stt(selm[:, :], selm[:, :], -NEG, caus[:, :], ALU.mult, ALU.add).then_inc(mask_ready, 1)

            for i in range(NT):
                for q in range(4):
                    n = 4 * i + q
                    dve.wait_ge(xt_ready, n + 1)
                    ps = bank[2 + n % 2][:, :].rearrange("p (h c) -> p h c", c=HEAD)
                    d = xdt[:, i, 512 * q:512 * q + 512].rearrange("p (h c) -> p h c", c=HEAD)
                    tt(d, ps, dt[:, i, 8 * q:8 * q + 8].unsqueeze(2).to_broadcast([P, 8, HEAD]), ALU.mult)\
                        .then_inc(xdt_done, 1)

            def softmax_in(b):
                dve.wait_ge(sc_ready, b + 1)
                c = 72 + 4 * (b % 2)
                for a in range(2):
                    dve.wait_ge(albi_ready, 2 * b + a + 1)
                    pb = prob[:, 2 * (b % 2) + a, :]
                    if b >= 2:
                        dve.wait_ge(pt_ready, 2 * (b - 1))
                    tt(pb[:, 0:128], bank[4][:, 128 * a:128 * a + 128], albi[:, a, 0:128], ALU.add)
                    tt(pb[:, 128:384], bank[5][:, 256 * a:256 * a + 256], albi[:, a, 128:384], ALU.add)\
                        .then_inc(sc_used, 1)
                dve.wait_ge(sc_used, 2 * b + 2)
                for a in range(2):
                    pb = prob[:, 2 * (b % 2) + a, :]
                    nc.vector.tensor_reduce(out=st[:, c + 2 * a:c + 2 * a + 1], in_=pb[:, 0:128], axis=AXX,
                                            op=ALU.max, negate=True)
                    last = nc.vector.tensor_reduce(out=st[:, c + 2 * a + 1:c + 2 * a + 2], in_=pb[:, 128:384],
                                                   axis=AXX, op=ALU.max, negate=True)
                last.then_inc(mx_ready, 1)

            def sums(b):
                c = 80 + 4 * (b % 2)
                dve.wait_ge(exp_done, b + 1)
                nc.vector.reciprocal(st[:, c + 16:c + 20], st[:, c:c + 4]).then_inc(rcp_ready, 1)

            def probs_out(b):
                for a in range(2):
                    dve.wait_ge(pt_ready, 2 * b + a + 1)
                    if b >= 1:
                        dve.wait_ge(pv_ready, b)
                    nc.vector.tensor_copy(probT[:, a, :], bank[2 + a][:, 0:384]).then_inc(pt_evac, 1)

            for b in range(8):
                softmax_in(b)
                sums(b)
                probs_out(b)

            def y_out(b):
                dve.wait_ge(y_ready, b + 1)
                stt(ysT[:, b, :], ysT[:, b, :], dskip[:, b:b + 1], bank[6 + b % 2][:, 0:SEQ], ALU.mult, ALU.add)\
                    .then_inc(y_used, 1)

            for b in range(16):
                dve.wait_ge(r_ready, b + 1)
                if b == 0:
                    dve.wait_ge(pt_ready, 16)
                if b >= 2:
                    dve.wait_ge(m_ready, 2 * (b - 1))
                for a in range(2):
                    h = 2 * b + a
                    sg = seg[:, 2 * (b % 2) + a, :]
                    rr = bank[4 + b % 2][:, 256 * a:256 * a + 256]
                    ts_(sg[:, 0:128], rr[:, 0:128], bias3[:, 0, h:h + 1], 0.0, ALU.add, ALU.min)
                    ts_(sg[:, 128:256], rr[:, 128:256], bias3[:, 1, h:h + 1], 0.0, ALU.add, ALU.min)
                    ts_(sg[:, 256:384], rr[:, 128:256], bias3[:, 2, h:h + 1], 0.0, ALU.add, ALU.min)\
                        .then_inc(seg_ready, 1)
                if b >= 1:
                    y_out(b - 1)
            y_out(15)
            dve.wait_ge(ssq_mm, 16)
            link(ts_(rs_bc, bank[2][:, 0:SEQ], 1.0 / D_INNER, EPS, ALU.mult, ALU.add))
            nc.vector.reciprocal(rs_bc, rs_bc).then_inc(gn_ms, 1)

            norm_apply(1, memx, memn, g_mem, memT)
            dve.wait_ge(gsig, 1)
            for b in range(8):
                n = STEP[f"ao{b}"]
                dve.wait_ge(proj_ready, n + 1)
                tt(uT[:, b, :], bank[n % 2][:, 0:SEQ], gates[:, 8 + b, :], ALU.mult).then_inc(evac_dve, 1)
            dve.wait_ge(gn_rstd, 1)
            for b in range(8):
                n = STEP[f"so{b}"]
                link(tt(gates[:, b, :], gates[:, b, :], rs_bc, ALU.mult))
                dve.wait_ge(proj_ready, n + 1)
                link(tt(gates[:, b, :], bank[n % 2][:, 0:SEQ], gates[:, b, :], ALU.mult))
                tt(uT[:, b, :], uT[:, b, :], gates[:, b, :], ALU.add).then_inc(evac_dve, 1)

            def residual(prefix):
                for c in range(2):
                    for i in range(NT):
                        n = STEP[f"{prefix}{c}{i}"]
                        dve.wait_ge(proj_ready, n + 1)
                        d = xres[:, i, 512 * c:512 * c + 512]
                        tt(d, bank[n % 2][:, :], d, ALU.add).then_inc(evac_dve, 1)

            residual("mo")
            wait_evac(dve, "mo11")
            norm_apply(2, xres, xn1, g_x, hxT)

            for h in range(X_HEADS):
                for i in range(NT):
                    n = NT * h + i
                    dve.wait_ge(xs_ready, n + 1)
                    nc.vector.tensor_reduce(out=st[:, 104 + n:105 + n], in_=bank[4 + i][:, 0:256], axis=AXX,
                                            op=ALU.max, negate=True).then_inc(xmx_ready, 1)
                for i in range(NT):
                    n = NT * h + i
                    dve.wait_ge(xexp_done, n + 1)
                    link(nc.vector.reciprocal(st[:, 120 + n:121 + n], st[:, 112 + n:113 + n]))
                    pb = pX[:, 2 * (h % 2) + i, 0:256]
                    ts_(pb, pb, st[:, 120 + n:121 + n], None, ALU.mult).then_inc(xpn_ready, 1)
                dve.wait_ge(xpt_ready, h + 1)
                if h >= 1:
                    dve.wait_ge(xo_ready, 2 * h)
                nc.vector.tensor_copy(pXT[:, 0, 0:256], bank[2][:, 0:256])
                nc.vector.tensor_copy(pXT[:, 1, 0:256], bank[2][:, 256:512]).then_inc(xpt_evac, 1)
            residual("xo")
            wait_evac(dve, "xo11")
            norm_apply(3, xres, xn2, g_moe, tT)

            L = rt[:, 0:72].rearrange("p (i n) -> p i n", i=NT)
            dve.wait_ge(rl_ready, 1)
            link(tt(L, bank[4][:, 0:72].rearrange("p (i n) -> p i n", i=NT),
                    brt.unsqueeze(1).to_broadcast([P, NT, 36]), ALU.add))
            glog = L[:, :, 0:4]
            gmx = rt[:, 72:74]
            ge = rt[:, 80:88].rearrange("p (i n) -> p i n", i=NT)
            dexp = rt[:, 96:98]
            oh_g = rt[:, 88:96].rearrange("p (i n) -> p i n", i=NT)
            pg = rt[:, 74:76]
            v1, v2, tmp2 = rt[:, 76:78], rt[:, 78:80], rt[:, 98:100]
            em = rt[:, 104:168].rearrange("p (i n) -> p i n", i=NT)
            oh1 = rt[:, 168:232].rearrange("p (i n) -> p i n", i=NT)
            oh2 = rt[:, 232:296].rearrange("p (i n) -> p i n", i=NT)
            msk = rt[:, 296:360].rearrange("p (i n) -> p i n", i=NT)
            cmb = rt[:, 360:424].rearrange("p (i n) -> p i n", i=NT)
            pm = rt[:, 424:488].rearrange("p (i n) -> p i n", i=NT)

            def over(v, n):
                return v.unsqueeze(2).to_broadcast([P, NT, n])

            def first_max(dst, src, rev, n, vmax):
                link(nc.vector.tensor_reduce(out=vmax, in_=src, axis=AXX, op=ALU.max))
                link(tt(dst, src, over(vmax, n), ALU.is_equal))
                link(tt(dst, dst, rev.unsqueeze(1).to_broadcast([P, NT, n]), ALU.mult))
                link(nc.vector.tensor_reduce(out=tmp2, in_=dst, axis=AXX, op=ALU.max))
                link(tt(dst, dst, over(tmp2, n), ALU.is_equal))

            first_max(oh_g, glog, rev4, GROUPS, gmx)
            tt(ge, glog, over(gmx, GROUPS), ALU.subtract).then_inc(rexp_in, 1)
            link(ts_(oh2[:, :, 0:4], oh_g, -1.0, -NEG, ALU.add, ALU.mult))
            link(tt(em.rearrange("p i (g e) -> p i g e", g=GROUPS),
                    L[:, :, 4:36].rearrange("p i (g e) -> p i g e", g=GROUPS),
                    oh2[:, :, 0:4].unsqueeze(3).to_broadcast([P, NT, GROUPS, PER_GROUP]), ALU.add))
            first_max(oh1, em, rev32, EXPERTS, v1)
            link(stt(em, oh1, 3 * NEG, em, ALU.mult, ALU.add))
            first_max(oh2, em, rev32, EXPERTS, v2)
            tt(dexp, v2, v1, ALU.subtract).then_inc(rexp_in, 1)
            tt(msk, oh1, oh2, ALU.add).then_inc(rmask, 1)
            dve.wait_ge(rexp_done, 1)
            link(nc.vector.tensor_reduce(out=pg, in_=ge, axis=AXX, op=ALU.add))
            link(nc.vector.reciprocal(pg, pg))
            dve.wait_ge(rexp_done, 2)
            link(ts_(tmp2, dexp, 1.0, None, ALU.add))
            link(nc.vector.reciprocal(tmp2, tmp2))
            link(tt(v1, pg, tmp2, ALU.mult))
            link(tt(v2, v1, dexp, ALU.mult))
            link(tt(oh1, oh1, over(v1, EXPERTS), ALU.mult))
            link(tt(oh2, oh2, over(v2, EXPERTS), ALU.mult))
            link(tt(cmb, oh1, oh2, ALU.add))
            dve.wait_ge(rpos, 1)
            link(tt(pm, bank[5][:, 0:64].rearrange("p (i n) -> p i n", i=NT), msk, ALU.mult))
            link(nc.vector.memset(pos_all[:, :, MAX_PASSES * EXPERTS:], -1000.0))
            link(nc.vector.memset(comb_all[:, :, MAX_PASSES * EXPERTS:], 0.0))
            for k in range(MAX_PASSES):
                link(ts_(pos_all[:, :, EXPERTS * k:EXPERTS * k + EXPERTS], pm, -1.0 - CAP * k, None, ALU.add))
                link(nc.vector.tensor_copy(comb_all[:, :, EXPERTS * k:EXPERTS * k + EXPERTS], cmb))
            link(nc.vector.tensor_reduce(out=rt[:, 500:501], in_=bank[5][:, 64:96], axis=AXX, op=ALU.max))
            link(ts_(rt[:, 501:502], rt[:, 500:501], CAP + 0.5, 1.0, ALU.is_gt, ALU.add))
            for k in range(2, MAX_PASSES):
                link(stt(rt[:, 501:502], rt[:, 500:501], CAP * k + 0.5, rt[:, 501:502], ALU.is_gt, ALU.add))
            link(ts_(n_it[:, 0:1], rt[:, 501:502], float(PAIRS), None, ALU.mult))
            nc.vector.tensor_copy(n_it[:, 1:2], rt[:, 501:502]).then_inc(route_ready, 1)
            dve.wait_ge(route_ready, 1)

            iota_b = iota64[:, :].unsqueeze(1).to_broadcast([P, 2, CAP])

            def select(col):
                for i in range(NT):
                    pc = pos_all[:, i, bass.ds(col, 2)].unsqueeze(2).to_broadcast([P, 2, CAP])
                    last = tt(S[:, i, :, :], iota_b, pc, ALU.is_equal)
                last.then_inc(m_sel, 1)

            def gathered_out(n):
                dve.wait_ge(m_gath, n)
                for q in range(2):
                    gb = g_moe[:, 4 * q:4 * q + 4].unsqueeze(2).to_broadcast([P, 4, P])
                    last = tt(xg[:, 4 * q:4 * q + 4, :], bank[2 + q][:, :].rearrange("p (k j) -> p k j", k=4), gb,
                              ALU.mult)
                last.then_inc(m_xg, 1)

            n_iter = dve.value_load(n_it[0:1, 0:1], min_val=PAIRS, max_val=PAIRS * MAX_PASSES)
            select(0)
            gathered_out(1)
            with dve.Fori(0, n_iter) as it:
                dve.wait_ge(m_sel, it + 1)
                for i in range(NT):
                    cc = comb_all[:, i, bass.ds(2 * it, 2)].unsqueeze(2).to_broadcast([P, 2, CAP])
                    last = tt(Sw[:, i, :, :], S[:, i, :, :], cc, ALU.mult)
                last.then_inc(m_sw, 1)
                dve.wait_ge(m_sw, it + 1)
                select(2 * it + 2)
                dve.wait_ge(m_silu, it + 1)
                tt(hh, hs, bank[5][:, :], ALU.mult).then_inc(m_h, 1)
                gathered_out(it + 2)
                dve.wait_ge(m_tr, it + 1)
                nc.vector.tensor_copy(hT[:, :, :], bank[4][:, :].rearrange("p (k j) -> p k j", k=4)).then_inc(m_ht, 1)
                nc.vector.tensor_copy(SwT[:, :, :], bank[5][:, 0:256].rearrange("p (i t) -> p i t", i=NT))\
                    .then_inc(m_st, 1)
                dve.wait_ge(down_used, it + 1)
                nc.vector.tensor_copy(yj[:, 512:1024], bank[3][:, :]).then_inc(m_y1, 1)

            dve.wait_ge(f_ssq, 1)
            link(nc.vector.tensor_reduce(out=st[:, 136:138], in_=st[:, 128:132].rearrange("p (i c) -> p i c", c=2),
                                         axis=AXX, op=ALU.add))
            link(ts_(st[:, 136:138], st[:, 136:138], 1.0 / D, EPS, ALU.mult, ALU.add))
            nc.vector.reciprocal(st[:, 136:138], st[:, 136:138]).then_inc(f_ms, 1)
            dve.wait_ge(f_rstd, 1)
            dve.wait_ge(gainf_in, 16)
            for i in range(NT):
                for c in range(2):
                    last = stt(outb[:, i, 512 * c:512 * c + 512], acc_bank[i][c][:, :], st[:, 136 + i:137 + i],
                               gain_f[:, 512 * c:512 * c + 512], ALU.mult, ALU.mult)
                last.then_inc(f_out, 1)

        @block.tensor
        def _(pe):
            mm, tp = nc.tensor.matmul, nc.tensor.transpose
            group = [0]

            def use_unit(name):
                n = UN[name]
                pe.wait_ge(landed[n % RING], landed_value(n))

            def transposes(xn):
                for i in range(NT):
                    pe.wait_ge(xn_ready, group[0] // 2 + 1)
                    for q in range(2):
                        g = group[0]
                        if g >= 2:
                            pe.wait_ge(tr_evac, g - 1)
                        for k in range(4):
                            last = tp(bank[2 + g % 2][:, P * k:P * k + P], xn[:, i, 4 * q + k::KT], ident[:, :])
                        last.then_inc(tr_ready, 1)
                        group[0] += 1

            def bank_of(name):
                n = STEP[name]
                if n >= 2:
                    wait_evac(pe, n - 2)
                return bank[n % 2]

            def fm_step(name, w, c0, actT, nk=KT, last_of_unit=None):
                b = bank_of(name)
                for k in range(nk):
                    last = mm(b[:, 0:SEQ], w[:, k, c0:c0 + P], actT[:, k, :], start=(k == 0), stop=(k == nk - 1))
                last.then_inc(proj_ready, 1)

            def tm_step(name, w, c0, n_cols, actT, i):
                b = bank_of(name)
                for k in range(KT):
                    last = mm(b[:, 0:n_cols], actT[:, k, P * i:P * i + P], w[:, k, c0:c0 + n_cols],
                              start=(k == 0), stop=(k == KT - 1))
                last.then_inc(proj_ready, 1)

            pe.wait_ge(consts, 1)
            transposes(xn0)
            pe.wait_ge(prm_in, 16 * 14)
            for k in range(CONV_K):
                tp(bank[4][:, 24 * k:24 * k + 24], cwrow[:, k::CONV_K], ident[0:24, 0:24])
            tp(bank[4][:, 96:136], prow[:, :], ident[0:40, 0:40])
            mm(bank[5][:, 0:16], sel2[:, :], drow[:, :], start=True, stop=True).then_inc(prm_tr, 1)

            pe.wait_ge(tr_evac, 4)
            use_unit("small")
            for name, c0 in (("k", SM_K), ("ki", SM_KI)):
                b = bank_of(name)
                for k in range(KT):
                    for a in range(2):
                        last = mm(b[64 * a:64 * a + 64, 0:SEQ], small_w[:, k, c0:c0 + HEAD], uT[:, k, :],
                                  start=(k == 0), stop=(k == KT - 1))
                last.then_inc(proj_ready, 1)
            for i in range(NT):
                tm_step(f"tm{i}", small_w, SM_V, TM_W, uT, i)

            def indexer(b):
                wait_evac(pe, f"qi{b}")
                if b == 0:
                    pe.wait_ge(prm_ready, 2)
                else:
                    pe.wait_ge(idx_relu, b)
                mm(bank[4][:, 0:256].rearrange("p (a s) -> p a s", a=2), qiT[:, b, 0:P], kiz[:, :, 0:P],
                   start=True, stop=True)
                mm(bank[5][:, :].rearrange("p (a s) -> p a s", a=2), qiT[:, b, P:SEQ], kiz[:, :, :],
                   start=True, stop=True).then_inc(idx_ready, 1)

            use_unit("qi")
            w = unit_view("qi", KT)
            for b in range(4):
                fm_step(f"qi{b}", w, P * b, uT)
                if b >= 1:
                    indexer(b - 1)
            for j in range(2):
                use_unit(f"bc{j}")
                w = unit_view(f"bc{j}", KT)
                for c in range(4):
                    fm_step(f"bc{4 * j + c}", w, P * c, uT)
                    if j == 0 and c == 0:
                        indexer(3)
            for j in range(4):
                use_unit(f"xs{j}")
                w = unit_view(f"xs{j}", KT)
                for c in range(4):
                    fm_step(f"xs{4 * j + c}", w, P * c, uT)
                if j == 0:
                    pe.wait_ge(dt_ready, 1)
                    mm(bank[6][:, 0:32], tri[:, :], dA[:, 0, :], start=True, stop=True)
                    mm(bank[6][:, 32:64], tri[:, :], dA[:, 1, :], start=True, stop=True)
                    mm(bank[6][:, 64:96], ones[:, :], dA[:, 0, :], start=True, stop=True).then_inc(acs_ready, 1)
                if j == 1:
                    pe.wait_ge(conv_silu, 8)
                    pe.wait_ge(idx_relu, 4)
                    for g in range(N_GROUPS):
                        if g >= 2:
                            pe.wait_ge(cb_done, g - 1)
                        mm(bank[4 + g % 2][:, 0:256], bc[:, g, 0:P], bc[:, 4 + g, :], start=True, stop=True)
                        mm(bank[4 + g % 2][:, 256:384], bc[:, g, P:SEQ], bc[:, 4 + g, P:SEQ], start=True,
                           stop=True).then_inc(cb_ready, 1)
            for j in range(2):
                use_unit(f"q{j}")
                w = unit_view(f"q{j}", KT)
                for c in range(4):
                    fm_step(f"q{4 * j + c}", w, P * c, uT)
            for i in range(NT):
                for q in range(4):
                    n = 4 * i + q
                    pe.wait_ge(conv_silu, 24)
                    if n >= 2:
                        pe.wait_ge(xdt_done, n - 1)
                    for c in range(4):
                        last = tp(bank[2 + n % 2][:, P * c:P * c + P], ysT[:, 4 * q + c, P * i:P * i + P], ident[:, :])
                    last.then_inc(xt_ready, 1)

            def scores(b):
                wait_evac(pe, f"q{b}")
                if b == 0:
                    pe.wait_ge(cb_done, N_GROUPS)
                else:
                    pe.wait_ge(sc_used, 2 * b)
                mm(bank[4][:, 0:256].rearrange("p (a s) -> p a s", a=2), qT[:, b, 0:P], kz[:, :, 0:P],
                   start=True, stop=True)
                mm(bank[5][:, :].rearrange("p (a s) -> p a s", a=2), qT[:, b, P:SEQ], kz[:, :, :],
                   start=True, stop=True).then_inc(sc_ready, 1)

            def prob_transposes(b):
                for a in range(2):
                    pe.wait_ge(pn_ready, 2 * b + a + 1)
                    if b == 0:
                        pe.wait_ge(xdt_done, 8)
                    else:
                        pe.wait_ge(pt_evac, 2 * (b - 1) + a + 1)
                    pb = prob[:, 2 * (b % 2) + a, :]
                    for c in range(3):
                        last = tp(bank[2 + a][:, P * c:P * c + P], pb[:, P * c:P * c + P], ident[:, :])
                    last.then_inc(pt_ready, 1)

            def weighted_sum(dst, left0, left1, right):
                mm(dst[:, 0:256], left0, right[:, 0:256], start=True, stop=False, skip_group_check=True)
                return mm(dst[:, 128:256], left1, right[:, 256:384], start=False, stop=True, skip_group_check=True)

            def values(b):
                pe.wait_ge(pt_evac, 2 * b + 2)
                if b >= 2:
                    pe.wait_ge(pv_evac, b - 1)
                if b == 0:
                    pe.wait_ge(acs_done, 2)
                for a in range(2):
                    last = weighted_sum(bank[6 + b % 2][64 * a:64 * a + 64, :], small_tm[:, 0, 0:HEAD],
                                        small_tm[:, 1, 0:HEAD], probT[:, a, :])
                last.then_inc(pv_ready, 1)

            for b in range(8):
                scores(b)
                if b % 2 == 0:
                    use_unit(f"z{b // 2}")
                w = unit_view(f"z{b // 2}", KT)
                fm_step(f"z{2 * b}", w, 256 * (b % 2), uT)
                if b >= 1:
                    values(b - 1)
                fm_step(f"z{2 * b + 1}", w, 256 * (b % 2) + P, uT)
                prob_transposes(b)

            def cumsum_rows(b):
                if b < 2:
                    pe.wait_ge(sc_used, 16)
                else:
                    pe.wait_ge(seg_ready, 2 * (b - 1))
                for a in range(2):
                    for i in range(NT):
                        left = dA[:, i, 2 * b + a:2 * b + a + 1].to_broadcast([P, P])
                        last = mm(bank[4 + b % 2][:, 256 * a + P * i:256 * a + P * i + P], left, tri[:, :],
                                  start=True, stop=True)
                last.then_inc(r_ready, 1)

            def sum_squares(b):
                pe.wait_ge(sq_ready, b + 1)
                mm(bank[2][:, 0:SEQ], ones[:, :], ysq[:, b % 2, :], start=(b == 0), stop=(b == 15))\
                    .then_inc(ssq_mm, 1)

            cumsum_rows(0)
            pe.wait_ge(xdt_done, 8)
            for b in range(16):
                if b % 4 == 0:
                    use_unit(f"g{b // 4}")
                w = unit_view(f"g{b // 4}", KT)
                if b + 1 < 16:
                    cumsum_rows(b + 1)
                fm_step(f"g{b}", w, P * (b % 4), uT)
                if b == 0:
                    values(7)
                pe.wait_ge(m_ready, 2 * b + 2)
                if b >= 2:
                    pe.wait_ge(y_used, b - 1)
                else:
                    pe.wait_ge(pv_evac, 7 + b)
                for a in range(2):
                    h = 2 * b + a
                    last = weighted_sum(bank[6 + b % 2][64 * a:64 * a + 64, :], xdt[:, 0, HEAD * h:HEAD * h + HEAD],
                                        xdt[:, 1, HEAD * h:HEAD * h + HEAD], mdec[:, 2 * (b % 2) + a, :])
                last.then_inc(y_ready, 1)
                if b >= 3:
                    sum_squares(b - 3)
            for b in (13, 14, 15):
                sum_squares(b)

            pe.wait_ge(gn_ms, 1)
            transposes(memn)
            pe.wait_ge(tr_evac, 8)
            for j in range(2):
                use_unit(f"kv{j}")
                w = unit_view(f"kv{j}", KT)
                for c in range(4):
                    fm_step(f"kx{4 * j + c}", w, P * c, memT)
            for j in range(2):
                use_unit(f"kv{2 + j}")
                w = unit_view(f"kv{2 + j}", KT)
                for i in range(NT):
                    tm_step(f"vx{j}{i}", w, 0, 512, memT, i)
            pe.wait_ge(pv_evac, 8)
            for j in range(2):
                use_unit(f"ao{j}")
                w = unit_view(f"ao{j}", 8)
                for c in range(4):
                    fm_step(f"ao{4 * j + c}", w, P * c, qT, 8)
            pe.wait_ge(yfin, 16)
            for j in range(4):
                use_unit(f"so{j}")
                w = unit_view(f"so{j}", 16)
                for c in range(2):
                    fm_step(f"so{2 * j + c}", w, P * c, zs, 16)
            wait_evac(pe, "so7")
            for j in range(2):
                use_unit(f"mo{j}")
                w = unit_view(f"mo{j}", 8)
                for i in range(NT):
                    tm_step(f"mo{j}{i}", w, 0, 512, uT, i)

            transposes(xn1)
            pe.wait_ge(tr_evac, 12)
            for j in range(2):
                use_unit(f"xq{j}")
                w = unit_view(f"xq{j}", KT)
                for c in range(4):
                    fm_step(f"qx{4 * j + c}", w, P * c, hxT)
            wait_evac(pe, "qx7")

            def x_scores(h):
                for i in range(NT):
                    if h == 0:
                        pe.wait_ge(seg_ready, 32)
                    else:
                        pe.wait_ge(xexp_done, NT * (h - 1) + i + 1)
                    for c in range(2):
                        last = mm(bank[4 + i][:, 0:256], qxT[:, 2 * h + c, P * i:P * i + P], kxT[:, 2 * h + c, :],
                                  start=(c == 0), stop=(c == 1))
                    last.then_inc(xs_ready, 1)

            x_scores(0)
            for h in range(X_HEADS):
                if h + 1 < X_HEADS:
                    x_scores(h + 1)
                pe.wait_ge(xpn_ready, NT * (h + 1))
                if h >= 1:
                    pe.wait_ge(xpt_evac, h)
                for m in range(2):
                    for i in range(NT):
                        last = tp(bank[2][:, 256 * m + P * i:256 * m + P * i + P],
                                  pX[:, 2 * (h % 2) + i, P * m:P * m + P], ident[:, :])
                last.then_inc(xpt_ready, 1)
                pe.wait_ge(xpt_evac, h + 1)
                for c in range(2):
                    if h == 0:
                        pe.wait_ge(y_used, 16)
                    else:
                        pe.wait_ge(xo_evac, 2 * (h - 1) + c + 1)
                    for m in range(2):
                        f0 = 256 * h + P * c
                        last = mm(bank[6 + c][:, 0:SEQ], vx[:, m, f0:f0 + P], pXT[:, m, 0:256],
                                  start=(m == 0), stop=(m == 1))
                    last.then_inc(xo_ready, 1)
            pe.wait_ge(xo_evac, 8)
            for j in range(2):
                use_unit(f"xo{j}")
                w = unit_view(f"xo{j}", 8)
                for i in range(NT):
                    tm_step(f"xo{j}{i}", w, 0, 512, qT, i)

            transposes(xn2)
            pe.wait_ge(tr_evac, 16)
            pe.wait_ge(xexp_done, 8)
            for i in range(NT):
                for k in range(KT):
                    last = mm(bank[4][:, 36 * i:36 * i + 36], tT[:, k, P * i:P * i + P], wr[:, k, :],
                              start=(k == 0), stop=(k == KT - 1))
            last.then_inc(rl_ready, 1)
            wait_evac(pe, "xo11")
            for i in range(NT):
                for c in range(2):
                    mm(acc_bank[i][c][:, :], ident[:, :], xres[:, i, 512 * c:512 * c + 512], start=True, stop=False,
                       skip_group_check=True)
            pe.wait_ge(rmask, 1)
            m_t = rt[:, 296:360].rearrange("p (i n) -> p i n", i=NT)
            mm(bank[5][:, 0:32], tri[:, :], m_t[:, 0, :], start=True, stop=True)
            mm(bank[5][:, 32:64], ones[:, :], m_t[:, 0, :], start=True, stop=False)
            mm(bank[5][:, 32:64], tri[:, :], m_t[:, 1, :], start=False, stop=True)
            mm(bank[5][:, 64:96], ones[:, :], m_t[:, 0, :], start=True, stop=False)
            mm(bank[5][:, 64:96], ones[:, :], m_t[:, 1, :], start=False, stop=True).then_inc(rpos, 1)

            def gather():
                for k in range(KT):
                    for i in range(NT):
                        last = mm(bank[2 + k // 4][:, P * (k % 4):P * (k % 4) + P], xn2[:, i, k::KT],
                                  S[:, i, :, :], start=(i == 0), stop=(i == NT - 1))
                last.then_inc(m_gath, 1)

            def gate_up(it):
                pe.wait_ge(m_xg, it + 1)
                for kind, used in ((0, gate_used), (1, up_used)):
                    for a in range(2):
                        pe.wait_ge(moe_landed[2 * kind + a], 16 * it + 16)
                    for k in range(KT):
                        for a in range(2):
                            w = moe_slot[2 * kind + a].rearrange("p (t n) -> p t n", t=KT)
                            last = mm(bank[4 + kind][64 * a:64 * a + 64, :], xg[:, k, CAP * a:CAP * a + CAP],
                                      w[:, k, :], start=(k == 0), stop=(k == KT - 1))
                    last.then_inc(used, 1)

            def transposes_and_down(it):
                pe.wait_ge(m_h, it + 1)
                for k in range(4):
                    tp(bank[4][:, P * k:P * k + P], hh[:, k::4], ident[:, :])
                pe.wait_ge(m_sw, it + 1)
                for i in range(NT):
                    last = tp(bank[5][:, P * i:P * i + P], Sw[:, i, :, :], ident[:, :])
                last.then_inc(m_tr, 1)
                for a in range(2):
                    pe.wait_ge(moe_landed[4 + a], 16 * it + 16)
                pe.wait_ge(m_xg, it + 2)
                pe.wait_ge(m_ht, it + 1)
                for c in range(2):
                    for k in range(4):
                        for a in range(2):
                            w = moe_slot[4 + a].rearrange("p (t n) -> p t n", t=4)
                            last = mm(bank[2 + c][64 * a:64 * a + 64, :], hT[:, k, CAP * a:CAP * a + CAP],
                                      w[:, k, 512 * c:512 * c + 512], start=(k == 0), stop=(k == 3))
                last.then_inc(down_used, 1)

            def scatter(n):
                pe.wait_ge(m_y0, n)
                pe.wait_ge(m_y1, n)
                pe.wait_ge(m_st, n)
                for i in range(NT):
                    for c in range(2):
                        last = mm(acc_bank[i][c][:, :], SwT[:, i, :], yj[:, 512 * c:512 * c + 512],
                                  start=False, stop=False, skip_group_check=True)
                return last

            pe.wait_ge(route_ready, 1)
            n_iter = pe.value_load(n_it[0:1, 0:1], min_val=PAIRS, max_val=PAIRS * MAX_PASSES)
            pe.wait_ge(m_sel, 1)
            gather()
            gate_up(0)
            pe.wait_ge(m_sel, 2)
            gather()
            transposes_and_down(0)
            with pe.Fori(1, n_iter) as it:
                pe.wait_ge(m_st, it)
                gate_up(it)
                pe.wait_ge(m_y0, it)
                pe.wait_ge(m_y1, it)
                pe.wait_ge(m_sel, it + 2)
                gather()
                scatter(it)
                transposes_and_down(it)
            scatter(n_iter).then_inc(moe_done, 1)


_INS = ["x", "mem", "norm_mix", "w_in", "conv_w", "conv_b", "dt_bias", "a_log", "d_skip", "ssm_norm",
        "w_ssm_out", "w_att_out", "w_mix_out", "norm_x", "norm_mem", "w_xq", "w_xkv", "w_xo", "norm_moe",
        "w_rg", "b_rg", "w_re", "b_re", "w_e_gate", "w_e_up", "w_e_down", "norm_final"]
_OUTS = [((1, 256, 1024), "float32")]


def kernel(**inputs):
    import numpy as _np
    import concourse.bacc as _bacc
    from concourse import mybir as _mybir
    from concourse.bass_utils import run_bass_kernel_spmd as _run

    nc = _bacc.Bacc("TRN2", target_bir_lowering=False, num_devices=1)
    arrays, args = {}, []
    for name in _INS:
        a = _np.ascontiguousarray(inputs[name])
        arrays[f"in_{name}_dram"] = a
        args.append(nc.dram_tensor(f"in_{name}_dram", a.shape, _mybir.dt.from_np(a.dtype), kind="ExternalInput").ap())
    for i, (shape, dtype) in enumerate(_OUTS):
        dt = _mybir.dt.from_np(_np.dtype(dtype))
        args.append(nc.dram_tensor(f"out_{i}_dram", shape, dt, kind="ExternalOutput").ap())
    hybrid_block(nc, *args)
    r = _run(nc, [arrays], core_ids=[0])
    return r.results[0]["out_0_dram"]
```

```python
import concourse.bass as bass
from concourse import mybir
from contextlib import ExitStack

F32 = mybir.dt.float32
F32R = mybir.dt.float32r
I32 = mybir.dt.int32
ACT = mybir.ActivationFunctionType
ALU = mybir.AluOpType
AXX = mybir.AxisListType.X

P = 128
SEQ, D = 256, 1024
NT = SEQ // P
KT = D // P
EPS = 1e-6
D_INNER, N_STATE, N_GROUPS, SSM_HEADS, HEAD = 2048, 128, 4, 32, 64
CONV_K = 4
ATT_HEADS, IDX_HEADS, TOPK = 16, 8, 64
X_HEADS = 4
EXPERTS, GROUPS, PER_GROUP, HID = 32, 4, 8, 512
CAP = 64
PAIRS = EXPERTS // 2
MAX_PASSES = SEQ // CAP
NEG = -1e30
TAKEN = -3e38
UNIT = 2048
RING = 5
HI_RING = 3
N_PRM = 13
MOE_SLOTS = 8

C_Z, C_XS, C_B, C_C = 0, 2048, 4096, 4608
C_DT, C_Q, C_K, C_V, C_QI, C_KI, C_WI, C_GS, C_GA = 5120, 5152, 6176, 6240, 6304, 6816, 6880, 6888, 7912
SM_V, SM_WI, SM_DT, TM_W = 0, 64, 72, 104


def hybrid_block(nc, x, mem, norm_mix, w_in, conv_w, conv_b, dt_bias, a_log, d_skip, ssm_norm,
                 w_ssm_out, w_att_out, w_mix_out, norm_x, norm_mem, w_xq, w_xkv, w_xo, norm_moe,
                 w_rg, b_rg, w_re, b_re, w_e_gate, w_e_up, w_e_down, norm_final, out):
    ctx = ExitStack()
    with ctx:
        def sb(name, shape, dt=F32):
            return ctx.enter_context(nc.sbuf_tensor(name, shape, dt))

        def sem(name):
            return ctx.enter_context(nc.semaphore(name))

        ctx.enter_context(nc.allow_non_contiguous_dma(reason="a few small parameter vectors"))

        KB = 1024
        sizes = (("raw", 40), ("hi", 24), ("zs", 16), ("gates", 16), ("xdt", 16), ("ys", 16), ("bc", 8), ("q", 8),
                 ("x", 8), ("u", 8))
        base = (nc.sbuf_base + 63) // 64 * 64
        at, total = {}, 0
        for region, kb in sizes:
            at[region] = base + total
            total += kb * KB
        ctx.enter_context(nc.sbuf_tensor("arena", [P, (total + 64) // 4], F32))

        def place(name, shape, region, dt=F32, skip=0):
            return nc.alloc_sbuf_tensor_at(name, shape, dt, offset=at[region] + skip)

        raw_w = place("raw_w", [P, RING, UNIT], "raw")
        lo_w = place("lo_w", [P, RING, UNIT], "raw", F32R)
        hi_w = place("hi_w", [P, HI_RING, UNIT], "hi", F32R)
        zs = place("zs", [P, 16, SEQ], "zs")
        z_lo = place("z_lo", [P, 16, SEQ], "zs", F32R)
        gates = place("gates", [P, 16, SEQ], "gates")
        xdt = place("xdt", [P, NT, D_INNER], "xdt")
        ysT = place("ysT", [P, 16, SEQ], "ys")
        y_hi = place("y_hi", [P, 16, SEQ], "ys", F32R)
        bc = place("bc", [P, 8, SEQ], "bc")
        a_hi = place("a_hi", [P, 8, SEQ], "bc", F32R)
        qT = place("qT", [P, 8, SEQ], "q")
        a_lo = place("a_lo", [P, 8, SEQ], "q", F32R)
        xres = place("xres", [P, NT, D], "x")
        u_lo = place("u_lo", [P, KT, SEQ], "x", F32R)
        u_hi = place("u_hi", [P, KT, SEQ], "u", F32R)
        outb = place("outb", [P, NT, D], "ys")
        moe_slot = [place("gate_a", [P, 4096], "zs"), place("gate_b", [P, 4096], "gates"),
                    place("up_a", [P, 4096], "xdt"), place("up_b", [P, 4096], "raw", skip=32 * KB),
                    place("down_a", [P, 4096], "raw"), place("down_b", [P, 4096], "raw", skip=16 * KB),
                    place("gate_c", [P, 4096], "bc"), place("gate_d", [P, 4096], "x")]
        moe_buf = place("moe_buf", [P, 4096], "raw", skip=48 * KB)
        cbm = sb("cbm", [P, N_GROUPS, 384])
        qiT = sb("qiT", [P, 4, SEQ])
        kz = sb("kz", [P, 2, SEQ])
        kiz = sb("kiz", [P, 2, SEQ])
        small_tm = sb("small_tm", [P, NT, TM_W])
        isc = sb("isc", [P, 384])
        selm = sb("selm", [P, 384])
        dist = sb("dist", [P, 384])
        caus = sb("caus", [P, 384])
        work = sb("work", [P, 12, 384])
        ident = sb("ident", [P, P])
        tri = sb("tri", [P, P])
        ones = sb("ones", [P, P])
        iota64 = sb("iota64", [P, CAP])
        prm = sb("prm", [P, 448])
        wr = sb("wr", [P, KT, 36])
        st = sb("st", [P, 480])

        flat_xdt = xdt[:, :, :].rearrange("p a b -> p (a b)")
        flat_ys = ysT[:, :, :].rearrange("p a b -> p (a b)")
        flat_bc = bc[:, :, :].rearrange("p a b -> p (a b)")
        flat_work = work[:, :, :].rearrange("p a b -> p (a b)")
        flat_qi = qiT[:, :, :].rearrange("p a b -> p (a b)")
        xn0 = flat_xdt[:, 0:2048].rearrange("p (i d) -> p i d", i=NT)
        memx = xn0
        memn = flat_xdt[:, 2048:4096].rearrange("p (i d) -> p i d", i=NT)
        kxT = flat_xdt[:, 0:2048].rearrange("p (k t) -> p k t", k=KT)
        vx = memn
        xn1 = flat_ys[:, 2048:4096].rearrange("p (i d) -> p i d", i=NT)
        qxT = flat_ys[:, 0:2048].rearrange("p (k t) -> p k t", k=KT)
        xn2 = xn1
        tT = qxT
        raw = flat_work[:, 0:3 * 260].rearrange("p (n w) -> p n w", n=3)
        cacc = flat_work[:, 780:780 + 512].rearrange("p (n w) -> p n w", n=2)
        rel = flat_work[:, 1536:1536 + 1536].rearrange("p (n w) -> p n w", n=2)
        prob = work[:, 0:4, :]
        probT = work[:, 4:6, :]
        albi = flat_qi[:, 0:768].rearrange("p (h w) -> p h w", h=2)
        seg = work[:, 0:4, :]
        mdec = work[:, 4:8, :]
        ysq = flat_work[:, 3072:3072 + 512].rearrange("p (n w) -> p n w", n=2)
        pX = flat_work[:, 0:2048].rearrange("p (n w) -> p n w", n=4)
        pXT = flat_work[:, 2048:3072].rearrange("p (n w) -> p n w", n=2)
        tr_tmp = flat_work[:, 3584:4608].rearrange("p (n w) -> p n w", n=2)
        mix_tmp = flat_work[:, 512:1024].rearrange("p (n w) -> p n w", n=2)
        rs_bc = flat_work[:, 0:256]

        cw = prm[:, 0:96].rearrange("p (k b) -> p k b", k=CONV_K)
        cbias = prm[:, 96:120]
        sgain = prm[:, 120:136]
        g_mix, g_mem, g_x, g_moe = (prm[:, 136 + 8 * i:144 + 8 * i] for i in range(4))
        dskip = prm[:, 168:184]
        dtb = prm[:, 184:216]
        alog = prm[:, 216:248]
        brt = prm[:, 248:284]
        rev4 = prm[:, 284:288]
        rev32 = prm[:, 288:320]
        dt = prm[:, 320:384].rearrange("p (i h) -> p i h", i=NT)
        dA = prm[:, 384:448].rearrange("p (i h) -> p i h", i=NT)
        flat_cb = cbm[:, :, :].rearrange("p a b -> p (a b)")
        cwrow = flat_cb[0:24, 0:512]
        prow = flat_cb[0:40, 768:896]
        sel2 = sb("sel2", [2, P])
        drow = sb("drow", [2, 16])
        n_it = sb("n_it", [P, 3], I32)
        pos_all = sb("pos_all", [P, NT, MAX_PASSES * EXPERTS + 2])
        comb_all = flat_cb[:, 0:NT * (MAX_PASSES * EXPERTS + 2)].rearrange("p (i n) -> p i n", i=NT)
        bias3 = pos_all[:, 0, 0:96].rearrange("p (k h) -> p k h", k=3)

        xg = moe_buf[:, 0:1024].rearrange("p (k j) -> p k j", k=KT)
        yj = moe_buf[:, 1024:2048]
        hs = moe_buf[:, 2048:2560]
        hh = moe_buf[:, 2560:3072]
        hT = moe_buf[:, 3072:3584].rearrange("p (k j) -> p k j", k=4)
        S = flat_work[:, 0:256].rearrange("p (i a j) -> p i a j", i=NT, a=2)
        Sw = flat_work[:, 256:512].rearrange("p (i a j) -> p i a j", i=NT, a=2)
        SwT = flat_work[:, 512:768].rearrange("p (i t) -> p i t", i=NT)
        gain_f = flat_work[:, 1024:2048]
        junk = moe_buf[:, 0:2048].rearrange("p (n w) -> p n w", n=4)
        rt = flat_work[:, 3072:4096]

        bank = [ctx.enter_context(nc.psum_tensor(f"bank{i}", [P, 512], F32)) for i in range(8)]
        acc_bank = [[bank[0], bank[1]], [bank[6], bank[7]]]

        landed = [sem(f"landed{s}") for s in range(RING)]
        moe_landed = [sem(f"moe_landed{s}") for s in range(MOE_SLOTS)]
        hi_done = sem("hi_done")
        lo_done = sem("lo_done")
        lo_pool = sem("lo_pool")
        x_in = sem("x_in")
        gmix_in = sem("gmix_in")
        ident_ready = sem("ident_ready")
        tr_gain = sem("tr_gain")
        tr_hi = sem("tr_hi")
        mem_in = sem("mem_in")
        prm_in = sem("prm_in")
        gainf_in = sem("gainf_in")
        consts = sem("consts")
        pool_chain = sem("pool_chain")
        act_chain = sem("act_chain")
        dve_chain = sem("dve_chain")
        ssq_done = sem("ssq_done")
        ms_ready = sem("ms_ready")
        rstd_done = sem("rstd_done")
        xn_ready = sem("xn_ready")
        tr_ready = sem("tr_ready")
        tr_evac = sem("tr_evac")
        prm_tr = sem("prm_tr")
        prm_ready = sem("prm_ready")
        proj_ready = sem("proj_ready")
        evac_act = sem("evac_act")
        evac_dve = sem("evac_dve")
        dt_exp_in, dt_exp, dt_ready = sem("dt_exp_in"), sem("dt_exp"), sem("dt_ready")
        idx_ready, idx_relu, idx_used = sem("idx_ready"), sem("idx_relu"), sem("idx_used")
        conv_done, conv_silu = sem("conv_done"), sem("conv_silu")
        cb_ready, cb_done = sem("cb_ready"), sem("cb_done")
        acs_ready, acs_done = sem("acs_ready"), sem("acs_done")
        xt_ready, xdt_done = sem("xt_ready"), sem("xdt_done")
        mask_ready = sem("mask_ready")
        albi_ready, sc_ready, sc_used, mx_ready, exp_done, pn_ready = (
            sem(n) for n in ("albi_ready", "sc_ready", "sc_used", "mx_ready", "exp_done", "pn_ready"))
        rcp_ready = sem("rcp_ready")
        pt_ready, pt_evac, pv_ready, pv_evac = (sem(n) for n in ("pt_ready", "pt_evac", "pv_ready", "pv_evac"))
        zsilu, gsig = sem("zsilu"), sem("gsig")
        r_ready, seg_ready, dec_ready, m_ready, y_ready, y_used = (
            sem(n) for n in ("r_ready", "seg_ready", "dec_ready", "m_ready", "y_ready", "y_used"))
        yg_ready, sq_ready, ssq_mm, yfin = sem("yg_ready"), sem("sq_ready"), sem("ssq_mm"), sem("yfin")
        y_hi_done, y_lo_done = sem("y_hi_done"), sem("y_lo_done")
        pv_lo, mix_ready, mix_hi, xo_lo = sem("pv_lo"), sem("mix_ready"), sem("mix_hi"), sem("xo_lo")
        gn_ms, gn_rstd = sem("gn_ms"), sem("gn_rstd")
        xs_ready, xmx_ready, xexp_done, xpn_ready, xpt_ready, xpt_evac, xo_ready, xo_evac = (
            sem(n) for n in ("xs_ready", "xmx_ready", "xexp_done", "xpn_ready", "xpt_ready", "xpt_evac",
                             "xo_ready", "xo_evac"))
        rl_ready, rexp_in, rexp_done, rmask, rpos = (
            sem(n) for n in ("rl_ready", "rexp_in", "rexp_done", "rmask", "rpos"))
        route_ready = sem("route_ready")
        m_sel, m_gath, m_xg, m_silu, m_h, m_tr, m_ht, m_st, m_y0, m_y1, m_sw = (
            sem("moe_" + n) for n in ("sel", "gathered", "xg", "silu", "h", "transposed", "hT", "swT", "y_act", "y_dve", "sw"))
        gate_used, up_used, down_used = sem("gate_used"), sem("up_used"), sem("down_used")
        residual_in = sem("residual_in")
        moe_done, f_ssq, f_ms, f_rstd, f_out, stored = (
            sem(n) for n in ("moe_done", "f_ssq", "f_ms", "f_rstd", "f_out", "stored"))

        GATE, UP, DOWN = (0, 6), 2, 4

        steps = (["k", "ki", "tm0", "tm1"] + [f"qi{b}" for b in range(4)] + [f"bc{b}" for b in range(8)]
                 + [f"xs{b}" for b in range(16)] + [f"q{b}" for b in range(8)] + [f"z{b}" for b in range(16)]
                 + [f"g{b}" for b in range(16)] + [f"ao{b}" for b in range(8)] + [f"kx{b}" for b in range(8)]
                 + [f"vx{c}{i}" for c in range(2) for i in range(NT)]
                 + [f"so{b}" for b in range(8)]
                 + [f"mo{c}{i}" for c in range(2) for i in range(NT)] + [f"qx{b}" for b in range(8)]
                 + [f"xo{c}{i}" for c in range(2) for i in range(NT)])
        STEP = {s: n for n, s in enumerate(steps)}
        by_dve = [s[:2] in ("ao", "so", "mo", "xo") for s in steps]

        def wait_evac(eng, name_or_n):
            n = STEP[name_or_n] if isinstance(name_or_n, str) else name_or_n
            if by_dve[n]:
                eng.wait_ge(evac_dve, sum(by_dve[:n + 1]))
            else:
                eng.wait_ge(evac_act, n + 1 - sum(by_dve[:n + 1]))

        def cols(w, c0, n):
            return w[0, :, c0:c0 + n].rearrange("(p t) n -> p t n", t=KT)

        def rows(w, half, c0):
            return w[0, 512 * half:512 * half + 512, c0:c0 + 512].rearrange("(t p) n -> p t n", p=P)

        units, LAST_STEP = [("kk", None, KT), ("tm", None, KT)], {"kk": "ki", "tm": "tm1"}
        for kind, w, c0, n in (("qi", w_in, C_QI, 2), ("bc", w_in, C_B, 4), ("xs", w_in, C_XS, 8), ("q", w_in, C_Q, 4),
                               ("z", w_in, C_Z, 8), ("g", w_in, C_GS, 8), ("ao", w_att_out, 0, 4),
                               ("kx", w_xkv, 0, 4), ("vx", w_xkv, D, 2), ("so", w_ssm_out, 0, 8),
                               ("mo", w_mix_out, 0, 2), ("qx", w_xq, 0, 4), ("xo", w_xo, 0, 2)):
            for j in range(n):
                if kind == "ao":
                    units.append((f"ao{j}", w[0, :, 256 * j:256 * j + 256].rearrange("(t p) n -> p t n", p=P), 8))
                elif kind == "so":
                    units.append((f"so{j}", w[0, :, P * j:P * j + P].rearrange("(t p) n -> p t n", p=P), 16))
                elif kind in ("vx", "mo", "xo"):
                    for half in range(2):
                        src = cols(w, c0 + 512 * j, 512)[:, 4 * half:4 * half + 4, :] if kind == "vx" \
                            else rows(w, half, 512 * j)
                        units.append((f"{kind}{j}{half}", src, 4))
                        LAST_STEP[f"{kind}{j}{half}"] = f"{kind}{j}{half}"
                else:
                    units.append((f"{kind}{j}", cols(w, c0 + 256 * j, 256), KT))
                if kind == "so":
                    LAST_STEP[f"so{j}"] = f"so{j}"
                elif kind not in ("vx", "mo", "xo"):
                    LAST_STEP[f"{kind}{j}"] = f"{kind}{2 * j + 1}"
        UN = {u[0]: n for n, u in enumerate(units)}
        PIECES = [[(0, C_K, HEAD), (HEAD, C_K, HEAD), (2 * HEAD, C_KI, HEAD), (3 * HEAD, C_KI, HEAD)],
                  [(SM_V, C_V, HEAD), (SM_WI, C_WI, IDX_HEADS), (SM_DT, C_DT, SSM_HEADS)]]

        def unit_len(n):
            return KT * TM_W if n == UN["tm"] else UNIT

        def parts(name):
            n = UN[name]
            return [w[:, 0:unit_len(n)].rearrange("p (t n) -> p t n", t=units[n][2])
                    for w in (hi_w[:, n % HI_RING, :], lo_w[:, n % RING, :])]

        FIRST_STEP = {f"{k}{2 * j}": f"{k}{j}" for k in ("qi", "bc", "xs", "q", "z", "g", "ao", "kx", "qx")
                      for j in range(8) if f"{k}{j}" in UN}
        FIRST_STEP.update({"k": "kk", "tm0": "tm"})
        FIRST_STEP.update({f"so{j}": f"so{j}" for j in range(8)})
        FIRST_STEP.update({f"{k}{j}{h}": f"{k}{j}{h}" for k in ("vx", "mo", "xo") for j in range(2) for h in range(2)})

        def landed_value(n):
            return 16 * (n // RING + 1) + (16 * (len(PIECES[n % RING]) - 1) if n % RING < len(PIECES) else 0)

        LOW_ON_POOL = [UN[f"{kind}{j}"] for kind, n in (("bc", 4), ("xs", 8), ("q", 4)) for j in range(1, n, 2)]

        def wait_low(eng, n):
            if n in LOW_ON_POOL:
                eng.wait_ge(lo_pool, LOW_ON_POOL.index(n) + 1)
            else:
                eng.wait_ge(lo_done, sum(m not in LOW_ON_POOL for m in range(n + 1)))

        def wait_used(eng, n):
            eng.wait_ge(proj_ready, STEP[LAST_STEP[units[n][0]]] + 1)

        block = ctx.enter_context(nc.Block())

        @block.sync
        def _(sp):
            def load_expert(s, e, w):
                t = HID * D // P // w.shape[3]
                src = w[0:1, bass.ds(e, 1), :, :].rearrange("o e (p t) n -> p (o e t) n", p=P)
                sp.dma_start(moe_slot[s][:, :].rearrange("p (t n) -> p t n", t=t), src).then_inc(moe_landed[s], 16)

            small_dmas = [(prow[0:24, :], conv_b[0, :].rearrange("(b p) -> b p", p=P)),
                          (prow[24:40, :], ssm_norm[0, :].rearrange("(b p) -> b p", p=P)),
                          (cwrow, conv_w[0, :, :].rearrange("(b q) k -> b (q k)", q=P)),
                          (drow[:, :], d_skip[0, :].rearrange("(b a) -> a b", a=2)),
                          (dtb, dt_bias[0:1, :].to_broadcast([P, SSM_HEADS])),
                          (alog, a_log[0:1, :].to_broadcast([P, SSM_HEADS])),
                          (g_mem, norm_mem[0, :].rearrange("(p t) -> p t", t=KT)),
                          (g_x, norm_x[0, :].rearrange("(p t) -> p t", t=KT)),
                          (g_moe, norm_moe[0, :].rearrange("(p t) -> p t", t=KT)),
                          (brt[:, 0:4], b_rg[0:1, :].to_broadcast([P, GROUPS])),
                          (brt[:, 4:36], b_re[0:1, :].to_broadcast([P, EXPERTS])),
                          (wr[:, :, 0:4], w_rg[0, :, :].rearrange("(p t) n -> p t n", t=KT)),
                          (wr[:, :, 4:36], w_re[0, :, :].rearrange("(p t) n -> p t n", t=KT))]
            assert len(small_dmas) == N_PRM

            for i in range(NT):
                sp.dma_start(xres[:, i, :], x[0, P * i:P * i + P, :]).then_inc(x_in, 16)
            sp.dma_start(g_mix, norm_mix[0, :].rearrange("(p t) -> p t", t=KT)).then_inc(gmix_in, 16)
            for n, (name, src, k) in enumerate(units):
                if n >= RING:
                    wait_used(sp, n - RING)
                dst = raw_w[:, n % RING, 0:unit_len(n)].rearrange("p (t n) -> p t n", t=k)
                if n < len(PIECES):
                    for d0, s0, w in PIECES[n]:
                        sp.dma_start(dst[:, :, d0:d0 + w], cols(w_in, s0, w)).then_inc(landed[n], 16)
                else:
                    sp.dma_start(dst, src).then_inc(landed[n % RING], 16)
                if n == 2:
                    for dst, src in small_dmas:
                        sp.dma_start(dst, src).then_inc(prm_in, 16)
                if name == "ao3":
                    sp.wait_ge(y_ready, 16)
                    for i in range(NT):
                        sp.dma_start(memx[:, i, :], mem[0, P * i:P * i + P, :]).then_inc(mem_in, 16)
                if name == "so4":
                    sp.wait_ge(proj_ready, STEP["vx11"] + 1)
                    for i in range(NT):
                        sp.dma_start(xres[:, i, :], x[0, P * i:P * i + P, :]).then_inc(x_in, 16)
                if name == "qx2":
                    load_expert(GATE[0], 0, w_e_gate)
                    load_expert(GATE[0] + 1, 1, w_e_gate)

            def load_two(kind, pair, w, used=None, turns=None):
                if used is not None:
                    sp.wait_ge(used, turns)
                for a in range(2):
                    load_expert(kind + a, 2 * pair + a, w)

            def rest_of_pass(first):
                with sp.Fori(0, PAIRS // 2 - 1) as j:
                    for o in (1, 2):
                        n = 2 * j + o
                        load_two(GATE[(o + 1) % 2], n + 1, w_e_gate, gate_used, first + n)
                        load_two(UP, n, w_e_up, up_used, first + n)
                        load_two(DOWN, n, w_e_down, down_used, first + n)
                load_two(UP, PAIRS - 1, w_e_up, up_used, first + PAIRS - 1)
                load_two(DOWN, PAIRS - 1, w_e_down, down_used, first + PAIRS - 1)

            sp.wait_ge(xo_ready, 2 * X_HEADS)
            load_expert(UP, 0, w_e_up)
            last = len(units) - 1
            for s, e, w, raw_slots, hi_slots in ((UP + 1, 1, w_e_up, (4,), (0,)), (DOWN, 0, w_e_down, (0, 1), ()),
                                                 (DOWN + 1, 1, w_e_down, (2, 3), ())):
                wait_used(sp, max([n for n in range(last + 1) if n % RING in raw_slots or n % HI_RING in hi_slots]))
                load_expert(s, e, w)
            load_expert(GATE[1], 2, w_e_gate)
            sp.wait_ge(residual_in, 1)
            load_expert(GATE[1] + 1, 3, w_e_gate)
            rest_of_pass(0)
            sp.wait_ge(route_ready, 1)
            n_pass = sp.value_load(n_it[0:1, 1:2], min_val=1, max_val=MAX_PASSES)
            with sp.If(n_pass > 1):
                with sp.Fori(1, n_pass) as r:
                    load_two(GATE[0], 0, w_e_gate, gate_used, r * PAIRS - 1)
                    load_two(GATE[1], 1, w_e_gate, gate_used, r * PAIRS)
                    load_two(UP, 0, w_e_up, up_used, r * PAIRS)
                    load_two(DOWN, 0, w_e_down, down_used, r * PAIRS)
                    rest_of_pass(r * PAIRS)
            for i in range(NT):
                sp.wait_ge(f_out, i + 1)
                sp.dma_start(out[0, P * i:P * i + P, :], outb[:, i, :]).then_inc(stored, 16)
            sp.wait_ge(stored, 16 * NT)

        @block.gpsimd
        def _(pool):
            chain = [0]

            def link(ins):
                chain[0] += 1
                ins.then_inc(pool_chain, 1)
                pool.wait_ge(pool_chain, chain[0])

            link(nc.gpsimd.memset(ident[:, :], 0.0))
            link(nc.gpsimd.affine_select(out=ident[:, :], in_=ident[:, :], compare_op=ALU.not_equal, fill=1.0,
                                         base=0, pattern=[[-1, P]], channel_multiplier=1))
            nc.gpsimd.memset(st[:, 470:474], 0.0).then_inc(ident_ready, 1)
            link(nc.gpsimd.memset(ones[:, :], 1.0))
            link(nc.gpsimd.affine_select(out=tri[:, :], in_=ones[:, :], compare_op=ALU.is_ge, fill=0.0,
                                         base=0, pattern=[[1, P]], channel_multiplier=-1))
            link(nc.gpsimd.affine_select(out=sel2[:, :], in_=ones[0:2, :], compare_op=ALU.is_ge, fill=0.0,
                                         base=0, pattern=[[1, P]], channel_multiplier=-64))
            link(nc.gpsimd.affine_select(out=sel2[:, :], in_=sel2[:, :], compare_op=ALU.is_ge, fill=0.0,
                                         base=63, pattern=[[-1, P]], channel_multiplier=64))
            for d in (kz, kiz):
                link(nc.gpsimd.memset(d[0:64, 1, :], 0.0))
                link(nc.gpsimd.memset(d[64:128, 0, :], 0.0))
            for n in range(3):
                last = nc.gpsimd.memset(raw[:, n, 0:3], 0.0)
            last.then_inc(consts, 1)
            link(nc.gpsimd.iota(dist[:, 0:128], pattern=[[-1, 128]], base=0, channel_multiplier=1,
                                allow_small_or_imprecise_dtypes=True))
            link(nc.gpsimd.iota(dist[:, 128:384], pattern=[[-1, 256]], base=128, channel_multiplier=1,
                                allow_small_or_imprecise_dtypes=True))
            link(nc.gpsimd.iota(iota64[:, :], pattern=[[1, CAP]], base=0, channel_multiplier=0,
                                allow_small_or_imprecise_dtypes=True))
            link(nc.gpsimd.iota(rev4, pattern=[[-1, GROUPS]], base=GROUPS, channel_multiplier=0,
                                allow_small_or_imprecise_dtypes=True))
            link(nc.gpsimd.iota(rev32, pattern=[[-1, EXPERTS]], base=EXPERTS, channel_multiplier=0,
                                allow_small_or_imprecise_dtypes=True))
            link(nc.gpsimd.memset(caus[:, :], 0.0))
            nc.gpsimd.affine_select(out=caus[:, 0:128], in_=caus[:, 0:128], compare_op=ALU.is_ge, fill=NEG,
                                    base=0, pattern=[[-1, 128]], channel_multiplier=1)
            nc.gpsimd.affine_select(out=caus[:, 128:384], in_=caus[:, 128:384], compare_op=ALU.is_ge, fill=NEG,
                                    base=128, pattern=[[-1, 256]], channel_multiplier=1).then_inc(consts, 1)

            def albi_tile(h):
                if h >= 2:
                    pool.wait_ge(sc_used, h - 1)
                slope = 2.0 ** (-8.0 * (h + 1) / ATT_HEADS)
                link(nc.gpsimd.tensor_scalar(albi[:, h % 2, :], dist[:, :], -slope, None, ALU.mult))
                nc.gpsimd.tensor_tensor(albi[:, h % 2, :], albi[:, h % 2, :], selm[:, :], ALU.add)\
                    .then_inc(albi_ready, 1)

            def normalise(h):
                pool.wait_ge(rcp_ready, h // 2 + 1)
                pb = prob[:, 2 * (h // 2 % 2) + h % 2, :]
                for i, (a, b) in enumerate(((0, 128), (128, 384))):
                    k = 96 + 4 * (h // 2 % 2) + 2 * (h % 2) + i
                    last = nc.gpsimd.tensor_scalar(pb[:, a:b], pb[:, a:b], st[:, k:k + 1], None, ALU.mult)
                last.then_inc(pn_ready, 1)

            pool.wait_ge(consts, 2)
            for m in LOW_ON_POOL:
                pool.wait_ge(hi_done, m + 1)
                nc.gpsimd.tensor_tensor(lo_w[:, m % RING, :], raw_w[:, m % RING, :],
                                        hi_w[:, m % HI_RING, :].bitcast(F32), ALU.subtract).then_inc(lo_pool, 1)
            pool.wait_ge(mask_ready, 1)
            pool.wait_ge(idx_ready, 4)
            albi_tile(0)
            albi_tile(1)
            for b in range(ATT_HEADS // 2):
                if b + 1 < ATT_HEADS // 2:
                    albi_tile(2 * b + 2)
                    albi_tile(2 * b + 3)
                normalise(2 * b)
                normalise(2 * b + 1)

            def gate_y(b):
                pool.wait_ge(y_used, b + 1)
                if b == 0:
                    pool.wait_ge(zsilu, 1)
                nc.gpsimd.tensor_tensor(ysT[:, b, :], ysT[:, b, :], zs[:, b, :], ALU.mult).then_inc(yg_ready, 1)
                pool.wait_ge(yg_ready, b + 1)
                nc.gpsimd.tensor_scalar(zs[:, b, :], ysT[:, b, :], sgain[:, b:b + 1], None, ALU.mult)\
                    .then_inc(yfin, 1)

            pool.wait_ge(cb_done, N_GROUPS)
            pool.wait_ge(prm_ready, 2)
            for b in range(SSM_HEADS // 2):
                for a in range(2):
                    h = 2 * b + a
                    pool.wait_ge(dec_ready, h + 1)
                    if b == 1:
                        pool.wait_ge(pv_ready, 8)
                    if b >= 2:
                        pool.wait_ge(y_ready, b - 1)
                    nc.gpsimd.tensor_tensor(mdec[:, 2 * ((b + 1) % 2) + a, :], seg[:, 2 * (b % 2) + a, :],
                                            cbm[:, h // 8, :], ALU.mult).then_inc(m_ready, 1)
                if b >= 1:
                    gate_y(b - 1)
            gate_y(SSM_HEADS // 2 - 1)

        @block.scalar
        def _(act):
            chain = [0]

            def link(ins):
                chain[0] += 1
                ins.then_inc(act_chain, 1)
                act.wait_ge(act_chain, chain[0])

            split = [0]

            def split_hi_through(n):
                while split[0] <= min(n, len(units) - 1):
                    m = split[0]
                    act.wait_ge(landed[m % RING], landed_value(m))
                    if m >= HI_RING:
                        wait_used(act, m - HI_RING)
                    w = unit_len(m)
                    nc.scalar.activation(hi_w[:, m % HI_RING, 0:w], raw_w[:, m % RING, 0:w], ACT.Copy)\
                        .then_inc(hi_done, 1)
                    split[0] += 1

            group = [0]

            def transposed_hi(dst):
                for i in range(NT):
                    for q in range(2):
                        g = group[0]
                        act.wait_ge(tr_gain, g + 1)
                        nc.scalar.activation(dst[:, 4 * q:4 * q + 4, P * i:P * i + P],
                                             tr_tmp[:, g % 2, :].rearrange("p (k t) -> p k t", k=4), ACT.Copy)\
                            .then_inc(tr_hi, 1)
                        group[0] += 1

            def norm_stats(n, src, junk_to, between=None):
                for i in range(NT):
                    last = nc.scalar.activation(junk_to[:, i, :], src[:, i, :], ACT.Square,
                                                accum_out=st[:, 4 * n + i:4 * n + i + 1])
                last.then_inc(ssq_done, 1)
                if between is not None:
                    split_hi_through(between)
                act.wait_ge(ms_ready, n + 1)
                nc.scalar.activation(st[:, 4 * n + 2:4 * n + 4], st[:, 4 * n + 2:4 * n + 4], ACT.Sqrt)\
                    .then_inc(rstd_done, 1)

            def evac(name, dst, scale=1.0, src=None):
                n = STEP[name]
                if name in FIRST_STEP:
                    split_hi_through(UN[FIRST_STEP[name]] + 2)
                act.wait_ge(proj_ready, n + 1)
                src = bank[n % 2][:, 0:SEQ] if src is None else src
                nc.scalar.activation(dst, src, ACT.Copy, scale=scale).then_inc(evac_act, 1)

            act.wait_ge(x_in, 32)
            norm_stats(0, xres, xn0)
            split_hi_through(0)
            transposed_hi(u_hi)
            split_hi_through(2)
            act.wait_ge(consts, 1)

            for name, d in (("k", kz), ("ki", kiz)):
                n = STEP[name]
                act.wait_ge(proj_ready, n + 1)
                nc.scalar.activation(d[0:64, 0, :], bank[n % 2][0:64, 0:SEQ], ACT.Copy)
                nc.scalar.activation(d[64:128, 1, :], bank[n % 2][64:128, 0:SEQ], ACT.Copy).then_inc(evac_act, 1)
            for i in range(NT):
                n = STEP[f"tm{i}"]
                evac(f"tm{i}", small_tm[:, i, :], src=bank[n % 2][:, 0:TM_W])
            act.wait_ge(prm_in, 16 * N_PRM)
            nc.scalar.activation(alog, alog, ACT.Exp)
            act.wait_ge(dt_exp_in, 1)
            nc.scalar.activation(st[:, 160:224], st[:, 160:224], ACT.Exp).then_inc(dt_exp, 1)

            def relu(b):
                act.wait_ge(idx_ready, b + 1)
                if b >= 2:
                    act.wait_ge(idx_used, b - 1)
                nc.scalar.activation(rel[:, b % 2, 0:256], bank[4][:, 0:256], ACT.Relu)
                nc.scalar.activation(rel[:, b % 2, 256:768], bank[5][:, :], ACT.Relu).then_inc(idx_relu, 1)

            for b in range(4):
                evac(f"qi{b}", qiT[:, b, :])
                if b >= 1:
                    relu(b - 1)
            relu(3)

            xbc = [f"bc{b}" for b in range(8)] + [f"xs{b}" for b in range(16)]

            def conv_out(n):
                act.wait_ge(conv_done, n + 1)
                dst = bc[:, n, :] if n < 8 else ysT[:, n - 8, :]
                nc.scalar.activation(dst, cacc[:, n % 2, :], ACT.Silu).then_inc(conv_silu, 1)

            for n, name in enumerate(xbc):
                if n >= 3:
                    act.wait_ge(conv_done, n - 2)
                evac(name, raw[:, n % 3, 3:259])
                if n >= 1:
                    conv_out(n - 1)
            conv_out(23)

            for b in range(8):
                evac(f"q{b}", qT[:, b, :], scale=HEAD ** -0.5)

            def exps(b):
                act.wait_ge(mx_ready, b + 1)
                if b >= 2:
                    act.wait_ge(pt_ready, 2 * (b - 1))
                for a in range(2):
                    for i, (lo, hi) in enumerate(((0, 128), (128, 384))):
                        k = 2 * a + i
                        pb = prob[:, 2 * (b % 2) + a, lo:hi]
                        last = nc.scalar.activation(pb, pb, ACT.Exp, bias=st[:, 72 + 4 * (b % 2) + k:73 + 4 * (b % 2) + k],
                                                    accum_out=st[:, 80 + 4 * (b % 2) + k:81 + 4 * (b % 2) + k])
                last.then_inc(exp_done, 1)

            def values_hi(b):
                act.wait_ge(pv_ready, b + 1)
                nc.scalar.activation(a_hi[:, b, :], bank[6 + b % 2][:, 0:SEQ], ACT.Copy).then_inc(pv_evac, 1)

            exps(0)
            for b in range(8):
                evac(f"z{2 * b}", zs[:, 2 * b, :])
                if b + 1 < 8:
                    exps(b + 1)
                if b >= 1:
                    values_hi(b - 1)
                evac(f"z{2 * b + 1}", zs[:, 2 * b + 1, :])

            def square_y(b):
                act.wait_ge(yg_ready, b + 1)
                if b >= 2:
                    act.wait_ge(ssq_mm, b - 1)
                nc.scalar.activation(ysq[:, b % 2, :], ysT[:, b, :], ACT.Square).then_inc(sq_ready, 1)

            def gated_hi(b):
                act.wait_ge(yfin, b + 1)
                act.wait_ge(sq_ready, b + 1)
                nc.scalar.activation(y_hi[:, b, :], zs[:, b, :], ACT.Copy).then_inc(y_hi_done, 1)

            def decays(b):
                for h in (2 * b, 2 * b + 1):
                    act.wait_ge(seg_ready, h + 1)
                    sg = seg[:, h % 4, :]
                    nc.scalar.activation(sg, sg, ACT.Exp).then_inc(dec_ready, 1)

            decays(0)
            split_hi_through(UN["g0"] + 2)
            values_hi(7)
            decays(1)
            evac("g0", gates[:, 0, :])
            wait_evac(act, "z15")
            nc.scalar.activation(zs[:, :, :], zs[:, :, :], ACT.Silu).then_inc(zsilu, 1)
            evac("g1", gates[:, 1, :])
            for b in range(2, 16):
                decays(b)
                evac(f"g{b}", gates[:, b, :])
                square_y(b - 2)
                if b >= 3:
                    gated_hi(b - 3)
            split_hi_through(UN["ao0"] + 2)
            square_y(14)
            gated_hi(13)
            square_y(15)
            wait_evac(act, "g15")
            nc.scalar.activation(gates[:, 8:16, :], gates[:, 8:16, :], ACT.Sigmoid).then_inc(gsig, 1)
            gated_hi(14)
            gated_hi(15)
            nc.scalar.activation(gates[:, 0:8, :], gates[:, 0:8, :], ACT.Sigmoid).then_inc(gsig, 1)
            split_hi_through(UN["ao1"] + 2)
            act.wait_ge(mem_in, 32)
            norm_stats(1, memx, memn, between=UN["ao2"] + 2)
            act.wait_ge(gn_ms, 1)
            nc.scalar.activation(rs_bc, rs_bc, ACT.Sqrt).then_inc(gn_rstd, 1)
            split_hi_through(UN["ao3"] + 2)
            transposed_hi(u_hi)
            for b in range(8):
                evac(f"kx{b}", kxT[:, b, :])
            for c in range(2):
                for i in range(NT):
                    n = STEP[f"vx{c}{i}"]
                    evac(f"vx{c}{i}", vx[:, i, 512 * c:512 * c + 512], src=bank[n % 2][:, :])
            for b in range(8):
                split_hi_through(UN[f"so{b}"] + 2)
                if b >= 1:
                    act.wait_ge(mix_ready, b)
                    nc.scalar.activation(a_hi[:, b - 1, :], mix_tmp[:, (b - 1) % 2, :], ACT.Copy).then_inc(mix_hi, 1)
            act.wait_ge(mix_ready, 8)
            nc.scalar.activation(a_hi[:, 7, :], mix_tmp[:, 1, :], ACT.Copy).then_inc(mix_hi, 1)
            for c in range(2):
                for h in range(2):
                    split_hi_through(UN[f"mo{c}{h}"] + 2)

            wait_evac(act, "mo11")
            norm_stats(2, xres, xn1)
            transposed_hi(a_hi)
            for b in range(8):
                evac(f"qx{b}", qxT[:, b, :], scale=(D // X_HEADS) ** -0.5)
            for h in range(X_HEADS):
                for i in range(NT):
                    n = NT * h + i
                    act.wait_ge(xmx_ready, n + 1)
                    if h >= 2:
                        act.wait_ge(xpt_ready, h - 1)
                    nc.scalar.activation(pX[:, 2 * (h % 2) + i, 0:256], bank[4 + i][:, 0:256], ACT.Exp,
                                         bias=st[:, 104 + n:105 + n],
                                         accum_out=st[:, 112 + n:113 + n]).then_inc(xexp_done, 1)
                if h >= 1:
                    for c in range(2):
                        act.wait_ge(xo_ready, 2 * (h - 1) + c + 1)
                        nc.scalar.activation(a_hi[:, 2 * (h - 1) + c, :], bank[6 + c][:, 0:SEQ], ACT.Copy)\
                            .then_inc(xo_evac, 1)
            for c in range(2):
                act.wait_ge(xo_ready, 2 * (X_HEADS - 1) + c + 1)
                nc.scalar.activation(a_hi[:, 2 * (X_HEADS - 1) + c, :], bank[6 + c][:, 0:SEQ], ACT.Copy)\
                    .then_inc(xo_evac, 1)
            split_hi_through(len(units) - 1)
            wait_evac(act, "xo11")
            norm_stats(3, xres, xn2)
            act.wait_ge(rexp_in, 1)
            nc.scalar.activation(rt[:, 80:88], rt[:, 80:88], ACT.Exp).then_inc(rexp_done, 1)
            act.wait_ge(rexp_in, 2)
            nc.scalar.activation(rt[:, 96:98], rt[:, 96:98], ACT.Exp).then_inc(rexp_done, 1)
            act.wait_ge(xpt_ready, X_HEADS)
            act.dma_start(gain_f, norm_final.rearrange("(o d) -> o d", o=1).to_broadcast([P, D]))\
                .then_inc(gainf_in, 16)

            act.wait_ge(route_ready, 1)
            n_iter = act.value_load(n_it[0:1, 0:1], min_val=PAIRS, max_val=PAIRS * MAX_PASSES)
            with act.Fori(0, n_iter) as i:
                act.wait_ge(up_used, i + 1)
                nc.scalar.activation(hs, bank[4][:, :], ACT.Silu).then_inc(m_silu, 1)
                act.wait_ge(down_used, i + 1)
                nc.scalar.activation(yj[:, 0:512], bank[2][:, :], ACT.Copy).then_inc(m_y0, 1)
            act.wait_ge(moe_done, 1)
            for i in range(NT):
                for c in range(2):
                    last = nc.scalar.activation(junk[:, 2 * i + c, :], acc_bank[i][c][:, :], ACT.Square,
                                                accum_out=st[:, 128 + 2 * i + c:129 + 2 * i + c])
            last.then_inc(f_ssq, 1)
            act.wait_ge(f_ms, 1)
            nc.scalar.activation(st[:, 136:138], st[:, 136:138], ACT.Sqrt).then_inc(f_rstd, 1)

        @block.vector
        def _(dve):
            chain = [0]

            def link(ins):
                chain[0] += 1
                ins.then_inc(dve_chain, 1)
                dve.wait_ge(dve_chain, chain[0])

            tt, ts_, stt = nc.vector.tensor_tensor, nc.vector.tensor_scalar, nc.vector.scalar_tensor_tensor
            group, split, split_groups = [0], [0], [0]

            def split_lo_through(n):
                while split[0] <= min(n, len(units) - 1):
                    m = split[0]
                    split[0] += 1
                    if m in LOW_ON_POOL:
                        continue
                    w = unit_len(m)
                    dve.wait_ge(hi_done, m + 1)
                    tt(lo_w[:, m % RING, 0:w], raw_w[:, m % RING, 0:w], hi_w[:, m % HI_RING, 0:w].bitcast(F32),
                       ALU.subtract).then_inc(lo_done, 1)

            def norm_rows(n, src, dst):
                dve.wait_ge(ssq_done, n + 1)
                c = 4 * n
                link(ts_(st[:, c + 2:c + 4], st[:, c:c + 2], 1.0 / D, EPS, ALU.mult, ALU.add))
                nc.vector.reciprocal(st[:, c + 2:c + 4], st[:, c + 2:c + 4]).then_inc(ms_ready, 1)
                dve.wait_ge(rstd_done, n + 1)
                for i in range(NT):
                    ts_(dst[:, i, :], src[:, i, :], st[:, c + 2 + i:c + 3 + i], None, ALU.mult).then_inc(xn_ready, 1)

            def columns_of(i, gain, hiT, loT, tiles=1):
                def low(i, q, g):
                    dve.wait_ge(tr_hi, g + 1)
                    blk = (slice(None), slice(4 * q, 4 * q + 4), slice(P * i, P * i + P))
                    tt(loT[blk], tr_tmp[:, g % 2, :].rearrange("p (k t) -> p k t", k=4), hiT[blk].bitcast(F32),
                       ALU.subtract).then_inc(tr_evac, 1)

                before = None
                for ii in range(i, i + tiles):
                    for q in range(2):
                        g = group[0]
                        dve.wait_ge(tr_ready, g + 1)
                        if g >= 2:
                            dve.wait_ge(tr_evac, g - 1)
                        ps = bank[2 + g % 2][:, :].rearrange("p (k t) -> p k t", k=4)
                        gb = gain[:, 4 * q:4 * q + 4].unsqueeze(2).to_broadcast([P, 4, P])
                        tt(tr_tmp[:, g % 2, :].rearrange("p (k t) -> p k t", k=4), ps, gb, ALU.mult)\
                            .then_inc(tr_gain, 1)
                        if before is not None:
                            low(*before)
                        before = (ii, q, g)
                        group[0] += 1
                low(*before)

            def columns_f32(gain, dstT):
                for i in range(NT):
                    for q in range(2):
                        g = group[0]
                        dve.wait_ge(tr_ready, g + 1)
                        tt(dstT[:, 4 * q:4 * q + 4, P * i:P * i + P],
                           bank[2 + g % 2][:, :].rearrange("p (k t) -> p k t", k=4),
                           gain[:, 4 * q:4 * q + 4].unsqueeze(2).to_broadcast([P, 4, P]), ALU.mult)\
                            .then_inc(tr_evac, 1)
                        group[0] += 1

            dve.wait_ge(gmix_in, 16)
            norm_rows(0, xres, xn0)
            columns_of(0, g_mix, u_hi, u_lo, NT)
            split_lo_through(2)
            dve.wait_ge(consts, 1)
            dve.wait_ge(prm_in, 16 * N_PRM)

            dve.wait_ge(prm_tr, 1)
            nc.vector.tensor_copy(prm[:, 0:136], bank[4][:, 0:136]).then_inc(prm_ready, 1)
            nc.vector.tensor_copy(dskip, bank[5][:, 0:16]).then_inc(prm_ready, 1)

            wait_evac(dve, "tm1")
            r = st[:, 224:288].rearrange("p (i h) -> p i h", i=NT)
            e1 = st[:, 160:224].rearrange("p (i h) -> p i h", i=NT)
            e2 = st[:, 288:352].rearrange("p (i h) -> p i h", i=NT)
            z2 = st[:, 352:416].rearrange("p (i h) -> p i h", i=NT)
            hb = dtb.unsqueeze(1).to_broadcast([P, NT, SSM_HEADS])
            link(tt(r, small_tm[:, :, SM_DT - SM_V:SM_DT - SM_V + SSM_HEADS], hb, ALU.add))
            link(ts_(dt, r, 0.0, None, ALU.max))
            stt(e1, dt, -2.0, r, ALU.mult, ALU.add).then_inc(dt_exp_in, 1)
            dve.wait_ge(dt_exp_in, 1)
            dve.wait_ge(dt_exp, 1)
            link(ts_(e2, e1, 2.0, None, ALU.add))
            link(nc.vector.reciprocal(e2, e2))
            link(tt(e1, e1, e2, ALU.mult))
            link(tt(z2, e1, e1, ALU.mult))
            link(ts_(e2, z2, 1.0 / 19, None, ALU.mult))
            for k in (17, 15, 13, 11, 9, 7, 5, 3):
                link(stt(e2, e2, 1.0 / k, z2, ALU.add, ALU.mult))
            link(stt(e2, e2, 1.0, e1, ALU.add, ALU.mult))
            link(stt(dt, e2, 2.0, dt, ALU.mult, ALU.add))
            stt(dA, dt, -1.0, alog.unsqueeze(1).to_broadcast([P, NT, SSM_HEADS]), ALU.mult, ALU.mult)\
                .then_inc(dt_ready, 1)
            link(ts_(small_tm[:, :, SM_WI - SM_V:SM_WI - SM_V + 8], small_tm[:, :, SM_WI - SM_V:SM_WI - SM_V + 8],
                     IDX_HEADS ** -0.5 * HEAD ** -0.5, None, ALU.mult))

            for b in range(4):
                split_lo_through(UN["qi0"] + 2 + b // 2)
                dve.wait_ge(idx_relu, b + 1)
                for a in range(2):
                    h = 2 * b + a
                    for i, (lo, hi) in enumerate(((0, 128), (128, 384))):
                        w = hi - lo
                        src = rel[:, b % 2, 128 * a:128 * a + 128] if i == 0 else \
                            rel[:, b % 2, 256 + 256 * a:512 + 256 * a]
                        wi = small_tm[:, i, SM_WI - SM_V + h:SM_WI - SM_V + h + 1]
                        if h == 0:
                            link(ts_(isc[:, lo:hi], src, wi, None, ALU.mult))
                        elif h < 7 or i == 0:
                            link(stt(isc[:, lo:hi], src, wi, isc[:, lo:hi], ALU.mult, ALU.add))
                        else:
                            link(stt(isc[:, lo:hi], src, wi, isc[:, lo:hi], ALU.mult, ALU.add))
                nc.vector.tensor_copy(st[:, 472:473], st[:, 473:474]).then_inc(idx_used, 1)
            dve.wait_ge(consts, 2)
            link(stt(selm[:, :], caus[:, :], 0.0, isc[:, :], ALU.is_ge, ALU.mult))
            link(tt(isc[:, :], selm[:, :], caus[:, :], ALU.add))

            def topk_round(i):
                lo, hi = ((0, 128), (128, 384))[i]
                m8 = st[:, 416 + 8 * i:424 + 8 * i]
                link(nc.vector.max(out=m8, in_=isc[:, lo:hi]))
                link(nc.vector.match_replace(out=isc[:, lo:hi], in_to_replace=m8, in_values=isc[:, lo:hi],
                                             imm_value=TAKEN))

            def decay_and_cb():
                for g in range(N_GROUPS):
                    dve.wait_ge(cb_ready, g + 1)
                    ps = bank[4 + g % 2]
                    tt(cbm[:, g, 0:128], ps[:, 0:128], tri[:, :], ALU.mult)
                    nc.vector.tensor_copy(cbm[:, g, 128:256], ps[:, 128:256])
                    tt(cbm[:, g, 256:384], ps[:, 256:384], tri[:, :], ALU.mult).then_inc(cb_done, 1)
                dve.wait_ge(acs_ready, 1)
                ts_(bias3[:, 0, :], bank[6][:, 0:32], -1.0, None, ALU.mult)
                ts_(bias3[:, 2, :], bank[6][:, 32:64], -1.0, None, ALU.mult)
                nc.vector.tensor_copy(bias3[:, 1, :], bank[6][:, 64:96]).then_inc(acs_done, 1)
                dve.wait_ge(acs_done, 1)
                tt(bias3[:, 1, :], bias3[:, 1, :], bias3[:, 0, :], ALU.add).then_inc(acs_done, 1)

            dve.wait_ge(prm_ready, 2)
            for n in range(24):
                if n % 2 == 0:
                    split_lo_through(UN["bc0"] + n // 2 + 2)
                wait_evac(dve, STEP["bc0"] + n)
                if n >= 2:
                    dve.wait_ge(conv_silu, n - 1)
                rb, cbuf = raw[:, n % 3, :], cacc[:, n % 2, :]
                ch = n + 16 if n < 8 else n - 8
                link(ts_(cbuf, rb[:, 3:259], cw[:, 3, ch:ch + 1], cbias[:, ch:ch + 1], ALU.mult, ALU.add))
                for k in (2, 1):
                    link(stt(cbuf, rb[:, k:k + 256], cw[:, k, ch:ch + 1], cbuf, ALU.mult, ALU.add))
                stt(cbuf, rb[:, 0:256], cw[:, 0, ch:ch + 1], cbuf, ALU.mult, ALU.add).then_inc(conv_done, 1)
                if n % 3 == 0:
                    topk_round(n % 2)
                if n == 15:
                    decay_and_cb()
            for j in range(4):
                split_lo_through(UN["q0"] + j + 2)
                topk_round(0)
                topk_round(1)
            link(ts_(selm[:, :], isc[:, :], TAKEN, -1.0, ALU.is_equal, ALU.add))
            stt(selm[:, :], selm[:, :], -NEG, caus[:, :], ALU.mult, ALU.add).then_inc(mask_ready, 1)

            for i in range(NT):
                for q in range(4):
                    n = 4 * i + q
                    dve.wait_ge(xt_ready, n + 1)
                    ps = bank[2 + n % 2][:, :].rearrange("p (h c) -> p h c", c=HEAD)
                    d = xdt[:, i, 512 * q:512 * q + 512].rearrange("p (h c) -> p h c", c=HEAD)
                    tt(d, ps, dt[:, i, 8 * q:8 * q + 8].unsqueeze(2).to_broadcast([P, 8, HEAD]), ALU.mult)\
                        .then_inc(xdt_done, 1)

            def softmax_in(b):
                dve.wait_ge(sc_ready, b + 1)
                c = 72 + 4 * (b % 2)
                for a in range(2):
                    dve.wait_ge(albi_ready, 2 * b + a + 1)
                    pb = prob[:, 2 * (b % 2) + a, :]
                    if b >= 2:
                        dve.wait_ge(pt_ready, 2 * (b - 1))
                    tt(pb[:, 0:128], bank[4][:, 128 * a:128 * a + 128], albi[:, a, 0:128], ALU.add)
                    tt(pb[:, 128:384], bank[5][:, 256 * a:256 * a + 256], albi[:, a, 128:384], ALU.add)\
                        .then_inc(sc_used, 1)
                dve.wait_ge(sc_used, 2 * b + 2)
                for a in range(2):
                    pb = prob[:, 2 * (b % 2) + a, :]
                    nc.vector.tensor_reduce(out=st[:, c + 2 * a:c + 2 * a + 1], in_=pb[:, 0:128], axis=AXX,
                                            op=ALU.max, negate=True)
                    last = nc.vector.tensor_reduce(out=st[:, c + 2 * a + 1:c + 2 * a + 2], in_=pb[:, 128:384],
                                                   axis=AXX, op=ALU.max, negate=True)
                last.then_inc(mx_ready, 1)

            def sums(b):
                c = 80 + 4 * (b % 2)
                dve.wait_ge(exp_done, b + 1)
                nc.vector.reciprocal(st[:, c + 16:c + 20], st[:, c:c + 4]).then_inc(rcp_ready, 1)

            def probs_out(b):
                for a in range(2):
                    dve.wait_ge(pt_ready, 2 * b + a + 1)
                    if b >= 1:
                        dve.wait_ge(pv_ready, b)
                    nc.vector.tensor_copy(probT[:, a, :], bank[2 + a][:, 0:384]).then_inc(pt_evac, 1)

            def values_lo(b):
                dve.wait_ge(pv_evac, b + 1)
                tt(a_lo[:, b, :], bank[6 + b % 2][:, 0:SEQ], a_hi[:, b, :].bitcast(F32), ALU.subtract)\
                    .then_inc(pv_lo, 1)

            softmax_in(0)
            for b in range(8):
                sums(b)
                if b + 1 < 8:
                    softmax_in(b + 1)
                split_lo_through(UN[f"z{b}"] + 2)
                if b >= 1:
                    values_lo(b - 1)
                probs_out(b)

            def y_out(b):
                dve.wait_ge(y_ready, b + 1)
                stt(ysT[:, b, :], ysT[:, b, :], dskip[:, b:b + 1], bank[6 + b % 2][:, 0:SEQ], ALU.mult, ALU.add)\
                    .then_inc(y_used, 1)

            def gated_lo(b):
                dve.wait_ge(y_hi_done, b + 1)
                tt(z_lo[:, b, :], zs[:, b, :], y_hi[:, b, :].bitcast(F32), ALU.subtract).then_inc(y_lo_done, 1)

            for b in range(16):
                dve.wait_ge(r_ready, b + 1)
                if b == 0:
                    dve.wait_ge(pt_ready, 16)
                if b >= 2:
                    dve.wait_ge(m_ready, 2 * (b - 1))
                for a in range(2):
                    h = 2 * b + a
                    sg = seg[:, 2 * (b % 2) + a, :]
                    rr = bank[4 + b % 2][:, 256 * a:256 * a + 256]
                    ts_(sg[:, 0:128], rr[:, 0:128], bias3[:, 0, h:h + 1], 0.0, ALU.add, ALU.min)
                    ts_(sg[:, 128:256], rr[:, 128:256], bias3[:, 1, h:h + 1], 0.0, ALU.add, ALU.min)
                    ts_(sg[:, 256:384], rr[:, 128:256], bias3[:, 2, h:h + 1], 0.0, ALU.add, ALU.min)\
                        .then_inc(seg_ready, 1)
                if b == 0:
                    values_lo(7)
                if b % 2 == 0:
                    split_lo_through(UN[f"g{b // 2}"] + 2)
                if b >= 1:
                    y_out(b - 1)
                if b >= 4:
                    gated_lo(b - 4)
            y_out(15)
            split_lo_through(UN["ao0"] + 2)
            for b in range(12, 16):
                gated_lo(b)
            dve.wait_ge(gsig, 1)

            def att_gate(b):
                n = STEP[f"ao{b}"]
                if b % 2 == 0:
                    split_lo_through(UN[f"ao{b // 2}"] + 2)
                dve.wait_ge(proj_ready, n + 1)
                tt(gates[:, 8 + b, :], bank[n % 2][:, 0:SEQ], gates[:, 8 + b, :], ALU.mult).then_inc(evac_dve, 1)

            for b in range(8):
                att_gate(b)
                if b == 1:
                    dve.wait_ge(ssq_mm, 16)
                    link(ts_(rs_bc, bank[2][:, 0:SEQ], 1.0 / D_INNER, EPS, ALU.mult, ALU.add))
                    nc.vector.reciprocal(rs_bc, rs_bc).then_inc(gn_ms, 1)
                if b == 3:
                    norm_rows(1, memx, memn)
                if b == 5:
                    columns_of(0, g_mem, u_hi, u_lo)
            columns_of(1, g_mem, u_hi, u_lo)
            dve.wait_ge(gn_rstd, 1)
            for b in range(8):
                if b % 2 == 0:
                    split_lo_through(UN[f"kx{b // 2}"] + 2)
                if b == 0:
                    dve.wait_ge(gsig, 2)
                link(tt(gates[:, b, :], gates[:, b, :], rs_bc, ALU.mult))
            for c in range(2):
                for h in range(2):
                    split_lo_through(UN[f"vx{c}{h}"] + 2)
            for b in range(8):
                n = STEP[f"so{b}"]
                split_lo_through(UN[f"so{b}"] + 2)
                dve.wait_ge(proj_ready, n + 1)
                if b == 0:
                    dve.wait_ge(pv_lo, 8)
                m = mix_tmp[:, b % 2, :]
                if b >= 2:
                    dve.wait_ge(mix_hi, b - 1)
                tt(m, bank[n % 2][:, 0:SEQ], gates[:, b, :], ALU.mult).then_inc(evac_dve, 1)
                wait_evac(dve, n)
                tt(m, m, gates[:, 8 + b, :], ALU.add).then_inc(mix_ready, 1)
                dve.wait_ge(mix_hi, b + 1)
                tt(a_lo[:, b, :], m, a_hi[:, b, :].bitcast(F32), ALU.subtract).then_inc(y_lo_done, 1)

            def residual(prefix):
                for c in range(2):
                    for i in range(NT):
                        n = STEP[f"{prefix}{c}{i}"]
                        split_lo_through(UN[f"{prefix}{c}{i}"] + 2)
                        dve.wait_ge(proj_ready, n + 1)
                        d = xres[:, i, 512 * c:512 * c + 512]
                        tt(d, bank[n % 2][:, :], d, ALU.add).then_inc(evac_dve, 1)

            dve.wait_ge(x_in, 64)
            residual("mo")
            wait_evac(dve, "mo11")
            norm_rows(2, xres, xn1)
            columns_of(0, g_x, a_hi, a_lo, NT)
            for j in range(4):
                split_lo_through(UN[f"qx{j}"] + 2)

            def cross_lo(h):
                for c in range(2):
                    b = 2 * h + c
                    dve.wait_ge(xo_evac, b + 1)
                    tt(a_lo[:, b, :], bank[6 + c][:, 0:SEQ], a_hi[:, b, :].bitcast(F32), ALU.subtract)\
                        .then_inc(xo_lo, 1)

            for h in range(X_HEADS):
                for i in range(NT):
                    n = NT * h + i
                    dve.wait_ge(xs_ready, n + 1)
                    nc.vector.tensor_reduce(out=st[:, 104 + n:105 + n], in_=bank[4 + i][:, 0:256], axis=AXX,
                                            op=ALU.max, negate=True).then_inc(xmx_ready, 1)
                for i in range(NT):
                    n = NT * h + i
                    dve.wait_ge(xexp_done, n + 1)
                    link(nc.vector.reciprocal(st[:, 120 + n:121 + n], st[:, 112 + n:113 + n]))
                    pb = pX[:, 2 * (h % 2) + i, 0:256]
                    ts_(pb, pb, st[:, 120 + n:121 + n], None, ALU.mult).then_inc(xpn_ready, 1)
                dve.wait_ge(xpt_ready, h + 1)
                if h >= 1:
                    dve.wait_ge(xo_ready, 2 * h)
                nc.vector.tensor_copy(pXT[:, 0, 0:256], bank[2][:, 0:256])
                nc.vector.tensor_copy(pXT[:, 1, 0:256], bank[2][:, 256:512]).then_inc(xpt_evac, 1)
                if h >= 1:
                    cross_lo(h - 1)
            cross_lo(X_HEADS - 1)
            residual("xo")
            wait_evac(dve, "xo11")
            norm_rows(3, xres, xn2)
            columns_f32(g_moe, tT)

            iota_b = iota64[:, :].unsqueeze(1).to_broadcast([P, 2, CAP])

            def select(col):
                for i in range(NT):
                    pc = pos_all[:, i, bass.ds(col, 2)].unsqueeze(2).to_broadcast([P, 2, CAP])
                    last = tt(S[:, i, :, :], iota_b, pc, ALU.is_equal)
                last.then_inc(m_sel, 1)

            L = rt[:, 0:72].rearrange("p (i n) -> p i n", i=NT)
            dve.wait_ge(rl_ready, 1)
            link(tt(L, bank[4][:, 0:72].rearrange("p (i n) -> p i n", i=NT),
                    brt.unsqueeze(1).to_broadcast([P, NT, 36]), ALU.add))
            glog = L[:, :, 0:4]
            gmx = rt[:, 72:74]
            ge = rt[:, 80:88].rearrange("p (i n) -> p i n", i=NT)
            dexp = rt[:, 96:98]
            oh_g = rt[:, 88:96].rearrange("p (i n) -> p i n", i=NT)
            pg = rt[:, 74:76]
            v1, v2, tmp2 = rt[:, 76:78], rt[:, 78:80], rt[:, 98:100]
            em = rt[:, 104:168].rearrange("p (i n) -> p i n", i=NT)
            oh1 = rt[:, 168:232].rearrange("p (i n) -> p i n", i=NT)
            oh2 = rt[:, 232:296].rearrange("p (i n) -> p i n", i=NT)
            msk = rt[:, 296:360].rearrange("p (i n) -> p i n", i=NT)
            cmb = rt[:, 360:424].rearrange("p (i n) -> p i n", i=NT)
            pm = rt[:, 424:488].rearrange("p (i n) -> p i n", i=NT)

            def over(v, n):
                return v.unsqueeze(2).to_broadcast([P, NT, n])

            def first_max(dst, src, rev, n, vmax):
                link(nc.vector.tensor_reduce(out=vmax, in_=src, axis=AXX, op=ALU.max))
                link(tt(dst, src, over(vmax, n), ALU.is_equal))
                link(tt(dst, dst, rev.unsqueeze(1).to_broadcast([P, NT, n]), ALU.mult))
                link(nc.vector.tensor_reduce(out=tmp2, in_=dst, axis=AXX, op=ALU.max))
                link(tt(dst, dst, over(tmp2, n), ALU.is_equal))

            first_max(oh_g, glog, rev4, GROUPS, gmx)
            tt(ge, glog, over(gmx, GROUPS), ALU.subtract).then_inc(rexp_in, 1)
            link(ts_(oh2[:, :, 0:4], oh_g, -1.0, -NEG, ALU.add, ALU.mult))
            link(tt(em.rearrange("p i (g e) -> p i g e", g=GROUPS),
                    L[:, :, 4:36].rearrange("p i (g e) -> p i g e", g=GROUPS),
                    oh2[:, :, 0:4].unsqueeze(3).to_broadcast([P, NT, GROUPS, PER_GROUP]), ALU.add))
            first_max(oh1, em, rev32, EXPERTS, v1)
            link(stt(em, oh1, 3 * NEG, em, ALU.mult, ALU.add))
            first_max(oh2, em, rev32, EXPERTS, v2)
            tt(dexp, v2, v1, ALU.subtract).then_inc(rexp_in, 1)
            tt(msk, oh1, oh2, ALU.add).then_inc(rmask, 1)
            dve.wait_ge(rexp_done, 1)
            link(nc.vector.tensor_reduce(out=pg, in_=ge, axis=AXX, op=ALU.add))
            link(nc.vector.reciprocal(pg, pg))
            dve.wait_ge(rexp_done, 2)
            link(ts_(tmp2, dexp, 1.0, None, ALU.add))
            link(nc.vector.reciprocal(tmp2, tmp2))
            link(tt(v1, pg, tmp2, ALU.mult))
            link(tt(v2, v1, dexp, ALU.mult))
            link(tt(oh1, oh1, over(v1, EXPERTS), ALU.mult))
            link(tt(oh2, oh2, over(v2, EXPERTS), ALU.mult))
            link(tt(cmb, oh1, oh2, ALU.add))
            nc.vector.memset(pos_all[:, :, MAX_PASSES * EXPERTS:], -1000.0)
            nc.vector.memset(comb_all[:, :, MAX_PASSES * EXPERTS:], 0.0)
            for k in range(MAX_PASSES):
                last = nc.vector.tensor_copy(comb_all[:, :, EXPERTS * k:EXPERTS * k + EXPERTS], cmb)
            link(last)
            dve.wait_ge(rpos, 1)
            link(tt(pm, bank[5][:, 0:64].rearrange("p (i n) -> p i n", i=NT), msk, ALU.mult))
            link(ts_(pos_all[:, :, 0:EXPERTS], pm, -1.0, None, ALU.add))
            select(0)
            for k in range(1, MAX_PASSES):
                ts_(pos_all[:, :, EXPERTS * k:EXPERTS * k + EXPERTS], pm, -1.0 - CAP * k, None, ALU.add)
            link(nc.vector.tensor_reduce(out=rt[:, 500:501], in_=bank[5][:, 64:96], axis=AXX, op=ALU.max))
            link(ts_(rt[:, 501:502], rt[:, 500:501], CAP + 0.5, 1.0, ALU.is_gt, ALU.add))
            for k in range(2, MAX_PASSES):
                link(stt(rt[:, 501:502], rt[:, 500:501], CAP * k + 0.5, rt[:, 501:502], ALU.is_gt, ALU.add))
            ts_(n_it[:, 0:1], rt[:, 501:502], float(PAIRS), None, ALU.mult)
            ts_(n_it[:, 2:3], rt[:, 501:502], float(PAIRS // 2), None, ALU.mult)
            nc.vector.tensor_copy(n_it[:, 1:2], rt[:, 501:502]).then_inc(route_ready, 1)
            dve.wait_ge(route_ready, 1)

            def gathered_out(n):
                dve.wait_ge(m_gath, n)
                for q in range(2):
                    gb = g_moe[:, 4 * q:4 * q + 4].unsqueeze(2).to_broadcast([P, 4, P])
                    last = tt(xg[:, 4 * q:4 * q + 4, :], bank[2 + q][:, :].rearrange("p (k j) -> p k j", k=4), gb,
                              ALU.mult)
                last.then_inc(m_xg, 1)

            n_iter = dve.value_load(n_it[0:1, 0:1], min_val=PAIRS, max_val=PAIRS * MAX_PASSES)
            gathered_out(1)
            with dve.Fori(0, n_iter) as it:
                dve.wait_ge(m_sel, it + 1)
                for i in range(NT):
                    cc = comb_all[:, i, bass.ds(2 * it, 2)].unsqueeze(2).to_broadcast([P, 2, CAP])
                    last = tt(Sw[:, i, :, :], S[:, i, :, :], cc, ALU.mult)
                last.then_inc(m_sw, 1)
                dve.wait_ge(m_sw, it + 1)
                select(2 * it + 2)
                dve.wait_ge(m_silu, it + 1)
                tt(hh, hs, bank[5][:, :], ALU.mult).then_inc(m_h, 1)
                gathered_out(it + 2)
                dve.wait_ge(m_tr, it + 1)
                nc.vector.tensor_copy(hT[:, :, :], bank[4][:, :].rearrange("p (k j) -> p k j", k=4)).then_inc(m_ht, 1)
                nc.vector.tensor_copy(SwT[:, :, :], bank[5][:, 0:256].rearrange("p (i t) -> p i t", i=NT))\
                    .then_inc(m_st, 1)
                dve.wait_ge(down_used, it + 1)
                nc.vector.tensor_copy(yj[:, 512:1024], bank[3][:, :]).then_inc(m_y1, 1)

            dve.wait_ge(f_ssq, 1)
            link(nc.vector.tensor_reduce(out=st[:, 136:138], in_=st[:, 128:132].rearrange("p (i c) -> p i c", c=2),
                                         axis=AXX, op=ALU.add))
            link(ts_(st[:, 136:138], st[:, 136:138], 1.0 / D, EPS, ALU.mult, ALU.add))
            nc.vector.reciprocal(st[:, 136:138], st[:, 136:138]).then_inc(f_ms, 1)
            dve.wait_ge(f_rstd, 1)
            dve.wait_ge(gainf_in, 16)
            for i in range(NT):
                for c in range(2):
                    last = stt(outb[:, i, 512 * c:512 * c + 512], acc_bank[i][c][:, :], st[:, 136 + i:137 + i],
                               gain_f[:, 512 * c:512 * c + 512], ALU.mult, ALU.mult)
                last.then_inc(f_out, 1)

        @block.tensor
        def _(pe):
            mm, tp = nc.tensor.matmul, nc.tensor.transpose
            group = [0]

            def use_unit(name):
                wait_low(pe, UN[name])
                return parts(name)

            def product(dst, left, right, first, last):
                mm(dst, left[0], right[0], start=first, stop=False)
                mm(dst, left[0], right[1], start=False, stop=False)
                return mm(dst, left[1], right[0], start=False, stop=last)

            u_parts, a_parts, y_parts = (u_hi, u_lo), (a_hi, a_lo), (y_hi, z_lo)

            def transposes_of(xn, i, split=True):
                pe.wait_ge(xn_ready, group[0] // 2 + 1)
                for q in range(2):
                    g = group[0]
                    if g >= 2:
                        pe.wait_ge(tr_gain if split else tr_evac, g - 1)
                    for k in range(4):
                        last = tp(bank[2 + g % 2][:, P * k:P * k + P], xn[:, i, 4 * q + k::KT], ident[:, :])
                    last.then_inc(tr_ready, 1)
                    group[0] += 1

            def transposes(xn, split=True):
                for i in range(NT):
                    transposes_of(xn, i, split)

            def bank_of(name):
                n = STEP[name]
                if n >= 2:
                    wait_evac(pe, n - 2)
                return bank[n % 2]

            def fm_step(name, w, c0, act_parts, nk=KT):
                b = bank_of(name)
                for k in range(nk):
                    last = product(b[:, 0:SEQ], [x[:, k, c0:c0 + P] for x in w], [x[:, k, :] for x in act_parts],
                                   k == 0, k == nk - 1)
                last.then_inc(proj_ready, 1)

            def tm_steps(prefix, c, act_parts):
                banks = [bank_of(f"{prefix}{c}{i}") for i in range(NT)]
                for half in range(2):
                    w = use_unit(f"{prefix}{c}{half}")
                    for i in range(NT):
                        for k in range(4):
                            last = product(banks[i][:, :], [x[:, 4 * half + k, P * i:P * i + P] for x in act_parts],
                                           [x[:, k, :] for x in w], half == 0 and k == 0, half == 1 and k == 3)
                        if half == 1:
                            last.then_inc(proj_ready, 1)

            pe.wait_ge(ident_ready, 1)
            transposes(xn0)
            pe.wait_ge(consts, 1)
            pe.wait_ge(tr_evac, 4)
            w = use_unit("kk")
            fm_step("k", w, 0, u_parts)
            fm_step("ki", w, P, u_parts)
            w = use_unit("tm")
            for i in range(NT):
                b = bank_of(f"tm{i}")
                for k in range(KT):
                    last = product(b[:, 0:TM_W], [x[:, k, P * i:P * i + P] for x in u_parts],
                                   [x[:, k, :] for x in w], k == 0, k == KT - 1)
                last.then_inc(proj_ready, 1)

            pe.wait_ge(prm_in, 16 * N_PRM)
            for k in range(CONV_K):
                tp(bank[4][:, 24 * k:24 * k + 24], cwrow[:, k::CONV_K], ident[0:24, 0:24])
            tp(bank[4][:, 96:136], prow[:, :], ident[0:40, 0:40])
            mm(bank[5][:, 0:16], sel2[:, :], drow[:, :], start=True, stop=True).then_inc(prm_tr, 1)

            def indexer(b):
                wait_evac(pe, f"qi{b}")
                if b == 0:
                    pe.wait_ge(prm_ready, 2)
                else:
                    pe.wait_ge(idx_relu, b)
                mm(bank[4][:, 0:256].rearrange("p (a s) -> p a s", a=2), qiT[:, b, 0:P], kiz[:, :, 0:P],
                   start=True, stop=True)
                mm(bank[5][:, :].rearrange("p (a s) -> p a s", a=2), qiT[:, b, P:SEQ], kiz[:, :, :],
                   start=True, stop=True).then_inc(idx_ready, 1)

            for b in range(4):
                if b % 2 == 0:
                    w = use_unit(f"qi{b // 2}")
                fm_step(f"qi{b}", w, P * (b % 2), u_parts)
                if b >= 1:
                    indexer(b - 1)
            for b in range(8):
                if b % 2 == 0:
                    w = use_unit(f"bc{b // 2}")
                fm_step(f"bc{b}", w, P * (b % 2), u_parts)
                if b == 0:
                    indexer(3)
            for b in range(16):
                if b % 2 == 0:
                    w = use_unit(f"xs{b // 2}")
                fm_step(f"xs{b}", w, P * (b % 2), u_parts)
                if b == 3:
                    pe.wait_ge(dt_ready, 1)
                    mm(bank[6][:, 0:32], tri[:, :], dA[:, 0, :], start=True, stop=True)
                    mm(bank[6][:, 32:64], tri[:, :], dA[:, 1, :], start=True, stop=True)
                    mm(bank[6][:, 64:96], ones[:, :], dA[:, 0, :], start=True, stop=True).then_inc(acs_ready, 1)
                if b == 7:
                    pe.wait_ge(conv_silu, 8)
                    pe.wait_ge(idx_relu, 4)
                    for g in range(N_GROUPS):
                        if g >= 2:
                            pe.wait_ge(cb_done, g - 1)
                        mm(bank[4 + g % 2][:, 0:256], bc[:, g, 0:P], bc[:, 4 + g, :], start=True, stop=True)
                        mm(bank[4 + g % 2][:, 256:384], bc[:, g, P:SEQ], bc[:, 4 + g, P:SEQ], start=True,
                           stop=True).then_inc(cb_ready, 1)
            for b in range(8):
                if b % 2 == 0:
                    w = use_unit(f"q{b // 2}")
                fm_step(f"q{b}", w, P * (b % 2), u_parts)
            for i in range(NT):
                for q in range(4):
                    n = 4 * i + q
                    pe.wait_ge(conv_silu, 24)
                    if n >= 2:
                        pe.wait_ge(xdt_done, n - 1)
                    for c in range(4):
                        last = tp(bank[2 + n % 2][:, P * c:P * c + P], ysT[:, 4 * q + c, P * i:P * i + P], ident[:, :])
                    last.then_inc(xt_ready, 1)

            def scores(b):
                wait_evac(pe, f"q{b}")
                if b == 0:
                    pe.wait_ge(cb_done, N_GROUPS)
                else:
                    pe.wait_ge(sc_used, 2 * b)
                mm(bank[4][:, 0:256].rearrange("p (a s) -> p a s", a=2), qT[:, b, 0:P], kz[:, :, 0:P],
                   start=True, stop=True)
                mm(bank[5][:, :].rearrange("p (a s) -> p a s", a=2), qT[:, b, P:SEQ], kz[:, :, :],
                   start=True, stop=True).then_inc(sc_ready, 1)

            def prob_transposes(b):
                for a in range(2):
                    pe.wait_ge(pn_ready, 2 * b + a + 1)
                    if b == 0:
                        pe.wait_ge(xdt_done, 8)
                    else:
                        pe.wait_ge(pt_evac, 2 * (b - 1) + a + 1)
                    pb = prob[:, 2 * (b % 2) + a, :]
                    for c in range(3):
                        last = tp(bank[2 + a][:, P * c:P * c + P], pb[:, P * c:P * c + P], ident[:, :])
                    last.then_inc(pt_ready, 1)

            def weighted_sum(dst, left0, left1, right):
                mm(dst[:, 0:256], left0, right[:, 0:256], start=True, stop=False, skip_group_check=True)
                return mm(dst[:, 128:256], left1, right[:, 256:384], start=False, stop=True, skip_group_check=True)

            def values(b):
                pe.wait_ge(pt_evac, 2 * b + 2)
                if b >= 2:
                    pe.wait_ge(pv_lo, b - 1)
                if b == 0:
                    pe.wait_ge(acs_done, 2)
                for a in range(2):
                    last = weighted_sum(bank[6 + b % 2][64 * a:64 * a + 64, :], small_tm[:, 0, 0:HEAD],
                                        small_tm[:, 1, 0:HEAD], probT[:, a, :])
                last.then_inc(pv_ready, 1)

            scores(0)
            for b in range(8):
                if b + 1 < 8:
                    scores(b + 1)
                w = use_unit(f"z{b}")
                fm_step(f"z{2 * b}", w, 0, u_parts)
                if b >= 1:
                    values(b - 1)
                fm_step(f"z{2 * b + 1}", w, P, u_parts)
                prob_transposes(b)

            def cumsum_rows(b):
                if b < 2:
                    pe.wait_ge(sc_used, 16)
                else:
                    pe.wait_ge(seg_ready, 2 * (b - 1))
                for a in range(2):
                    for i in range(NT):
                        left = dA[:, i, 2 * b + a:2 * b + a + 1].to_broadcast([P, P])
                        last = mm(bank[4 + b % 2][:, 256 * a + P * i:256 * a + P * i + P], left, tri[:, :],
                                  start=True, stop=True)
                last.then_inc(r_ready, 1)

            def sum_squares(b):
                pe.wait_ge(sq_ready, b + 1)
                mm(bank[2][:, 0:SEQ], ones[:, :], ysq[:, b % 2, :], start=(b == 0), stop=(b == 15))\
                    .then_inc(ssq_mm, 1)

            cumsum_rows(0)
            pe.wait_ge(xdt_done, 8)
            for b in range(16):
                if b + 1 < 16:
                    cumsum_rows(b + 1)
                if b % 2 == 0:
                    w = use_unit(f"g{b // 2}")
                fm_step(f"g{b}", w, P * (b % 2), u_parts)
                if b == 0:
                    values(7)
                pe.wait_ge(m_ready, 2 * b + 2)
                if b >= 2:
                    pe.wait_ge(y_used, b - 1)
                else:
                    pe.wait_ge(pv_lo, 7 + b)
                for a in range(2):
                    h = 2 * b + a
                    last = weighted_sum(bank[6 + b % 2][64 * a:64 * a + 64, :], xdt[:, 0, HEAD * h:HEAD * h + HEAD],
                                        xdt[:, 1, HEAD * h:HEAD * h + HEAD], mdec[:, 2 * ((b + 1) % 2) + a, :])
                last.then_inc(y_ready, 1)
                if b >= 3:
                    sum_squares(b - 3)
            sum_squares(13)

            for b in range(8):
                if b % 2 == 0:
                    w = use_unit(f"ao{b // 2}")
                fm_step(f"ao{b}", w, P * (b % 2), a_parts)
                if b < 2:
                    sum_squares(14 + b)
                if b == 4:
                    pe.wait_ge(gn_ms, 1)
                if b >= 4 and b % 2 == 0:
                    transposes_of(memn, b // 2 - 2)
            pe.wait_ge(tr_evac, 8)
            for b in range(8):
                if b % 2 == 0:
                    w = use_unit(f"kx{b // 2}")
                fm_step(f"kx{b}", w, P * (b % 2), u_parts)
            for c in range(2):
                tm_steps("vx", c, u_parts)
            pe.wait_ge(y_lo_done, 16)
            for b in range(8):
                w = use_unit(f"so{b}")
                fm_step(f"so{b}", w, 0, y_parts, 16)
            pe.wait_ge(y_lo_done, 24)
            for c in range(2):
                tm_steps("mo", c, a_parts)

            transposes(xn1)
            pe.wait_ge(tr_evac, 12)
            for b in range(8):
                if b % 2 == 0:
                    w = use_unit(f"qx{b // 2}")
                fm_step(f"qx{b}", w, P * (b % 2), a_parts)
            wait_evac(pe, "qx7")

            def x_scores(h):
                for i in range(NT):
                    if h == 0:
                        pe.wait_ge(seg_ready, 32)
                    else:
                        pe.wait_ge(xexp_done, NT * (h - 1) + i + 1)
                    for c in range(2):
                        last = mm(bank[4 + i][:, 0:256], qxT[:, 2 * h + c, P * i:P * i + P], kxT[:, 2 * h + c, :],
                                  start=(c == 0), stop=(c == 1))
                    last.then_inc(xs_ready, 1)

            x_scores(0)
            for h in range(X_HEADS):
                if h + 1 < X_HEADS:
                    x_scores(h + 1)
                pe.wait_ge(xpn_ready, NT * (h + 1))
                if h >= 1:
                    pe.wait_ge(xpt_evac, h)
                for m in range(2):
                    for i in range(NT):
                        last = tp(bank[2][:, 256 * m + P * i:256 * m + P * i + P],
                                  pX[:, 2 * (h % 2) + i, P * m:P * m + P], ident[:, :])
                last.then_inc(xpt_ready, 1)
                pe.wait_ge(xpt_evac, h + 1)
                for c in range(2):
                    if h == 0:
                        pe.wait_ge(y_used, 16)
                    else:
                        pe.wait_ge(xo_lo, 2 * (h - 1) + c + 1)
                    for m in range(2):
                        f0 = 256 * h + P * c
                        last = mm(bank[6 + c][:, 0:SEQ], vx[:, m, f0:f0 + P], pXT[:, m, 0:256],
                                  start=(m == 0), stop=(m == 1))
                    last.then_inc(xo_ready, 1)
            pe.wait_ge(xo_lo, 8)
            for c in range(2):
                tm_steps("xo", c, a_parts)

            transposes(xn2, split=False)
            pe.wait_ge(tr_evac, 16)
            pe.wait_ge(xexp_done, 8)
            for i in range(NT):
                for k in range(KT):
                    last = mm(bank[4][:, 36 * i:36 * i + 36], tT[:, k, P * i:P * i + P], wr[:, k, :],
                              start=(k == 0), stop=(k == KT - 1))
            last.then_inc(rl_ready, 1)
            wait_evac(pe, "xo11")
            for i in range(NT):
                for c in range(2):
                    last = mm(acc_bank[i][c][:, :], ident[:, :], xres[:, i, 512 * c:512 * c + 512], start=True,
                              stop=False, skip_group_check=True)
            last.then_inc(residual_in, 1)
            pe.wait_ge(rmask, 1)
            m_t = rt[:, 296:360].rearrange("p (i n) -> p i n", i=NT)
            mm(bank[5][:, 0:32], tri[:, :], m_t[:, 0, :], start=True, stop=True)
            mm(bank[5][:, 32:64], ones[:, :], m_t[:, 0, :], start=True, stop=False)
            mm(bank[5][:, 32:64], tri[:, :], m_t[:, 1, :], start=False, stop=True)
            mm(bank[5][:, 64:96], ones[:, :], m_t[:, 0, :], start=True, stop=False)
            mm(bank[5][:, 64:96], ones[:, :], m_t[:, 1, :], start=False, stop=True).then_inc(rpos, 1)

            def gather():
                for k in range(KT):
                    for i in range(NT):
                        last = mm(bank[2 + k // 4][:, P * (k % 4):P * (k % 4) + P], xn2[:, i, k::KT],
                                  S[:, i, :, :], start=(i == 0), stop=(i == NT - 1))
                last.then_inc(m_gath, 1)

            def gate_up(it, j, odd):
                pe.wait_ge(m_xg, it + 1)
                for ps, slot, turns, used in ((bank[4], GATE[odd], j + 1, gate_used), (bank[5], UP, it + 1, up_used)):
                    for a in range(2):
                        pe.wait_ge(moe_landed[slot + a], 16 * turns)
                    for k in range(KT):
                        for a in range(2):
                            w = moe_slot[slot + a].rearrange("p (t n) -> p t n", t=KT)
                            last = mm(ps[64 * a:64 * a + 64, :], xg[:, k, CAP * a:CAP * a + CAP],
                                      w[:, k, :], start=(k == 0), stop=(k == KT - 1))
                    last.then_inc(used, 1)

            def transposes_and_down(it):
                pe.wait_ge(m_h, it + 1)
                for k in range(4):
                    tp(bank[4][:, P * k:P * k + P], hh[:, k::4], ident[:, :])
                pe.wait_ge(m_sw, it + 1)
                for i in range(NT):
                    last = tp(bank[5][:, P * i:P * i + P], Sw[:, i, :, :], ident[:, :])
                last.then_inc(m_tr, 1)
                for a in range(2):
                    pe.wait_ge(moe_landed[DOWN + a], 16 * it + 16)
                pe.wait_ge(m_xg, it + 2)
                pe.wait_ge(m_ht, it + 1)
                for c in range(2):
                    for k in range(4):
                        for a in range(2):
                            w = moe_slot[DOWN + a].rearrange("p (t n) -> p t n", t=4)
                            last = mm(bank[2 + c][64 * a:64 * a + 64, :], hT[:, k, CAP * a:CAP * a + CAP],
                                      w[:, k, 512 * c:512 * c + 512], start=(k == 0), stop=(k == 3))
                last.then_inc(down_used, 1)

            def scatter(n):
                pe.wait_ge(m_y0, n)
                pe.wait_ge(m_y1, n)
                pe.wait_ge(m_st, n)
                for i in range(NT):
                    for c in range(2):
                        last = mm(acc_bank[i][c][:, :], SwT[:, i, :], yj[:, 512 * c:512 * c + 512],
                                  start=False, stop=False, skip_group_check=True)
                return last

            def pair_of_experts(it, j, odd):
                pe.wait_ge(m_st, it)
                gate_up(it, j, odd)
                pe.wait_ge(m_y0, it)
                pe.wait_ge(m_y1, it)
                pe.wait_ge(m_sel, it + 2)
                gather()
                scatter(it)
                transposes_and_down(it)

            pe.wait_ge(m_sel, 1)
            gather()
            gate_up(0, 0, 0)
            pe.wait_ge(m_sel, 2)
            gather()
            transposes_and_down(0)
            pair_of_experts(1, 0, 1)
            pe.wait_ge(route_ready, 1)
            n_iter = pe.value_load(n_it[0:1, 0:1], min_val=PAIRS, max_val=PAIRS * MAX_PASSES)
            n_twice = pe.value_load(n_it[0:1, 2:3], min_val=PAIRS // 2, max_val=PAIRS // 2 * MAX_PASSES)
            with pe.Fori(1, n_twice) as j:
                for odd in range(2):
                    pair_of_experts(2 * j + odd, j, odd)
            scatter(n_iter).then_inc(moe_done, 1)


_INS = ["x", "mem", "norm_mix", "w_in", "conv_w", "conv_b", "dt_bias", "a_log", "d_skip", "ssm_norm",
        "w_ssm_out", "w_att_out", "w_mix_out", "norm_x", "norm_mem", "w_xq", "w_xkv", "w_xo", "norm_moe",
        "w_rg", "b_rg", "w_re", "b_re", "w_e_gate", "w_e_up", "w_e_down", "norm_final"]
_OUTS = [((1, 256, 1024), "float32")]


def kernel(**inputs):
    import numpy as _np
    import concourse.bacc as _bacc
    from concourse import mybir as _mybir
    from concourse.bass_utils import run_bass_kernel_spmd as _run

    nc = _bacc.Bacc("TRN2", target_bir_lowering=False, num_devices=1)
    arrays, args = {}, []
    for name in _INS:
        a = _np.ascontiguousarray(inputs[name])
        arrays[f"in_{name}_dram"] = a
        args.append(nc.dram_tensor(f"in_{name}_dram", a.shape, _mybir.dt.from_np(a.dtype), kind="ExternalInput").ap())
    for i, (shape, dtype) in enumerate(_OUTS):
        dt = _mybir.dt.from_np(_np.dtype(dtype))
        args.append(nc.dram_tensor(f"out_{i}_dram", shape, dt, kind="ExternalOutput").ap())
    hybrid_block(nc, *args)
    r = _run(nc, [arrays], core_ids=[0])
    return r.results[0]["out_0_dram"]
```

```python
import concourse.bass as bass
from concourse import mybir
from contextlib import ExitStack

F32 = mybir.dt.float32
F32R = mybir.dt.float32r
I32 = mybir.dt.int32
ACT = mybir.ActivationFunctionType
ALU = mybir.AluOpType
AXX = mybir.AxisListType.X

P = 128
SEQ, D = 256, 1024
NT = SEQ // P
KT = D // P
EPS = 1e-6
D_INNER, N_STATE, N_GROUPS, SSM_HEADS, HEAD = 2048, 128, 4, 32, 64
CONV_K = 4
ATT_HEADS, IDX_HEADS, TOPK = 16, 8, 64
X_HEADS = 4
EXPERTS, GROUPS, PER_GROUP, HID = 32, 4, 8, 512
CAP = 64
PAIRS = EXPERTS // 2
MAX_PASSES = SEQ // CAP
NEG = -1e30
TAKEN = -3e38
UNIT = 2048
RING = 5
HI_RING = 3
N_PRM = 13
MOE_SLOTS = 8

C_Z, C_XS, C_B, C_C = 0, 2048, 4096, 4608
C_DT, C_Q, C_K, C_V, C_QI, C_KI, C_WI, C_GS, C_GA = 5120, 5152, 6176, 6240, 6304, 6816, 6880, 6888, 7912
SM_V, SM_WI, SM_DT, TM_W = 0, 64, 72, 104


def hybrid_block(nc, x, mem, norm_mix, w_in, conv_w, conv_b, dt_bias, a_log, d_skip, ssm_norm,
                 w_ssm_out, w_att_out, w_mix_out, norm_x, norm_mem, w_xq, w_xkv, w_xo, norm_moe,
                 w_rg, b_rg, w_re, b_re, w_e_gate, w_e_up, w_e_down, norm_final, out):
    ctx = ExitStack()
    with ctx:
        def sb(name, shape, dt=F32):
            return ctx.enter_context(nc.sbuf_tensor(name, shape, dt))

        def sem(name):
            return ctx.enter_context(nc.semaphore(name))

        ctx.enter_context(nc.allow_non_contiguous_dma(reason="a few small parameter vectors"))

        KB = 1024
        sizes = (("raw", 40), ("hi", 24), ("zs", 16), ("gates", 16), ("xdt", 16), ("ys", 16), ("bc", 8), ("q", 8),
                 ("x", 8), ("u", 8), ("work", 18))
        base = (nc.sbuf_base + 63) // 64 * 64
        at, total = {}, 0
        for region, kb in sizes:
            at[region] = base + total
            total += kb * KB
        ctx.enter_context(nc.sbuf_tensor("arena", [P, (total + 64) // 4], F32))

        def place(name, shape, region, dt=F32, skip=0):
            return nc.alloc_sbuf_tensor_at(name, shape, dt, offset=at[region] + skip)

        raw_w = place("raw_w", [P, RING, UNIT], "raw")
        lo_w = place("lo_w", [P, RING, UNIT], "raw", F32R)
        hi_w = place("hi_w", [P, HI_RING, UNIT], "hi", F32R)
        zs = place("zs", [P, 16, SEQ], "zs")
        y_hi = place("y_hi", [P, 16, SEQ], "zs", F32R)
        gates = place("gates", [P, 16, SEQ], "gates")
        xdt = place("xdt", [P, NT, D_INNER], "xdt")
        ysT = place("ysT", [P, 16, SEQ], "ys")
        y_lo = place("y_lo", [P, 16, SEQ], "ys", F32R)
        bc = place("bc", [P, 8, SEQ], "bc")
        a_hi = place("a_hi", [P, 8, SEQ], "bc", F32R)
        qT = place("qT", [P, 8, SEQ], "q")
        a_lo = place("a_lo", [P, 8, SEQ], "q", F32R)
        xres = place("xres", [P, NT, D], "x")
        u_lo = place("u_lo", [P, KT, SEQ], "x", F32R)
        u_hi = place("u_hi", [P, KT, SEQ], "u", F32R)
        outb = place("outb", [P, NT, D], "ys")
        def two_halves(name, *places):
            return [place(f"{name}_{h}", [P, 2048], region, skip=kb * KB) for h, (region, kb) in enumerate(places)]

        moe_slot = [two_halves("gate_a", ("zs", 0), ("zs", 8)), two_halves("gate_b", ("gates", 0), ("gates", 8)),
                    two_halves("up_a", ("xdt", 0), ("xdt", 8)), two_halves("up_b", ("raw", 24), ("raw", 32)),
                    two_halves("down_a", ("raw", 0), ("raw", 8)), two_halves("down_b", ("hi", 16), ("raw", 16)),
                    two_halves("gate_c", ("bc", 0), ("q", 0)), two_halves("gate_d", ("x", 0), ("u", 0))]
        moe_buf = place("moe_buf", [P, 4096], "hi")
        cbm = sb("cbm", [P, N_GROUPS, 384])
        qiT = sb("qiT", [P, 4, SEQ])
        kz = sb("kz", [P, 2, SEQ])
        kiz = sb("kiz", [P, 2, SEQ])
        small_tm = sb("small_tm", [P, NT, TM_W])
        isc = sb("isc", [P, 384])
        selm = sb("selm", [P, 384])
        dist = sb("dist", [P, 384])
        caus = sb("caus", [P, 384])
        work = place("work", [P, 12, 384], "work")
        m_lo = place("m_lo", [P, KT, SEQ], "work", F32R, skip=6 * KB)
        ident = sb("ident", [P, P])
        tri = sb("tri", [P, P])
        ones = sb("ones", [P, P])
        iota64 = sb("iota64", [P, CAP])
        prm = sb("prm", [P, 448])
        wr = sb("wr", [P, KT, 36])
        st = sb("st", [P, 480])

        flat_xdt = xdt[:, :, :].rearrange("p a b -> p (a b)")
        flat_ys = ysT[:, :, :].rearrange("p a b -> p (a b)")
        flat_work = work[:, :, :].rearrange("p a b -> p (a b)")
        flat_qi = qiT[:, :, :].rearrange("p a b -> p (a b)")
        xn0 = flat_xdt[:, 0:2048].rearrange("p (i d) -> p i d", i=NT)
        memx = xn0
        memn = flat_xdt[:, 2048:4096].rearrange("p (i d) -> p i d", i=NT)
        kxT = flat_xdt[:, 0:2048].rearrange("p (k t) -> p k t", k=KT)
        vx = memn
        xn1 = flat_ys[:, 2048:4096].rearrange("p (i d) -> p i d", i=NT)
        qxT = flat_ys[:, 0:2048].rearrange("p (k t) -> p k t", k=KT)
        xn2 = xn1
        tT = qxT
        raw = flat_work[:, 0:3 * 260].rearrange("p (n w) -> p n w", n=3)
        cacc = flat_work[:, 780:780 + 512].rearrange("p (n w) -> p n w", n=2)
        rel = flat_work[:, 1536:1536 + 1536].rearrange("p (n w) -> p n w", n=2)
        prob = work[:, 0:4, :]
        probT = work[:, 4:6, :]
        albi = flat_qi[:, 0:768].rearrange("p (h w) -> p h w", h=2)
        seg = work[:, 0:4, :]
        mdec = work[:, 4:8, :]
        ysq = flat_work[:, 3072:3072 + 512].rearrange("p (n w) -> p n w", n=2)
        pX = flat_work[:, 0:2048].rearrange("p (n w) -> p n w", n=4)
        pXT = flat_work[:, 2048:3072].rearrange("p (n w) -> p n w", n=2)
        tr_tmp = flat_work[:, 3584:4608].rearrange("p (n w) -> p n w", n=2)
        mix_tmp = flat_work[:, 512:1024].rearrange("p (n w) -> p n w", n=2)
        rs_bc = flat_work[:, 0:256]

        cw = prm[:, 0:96].rearrange("p (k b) -> p k b", k=CONV_K)
        cbias = prm[:, 96:120]
        sgain = prm[:, 120:136]
        g_mix, g_mem, g_x, g_moe = (prm[:, 136 + 8 * i:144 + 8 * i] for i in range(4))
        dskip = prm[:, 168:184]
        dtb = prm[:, 184:216]
        alog = prm[:, 216:248]
        brt = prm[:, 248:284]
        rev4 = prm[:, 284:288]
        rev32 = prm[:, 288:320]
        dt = prm[:, 320:384].rearrange("p (i h) -> p i h", i=NT)
        dA = prm[:, 384:448].rearrange("p (i h) -> p i h", i=NT)
        flat_cb = cbm[:, :, :].rearrange("p a b -> p (a b)")
        cwrow = flat_cb[0:24, 0:512]
        prow = flat_cb[0:40, 768:896]
        sel2 = sb("sel2", [2, P])
        drow = sb("drow", [2, 16])
        n_it = sb("n_it", [P, 3], I32)
        pos_all = sb("pos_all", [P, NT, MAX_PASSES * EXPERTS + 2])
        comb_all = flat_cb[:, 0:NT * (MAX_PASSES * EXPERTS + 2)].rearrange("p (i n) -> p i n", i=NT)
        bias3 = pos_all[:, 0, 0:96].rearrange("p (k h) -> p k h", k=3)

        xg = moe_buf[:, 0:1024].rearrange("p (k j) -> p k j", k=KT)
        yj = moe_buf[:, 1024:2048]
        hs = moe_buf[:, 2048:2560]
        hh = moe_buf[:, 2560:3072]
        hT = moe_buf[:, 3072:3584].rearrange("p (k j) -> p k j", k=4)
        S = flat_work[:, 0:256].rearrange("p (i a j) -> p i a j", i=NT, a=2)
        Sw = flat_work[:, 256:512].rearrange("p (i a j) -> p i a j", i=NT, a=2)
        SwT = flat_work[:, 512:768].rearrange("p (i t) -> p i t", i=NT)
        gain_f = flat_work[:, 1024:2048]
        junk = moe_buf[:, 0:2048].rearrange("p (n w) -> p n w", n=4)
        rt = flat_work[:, 3072:4096]

        bank = [ctx.enter_context(nc.psum_tensor(f"bank{i}", [P, 512], F32)) for i in range(8)]
        acc_bank = [[bank[0], bank[1]], [bank[6], bank[7]]]

        landed = [sem(f"landed{s}") for s in range(RING)]
        moe_landed = [[sem(f"moe_landed{s}_{h}") for h in range(2)] for s in range(MOE_SLOTS)]
        hi_done = sem("hi_done")
        lo_done = sem("lo_done")
        lo_pool = sem("lo_pool")
        x_in = sem("x_in")
        gmix_in = sem("gmix_in")
        ident_ready = sem("ident_ready")
        tr_gain = sem("tr_gain")
        tr_hi = sem("tr_hi")
        mem_in = sem("mem_in")
        prm_in = sem("prm_in")
        gainf_in = sem("gainf_in")
        consts = sem("consts")
        pool_chain = sem("pool_chain")
        act_chain = sem("act_chain")
        dve_chain = sem("dve_chain")
        ssq_done = sem("ssq_done")
        ms_ready = sem("ms_ready")
        rstd_done = sem("rstd_done")
        xn_ready = sem("xn_ready")
        tr_ready = sem("tr_ready")
        tr_evac = sem("tr_evac")
        prm_tr = sem("prm_tr")
        prm_ready = sem("prm_ready")
        proj_ready = sem("proj_ready")
        evac_act = sem("evac_act")
        evac_dve = sem("evac_dve")
        dt_exp_in, dt_exp, dt_ready = sem("dt_exp_in"), sem("dt_exp"), sem("dt_ready")
        idx_ready, idx_relu, idx_used = sem("idx_ready"), sem("idx_relu"), sem("idx_used")
        conv_done, conv_silu = sem("conv_done"), sem("conv_silu")
        cb_ready, cb_done = sem("cb_ready"), sem("cb_done")
        acs_ready, acs_done = sem("acs_ready"), sem("acs_done")
        xt_ready, xdt_done = sem("xt_ready"), sem("xdt_done")
        mask_ready = sem("mask_ready")
        albi_ready, sc_ready, sc_used, mx_ready, exp_done, pn_ready = (
            sem(n) for n in ("albi_ready", "sc_ready", "sc_used", "mx_ready", "exp_done", "pn_ready"))
        rcp_ready = sem("rcp_ready")
        pn_odd = sem("pn_odd")
        pt_ready, pt_evac, pv_ready, pv_evac = (sem(n) for n in ("pt_ready", "pt_evac", "pv_ready", "pv_evac"))
        zsilu, gsig = sem("zsilu"), sem("gsig")
        r_ready, seg_ready, dec_ready, m_ready, y_ready, y_used = (
            sem(n) for n in ("r_ready", "seg_ready", "dec_ready", "m_ready", "y_ready", "y_used"))
        yg_ready, sq_ready, ssq_mm = sem("yg_ready"), sem("sq_ready"), sem("ssq_mm")
        y_hi_done, y_lo_done = sem("y_hi_done"), sem("y_lo_done")
        pv_lo, mix_ready, mix_hi, mix_lo, xo_lo = (
            sem(n) for n in ("pv_lo", "mix_ready", "mix_hi", "mix_lo", "xo_lo"))
        gn_ms, gn_rstd = sem("gn_ms"), sem("gn_rstd")
        xs_ready, xmx_ready, xexp_done, xpn_ready, xpt_ready, xpt_evac, xo_ready, xo_evac = (
            sem(n) for n in ("xs_ready", "xmx_ready", "xexp_done", "xpn_ready", "xpt_ready", "xpt_evac",
                             "xo_ready", "xo_evac"))
        rl_ready, rexp_in, rexp_done, rmask, rpos = (
            sem(n) for n in ("rl_ready", "rexp_in", "rexp_done", "rmask", "rpos"))
        route_ready = sem("route_ready")
        m_sel, m_gath, m_xg, m_silu, m_h, m_tr, m_ht, m_st, m_y0, m_y1, m_sw = (
            sem("moe_" + n) for n in ("sel", "gathered", "xg", "silu", "h", "transposed", "hT", "swT", "y_act", "y_dve", "sw"))
        gate_used, up_used, down_used = sem("gate_used"), sem("up_used"), sem("down_used")
        residual_in = sem("residual_in")
        moe_done, f_ssq, f_ms, f_rstd, f_out, stored = (
            sem(n) for n in ("moe_done", "f_ssq", "f_ms", "f_rstd", "f_out", "stored"))

        GATE, UP, DOWN = (0, 6), 2, 4

        steps = (["k", "ki", "tm0", "tm1"] + [f"qi{b}" for b in range(4)] + [f"bc{b}" for b in range(8)]
                 + [f"xs{b}" for b in range(16)] + [f"q{b}" for b in range(8)] + [f"z{b}" for b in range(16)]
                 + [f"g{b}" for b in range(16)] + [f"ao{b}" for b in range(8)] + [f"so{b}" for b in range(8)]
                 + [f"kx{b}" for b in range(8)] + [f"mo{c}{i}" for c in range(2) for i in range(NT)]
                 + [f"vx{c}{i}" for c in range(2) for i in range(NT)] + [f"qx{b}" for b in range(8)]
                 + [f"xo{c}{i}" for c in range(2) for i in range(NT)])
        STEP = {s: n for n, s in enumerate(steps)}
        by_dve = [s[:2] in ("ao", "so", "mo", "xo") for s in steps]

        def wait_evac(eng, name_or_n):
            n = STEP[name_or_n] if isinstance(name_or_n, str) else name_or_n
            if by_dve[n]:
                eng.wait_ge(evac_dve, sum(by_dve[:n + 1]))
            else:
                eng.wait_ge(evac_act, n + 1 - sum(by_dve[:n + 1]))

        def cols(w, c0, n):
            return w[0, :, c0:c0 + n].rearrange("(p t) n -> p t n", t=KT)

        def rows(w, half, c0):
            return w[0, 512 * half:512 * half + 512, c0:c0 + 512].rearrange("(t p) n -> p t n", p=P)

        units, LAST_STEP = [("kk", None, KT), ("tm", None, KT)], {"kk": "ki", "tm": "tm1"}
        for kind, w, c0, n in (("qi", w_in, C_QI, 2), ("bc", w_in, C_B, 4), ("xs", w_in, C_XS, 8), ("q", w_in, C_Q, 4),
                               ("z", w_in, C_Z, 8), ("g", w_in, C_GS, 8), ("ao", w_att_out, 0, 4),
                               ("so", w_ssm_out, 0, 8), ("kx", w_xkv, 0, 4), ("mo", w_mix_out, 0, 2),
                               ("vx", w_xkv, D, 2), ("qx", w_xq, 0, 4), ("xo", w_xo, 0, 2)):
            for j in range(n):
                if kind == "ao":
                    units.append((f"ao{j}", w[0, :, 256 * j:256 * j + 256].rearrange("(t p) n -> p t n", p=P), 8))
                elif kind == "so":
                    units.append((f"so{j}", w[0, :, P * j:P * j + P].rearrange("(t p) n -> p t n", p=P), 16))
                elif kind in ("vx", "mo", "xo"):
                    for half in range(2):
                        src = cols(w, c0 + 512 * j, 512)[:, 4 * half:4 * half + 4, :] if kind == "vx" \
                            else rows(w, half, 512 * j)
                        units.append((f"{kind}{j}{half}", src, 4))
                        LAST_STEP[f"{kind}{j}{half}"] = f"{kind}{j}{half}"
                else:
                    units.append((f"{kind}{j}", cols(w, c0 + 256 * j, 256), KT))
                if kind == "so":
                    LAST_STEP[f"so{j}"] = f"so{j}"
                elif kind not in ("vx", "mo", "xo"):
                    LAST_STEP[f"{kind}{j}"] = f"{kind}{2 * j + 1}"
        UN = {u[0]: n for n, u in enumerate(units)}
        PIECES = [[(0, C_K, HEAD), (HEAD, C_K, HEAD), (2 * HEAD, C_KI, HEAD), (3 * HEAD, C_KI, HEAD)],
                  [(SM_V, C_V, HEAD), (SM_WI, C_WI, IDX_HEADS), (SM_DT, C_DT, SSM_HEADS)]]

        def unit_len(n):
            return KT * TM_W if n == UN["tm"] else UNIT

        def parts(name):
            n = UN[name]
            return [w[:, 0:unit_len(n)].rearrange("p (t n) -> p t n", t=units[n][2])
                    for w in (hi_w[:, n % HI_RING, :], lo_w[:, n % RING, :])]

        FIRST_STEP = {f"{k}{2 * j}": f"{k}{j}" for k in ("qi", "bc", "xs", "q", "z", "g", "ao", "kx", "qx")
                      for j in range(8) if f"{k}{j}" in UN}
        FIRST_STEP.update({"k": "kk", "tm0": "tm"})
        FIRST_STEP.update({f"so{j}": f"so{j}" for j in range(8)})
        FIRST_STEP.update({f"{k}{j}{h}": f"{k}{j}{h}" for k in ("vx", "mo", "xo") for j in range(2) for h in range(2)})

        def landed_value(n):
            return 16 * (n // RING + 1) + (16 * (len(PIECES[n % RING]) - 1) if n % RING < len(PIECES) else 0)

        LOW_ON_POOL = [UN[name] for name in ("kk", "bc1", "bc3", "xs1", "xs2", "xs4", "xs5", "xs6", "xs7", "q1", "q3")]

        def wait_low(eng, n):
            if n in LOW_ON_POOL:
                eng.wait_ge(lo_pool, LOW_ON_POOL.index(n) + 1)
            else:
                eng.wait_ge(lo_done, sum(m not in LOW_ON_POOL for m in range(n + 1)))

        def wait_used(eng, n):
            eng.wait_ge(proj_ready, STEP[LAST_STEP[units[n][0]]] + 1)

        block = ctx.enter_context(nc.Block())

        @block.sync
        def _(sp):
            def load_half(s, e, w, h):
                t = HID * D // P // w.shape[3]
                src = w[0:1, bass.ds(e, 1), :, :].rearrange("o e (p t) n -> p (o e t) n", p=P)
                sp.dma_start(moe_slot[s][h][:, :].rearrange("p (t n) -> p t n", t=t // 2),
                             src[:, t // 2 * h:t // 2 * h + t // 2, :])\
                    .then_inc(moe_landed[s][h], 16)

            def load_expert(s, e, w):
                for h in range(2):
                    load_half(s, e, w, h)

            small_dmas = [(prow[0:24, :], conv_b[0, :].rearrange("(b p) -> b p", p=P)),
                          (prow[24:40, :], ssm_norm[0, :].rearrange("(b p) -> b p", p=P)),
                          (cwrow, conv_w[0, :, :].rearrange("(b q) k -> b (q k)", q=P)),
                          (drow[:, :], d_skip[0, :].rearrange("(b a) -> a b", a=2)),
                          (dtb, dt_bias[0:1, :].to_broadcast([P, SSM_HEADS])),
                          (alog, a_log[0:1, :].to_broadcast([P, SSM_HEADS])),
                          (g_mem, norm_mem[0, :].rearrange("(p t) -> p t", t=KT)),
                          (g_x, norm_x[0, :].rearrange("(p t) -> p t", t=KT)),
                          (g_moe, norm_moe[0, :].rearrange("(p t) -> p t", t=KT)),
                          (brt[:, 0:4], b_rg[0:1, :].to_broadcast([P, GROUPS])),
                          (brt[:, 4:36], b_re[0:1, :].to_broadcast([P, EXPERTS])),
                          (wr[:, :, 0:4], w_rg[0, :, :].rearrange("(p t) n -> p t n", t=KT)),
                          (wr[:, :, 4:36], w_re[0, :, :].rearrange("(p t) n -> p t n", t=KT))]
            assert len(small_dmas) == N_PRM

            for i in range(NT):
                sp.dma_start(xres[:, i, :], x[0, P * i:P * i + P, :]).then_inc(x_in, 16)
            sp.dma_start(g_mix, norm_mix[0, :].rearrange("(p t) -> p t", t=KT)).then_inc(gmix_in, 16)
            for n, (name, src, k) in enumerate(units):
                if n >= RING:
                    wait_used(sp, n - RING)
                dst = raw_w[:, n % RING, 0:unit_len(n)].rearrange("p (t n) -> p t n", t=k)
                if n < len(PIECES):
                    for d0, s0, w in PIECES[n]:
                        sp.dma_start(dst[:, :, d0:d0 + w], cols(w_in, s0, w)).then_inc(landed[n], 16)
                else:
                    sp.dma_start(dst, src).then_inc(landed[n % RING], 16)
                if n == 2:
                    for dst, src in small_dmas:
                        sp.dma_start(dst, src).then_inc(prm_in, 16)
                if name == "ao3":
                    sp.wait_ge(y_ready, 16)
                    for i in range(NT):
                        sp.dma_start(memx[:, i, :], mem[0, P * i:P * i + P, :]).then_inc(mem_in, 16)
                if name == "so4":
                    sp.wait_ge(proj_ready, STEP["g15"] + 1)
                    for i in range(NT):
                        sp.dma_start(xres[:, i, :], x[0, P * i:P * i + P, :]).then_inc(x_in, 16)
                if name == "qx2":
                    load_expert(GATE[0], 0, w_e_gate)
                    load_expert(GATE[0] + 1, 1, w_e_gate)

            def load_two(kind, pair, w, used, turns):
                for h in range(2):
                    sp.wait_ge(used, 2 * turns - 1 + h)
                    for a in range(2):
                        load_half(kind + a, 2 * pair + a, w, h)

            def gate_of(n, odd, turns):
                load_two(GATE[odd], n, w_e_gate, gate_used, turns)

            def up_down_of(n, turns):
                load_two(UP, n, w_e_up, up_used, turns)
                load_two(DOWN, n, w_e_down, down_used, turns)

            def rest_of_pass(first):
                with sp.Fori(0, PAIRS // 2 - 2) as j:
                    for o in (1, 2):
                        n = 2 * j + o
                        gate_of(n + 1, (o + 1) % 2, first + n)
                        up_down_of(n, first + n)
                n = PAIRS - 3
                gate_of(n + 1, 0, first + n)
                up_down_of(n, first + n)
                up_down_of(n + 1, first + n + 1)
                gate_of(n + 2, 1, first + n + 1)
                up_down_of(n + 2, first + n + 2)

            def load_over_ring(s, h, e, w, raw_slot=None, hi_slot=None):
                wait_used(sp, max(n for n in range(len(units)) if raw_slot == n % RING or hi_slot == n % HI_RING))
                load_half(s, e, w, h)

            load_over_ring(UP + 1, 0, 1, w_e_up, raw_slot=3)
            sp.wait_ge(xo_ready, 2 * X_HEADS)
            load_expert(UP, 0, w_e_up)
            load_over_ring(UP + 1, 1, 1, w_e_up, raw_slot=4)
            load_over_ring(DOWN, 0, 0, w_e_down, raw_slot=0)
            load_over_ring(DOWN + 1, 0, 1, w_e_down, hi_slot=2)
            load_over_ring(DOWN, 1, 0, w_e_down, raw_slot=1)
            load_over_ring(DOWN + 1, 1, 1, w_e_down, raw_slot=2)
            load_expert(GATE[1], 2, w_e_gate)
            sp.wait_ge(residual_in, 1)
            load_expert(GATE[1] + 1, 3, w_e_gate)
            rest_of_pass(0)
            sp.wait_ge(route_ready, 1)
            n_pass = sp.value_load(n_it[0:1, 1:2], min_val=1, max_val=MAX_PASSES)
            with sp.If(n_pass > 1):
                with sp.Fori(1, n_pass) as r:
                    load_two(GATE[0], 0, w_e_gate, gate_used, r * PAIRS - 1)
                    load_two(GATE[1], 1, w_e_gate, gate_used, r * PAIRS)
                    load_two(UP, 0, w_e_up, up_used, r * PAIRS)
                    load_two(DOWN, 0, w_e_down, down_used, r * PAIRS)
                    rest_of_pass(r * PAIRS)
            for i in range(NT):
                sp.wait_ge(f_out, i + 1)
                sp.dma_start(out[0, P * i:P * i + P, :], outb[:, i, :]).then_inc(stored, 16)
            sp.wait_ge(stored, 16 * NT)

        @block.gpsimd
        def _(pool):
            chain = [0]

            def link(ins):
                chain[0] += 1
                ins.then_inc(pool_chain, 1)
                pool.wait_ge(pool_chain, chain[0])

            link(nc.gpsimd.memset(ident[:, :], 0.0))
            link(nc.gpsimd.affine_select(out=ident[:, :], in_=ident[:, :], compare_op=ALU.not_equal, fill=1.0,
                                         base=0, pattern=[[-1, P]], channel_multiplier=1))
            nc.gpsimd.memset(st[:, 470:474], 0.0).then_inc(ident_ready, 1)
            link(nc.gpsimd.memset(ones[:, :], 1.0))
            link(nc.gpsimd.affine_select(out=tri[:, :], in_=ones[:, :], compare_op=ALU.is_ge, fill=0.0,
                                         base=0, pattern=[[1, P]], channel_multiplier=-1))
            link(nc.gpsimd.affine_select(out=sel2[:, :], in_=ones[0:2, :], compare_op=ALU.is_ge, fill=0.0,
                                         base=0, pattern=[[1, P]], channel_multiplier=-64))
            link(nc.gpsimd.affine_select(out=sel2[:, :], in_=sel2[:, :], compare_op=ALU.is_ge, fill=0.0,
                                         base=63, pattern=[[-1, P]], channel_multiplier=64))
            for d in (kz, kiz):
                link(nc.gpsimd.memset(d[0:64, 1, :], 0.0))
                link(nc.gpsimd.memset(d[64:128, 0, :], 0.0))
            for n in range(3):
                last = nc.gpsimd.memset(raw[:, n, 0:3], 0.0)
            last.then_inc(consts, 1)
            link(nc.gpsimd.iota(dist[:, 0:128], pattern=[[-1, 128]], base=0, channel_multiplier=1,
                                allow_small_or_imprecise_dtypes=True))
            link(nc.gpsimd.iota(dist[:, 128:384], pattern=[[-1, 256]], base=128, channel_multiplier=1,
                                allow_small_or_imprecise_dtypes=True))
            link(nc.gpsimd.iota(iota64[:, :], pattern=[[1, CAP]], base=0, channel_multiplier=0,
                                allow_small_or_imprecise_dtypes=True))
            link(nc.gpsimd.iota(rev4, pattern=[[-1, GROUPS]], base=GROUPS, channel_multiplier=0,
                                allow_small_or_imprecise_dtypes=True))
            link(nc.gpsimd.iota(rev32, pattern=[[-1, EXPERTS]], base=EXPERTS, channel_multiplier=0,
                                allow_small_or_imprecise_dtypes=True))
            link(nc.gpsimd.memset(caus[:, :], 0.0))
            nc.gpsimd.affine_select(out=caus[:, 0:128], in_=caus[:, 0:128], compare_op=ALU.is_ge, fill=NEG,
                                    base=0, pattern=[[-1, 128]], channel_multiplier=1)
            nc.gpsimd.affine_select(out=caus[:, 128:384], in_=caus[:, 128:384], compare_op=ALU.is_ge, fill=NEG,
                                    base=128, pattern=[[-1, 256]], channel_multiplier=1).then_inc(consts, 1)

            def albi_tile(h):
                if h >= 2:
                    pool.wait_ge(sc_used, h - 1)
                slope = 2.0 ** (-8.0 * (h + 1) / ATT_HEADS)
                link(nc.gpsimd.tensor_scalar(albi[:, h % 2, :], dist[:, :], -slope, None, ALU.mult))
                nc.gpsimd.tensor_tensor(albi[:, h % 2, :], albi[:, h % 2, :], selm[:, :], ALU.add)\
                    .then_inc(albi_ready, 1)

            def normalise(h):
                pool.wait_ge(rcp_ready, h // 2 + 1)
                pb = prob[:, 2 * (h // 2 % 2) + h % 2, :]
                for i, (a, b) in enumerate(((0, 128), (128, 384))):
                    k = 96 + 4 * (h // 2 % 2) + 2 * (h % 2) + i
                    last = nc.gpsimd.tensor_scalar(pb[:, a:b], pb[:, a:b], st[:, k:k + 1], None, ALU.mult)
                last.then_inc(pn_ready, 1)

            pool.wait_ge(consts, 2)
            for m in LOW_ON_POOL:
                pool.wait_ge(hi_done, m + 1)
                nc.gpsimd.tensor_tensor(lo_w[:, m % RING, :], raw_w[:, m % RING, :],
                                        hi_w[:, m % HI_RING, :].bitcast(F32), ALU.subtract).then_inc(lo_pool, 1)
            pool.wait_ge(mask_ready, 1)
            pool.wait_ge(idx_ready, 4)
            albi_tile(0)
            albi_tile(1)
            for b in range(ATT_HEADS // 2):
                if b + 1 < ATT_HEADS // 2:
                    albi_tile(2 * b + 2)
                    albi_tile(2 * b + 3)
                normalise(2 * b)

            def gate_y(b):
                pool.wait_ge(y_used, b + 1)
                if b == 0:
                    pool.wait_ge(zsilu, 1)
                nc.gpsimd.tensor_tensor(ysT[:, b, :], ysT[:, b, :], zs[:, b, :], ALU.mult).then_inc(yg_ready, 1)

            pool.wait_ge(cb_done, N_GROUPS)
            pool.wait_ge(prm_ready, 2)
            for b in range(SSM_HEADS // 2):
                for a in range(2):
                    h = 2 * b + a
                    pool.wait_ge(dec_ready, h + 1)
                    if b == 1:
                        pool.wait_ge(pv_ready, 8)
                    if b >= 2:
                        pool.wait_ge(y_ready, b - 1)
                    nc.gpsimd.tensor_tensor(mdec[:, 2 * ((b + 1) % 2) + a, :], seg[:, 2 * (b % 2) + a, :],
                                            cbm[:, h // 8, :], ALU.mult).then_inc(m_ready, 1)
                if b >= 1:
                    gate_y(b - 1)
            gate_y(SSM_HEADS // 2 - 1)

        @block.scalar
        def _(act):
            chain = [0]

            def link(ins):
                chain[0] += 1
                ins.then_inc(act_chain, 1)
                act.wait_ge(act_chain, chain[0])

            split = [0]

            def split_hi_through(n):
                while split[0] <= min(n, len(units) - 1):
                    m = split[0]
                    act.wait_ge(landed[m % RING], landed_value(m))
                    if m >= HI_RING:
                        wait_used(act, m - HI_RING)
                    w = unit_len(m)
                    nc.scalar.activation(hi_w[:, m % HI_RING, 0:w], raw_w[:, m % RING, 0:w], ACT.Copy)\
                        .then_inc(hi_done, 1)
                    split[0] += 1

            group = [0]

            def transposed_hi(dst):
                for i in range(NT):
                    for q in range(2):
                        g = group[0]
                        act.wait_ge(tr_gain, g + 1)
                        nc.scalar.activation(dst[:, 4 * q:4 * q + 4, P * i:P * i + P],
                                             tr_tmp[:, g % 2, :].rearrange("p (k t) -> p k t", k=4), ACT.Copy)\
                            .then_inc(tr_hi, 1)
                        group[0] += 1

            def norm_stats(n, src, junk_to, between=None):
                for i in range(NT):
                    last = nc.scalar.activation(junk_to[:, i, :], src[:, i, :], ACT.Square,
                                                accum_out=st[:, 4 * n + i:4 * n + i + 1])
                last.then_inc(ssq_done, 1)
                if between is not None:
                    split_hi_through(between)
                act.wait_ge(ms_ready, n + 1)
                nc.scalar.activation(st[:, 4 * n + 2:4 * n + 4], st[:, 4 * n + 2:4 * n + 4], ACT.Sqrt)\
                    .then_inc(rstd_done, 1)

            def warm_sqrt():
                nc.scalar.activation(st[:, 474:475], st[:, 470:471], ACT.Sqrt)

            def norm_stats_by_tile(prefix, n, junk_to):
                warm_sqrt()
                for c in range(2):
                    for i in range(NT):
                        wait_evac(act, f"{prefix}{c}{i}")
                        k = 140 + 4 * (n - 2) + 2 * i + c
                        last = nc.scalar.activation(junk_to[:, i, 512 * c:512 * c + 512],
                                                    xres[:, i, 512 * c:512 * c + 512], ACT.Square,
                                                    accum_out=st[:, k:k + 1])
                        if c == 1:
                            last.then_inc(ssq_done, 1)
                        split_hi_through(UN[f"{prefix}00"] + 3 + 2 * c + i)
                        if c == 1:
                            act.wait_ge(ms_ready, 2 * n - 1 + i)
                            r = st[:, 4 * n + 2 + i:4 * n + 3 + i]
                            nc.scalar.activation(r, r, ACT.Sqrt).then_inc(rstd_done, 1)

            def evac(name, dst, scale=1.0, src=None):
                n = STEP[name]
                if name in FIRST_STEP:
                    split_hi_through(UN[FIRST_STEP[name]] + 2)
                act.wait_ge(proj_ready, n + 1)
                src = bank[n % 2][:, 0:SEQ] if src is None else src
                nc.scalar.activation(dst, src, ACT.Copy, scale=scale).then_inc(evac_act, 1)

            act.wait_ge(ident_ready, 1)
            warm_sqrt()
            act.wait_ge(x_in, 32)
            norm_stats(0, xres, xn0)
            split_hi_through(0)
            transposed_hi(u_hi)
            split_hi_through(2)
            act.wait_ge(consts, 1)

            for name, d in (("k", kz), ("ki", kiz)):
                n = STEP[name]
                act.wait_ge(proj_ready, n + 1)
                nc.scalar.activation(d[0:64, 0, :], bank[n % 2][0:64, 0:SEQ], ACT.Copy)
                nc.scalar.activation(d[64:128, 1, :], bank[n % 2][64:128, 0:SEQ], ACT.Copy).then_inc(evac_act, 1)
            for i in range(NT):
                n = STEP[f"tm{i}"]
                evac(f"tm{i}", small_tm[:, i, :], src=bank[n % 2][:, 0:TM_W])
            act.wait_ge(prm_in, 16 * N_PRM)
            nc.scalar.activation(alog, alog, ACT.Exp)
            act.wait_ge(dt_exp_in, 1)
            nc.scalar.activation(st[:, 160:224], st[:, 160:224], ACT.Exp).then_inc(dt_exp, 1)

            def relu(b):
                act.wait_ge(idx_ready, b + 1)
                if b >= 2:
                    act.wait_ge(idx_used, b - 1)
                nc.scalar.activation(rel[:, b % 2, 0:256], bank[4][:, 0:256], ACT.Relu)
                nc.scalar.activation(rel[:, b % 2, 256:768], bank[5][:, :], ACT.Relu).then_inc(idx_relu, 1)

            for b in range(4):
                evac(f"qi{b}", qiT[:, b, :])
                if b >= 1:
                    relu(b - 1)
            relu(3)

            xbc = [f"bc{b}" for b in range(8)] + [f"xs{b}" for b in range(16)]

            def conv_out(n):
                act.wait_ge(conv_done, n + 1)
                dst = bc[:, n, :] if n < 8 else ysT[:, n - 8, :]
                nc.scalar.activation(dst, cacc[:, n % 2, :], ACT.Silu).then_inc(conv_silu, 1)

            for n, name in enumerate(xbc):
                if n >= 3:
                    act.wait_ge(conv_done, n - 2)
                evac(name, raw[:, n % 3, 3:259])
                if n >= 1:
                    conv_out(n - 1)

            for b in range(8):
                evac(f"q{b}", qT[:, b, :], scale=HEAD ** -0.5)
                if b == 1:
                    conv_out(23)

            def exps(b):
                act.wait_ge(mx_ready, b + 1)
                if b >= 2:
                    act.wait_ge(pt_ready, 2 * (b - 1))
                for a in range(2):
                    for i, (lo, hi) in enumerate(((0, 128), (128, 384))):
                        k = 2 * a + i
                        pb = prob[:, 2 * (b % 2) + a, lo:hi]
                        last = nc.scalar.activation(pb, pb, ACT.Exp, bias=st[:, 72 + 4 * (b % 2) + k:73 + 4 * (b % 2) + k],
                                                    accum_out=st[:, 80 + 4 * (b % 2) + k:81 + 4 * (b % 2) + k])
                last.then_inc(exp_done, 1)

            def values_hi(b):
                act.wait_ge(pv_ready, b + 1)
                nc.scalar.activation(a_hi[:, b, :], bank[6 + b % 2][:, 0:SEQ], ACT.Copy).then_inc(pv_evac, 1)

            def normalise_odd(b):
                act.wait_ge(rcp_ready, b + 1)
                pb = prob[:, 2 * (b % 2) + 1, :]
                for i, (lo, hi) in enumerate(((0, 128), (128, 384))):
                    k = 98 + 4 * (b % 2) + i
                    last = nc.scalar.activation(pb[:, lo:hi], pb[:, lo:hi], ACT.Copy, scale=st[:, k:k + 1])
                last.then_inc(pn_odd, 1)

            exps(0)
            for b in range(8):
                evac(f"z{2 * b}", zs[:, 2 * b, :])
                if b + 1 < 8:
                    exps(b + 1)
                if b >= 1:
                    values_hi(b - 1)
                normalise_odd(b)
                evac(f"z{2 * b + 1}", zs[:, 2 * b + 1, :])

            def square_y(b):
                act.wait_ge(yg_ready, b + 1)
                if b >= 2:
                    act.wait_ge(ssq_mm, b - 1)
                nc.scalar.activation(ysq[:, b % 2, :], ysT[:, b, :], ACT.Square).then_inc(sq_ready, 1)

            def gated_hi(b):
                act.wait_ge(yg_ready, b + 1)
                nc.scalar.activation(y_hi[:, b, :], ysT[:, b, :], ACT.Copy, scale=sgain[:, b:b + 1])\
                    .then_inc(y_hi_done, 1)

            def decays(b):
                for h in (2 * b, 2 * b + 1):
                    act.wait_ge(seg_ready, h + 1)
                    sg = seg[:, h % 4, :]
                    nc.scalar.activation(sg, sg, ACT.Exp).then_inc(dec_ready, 1)

            decays(0)
            split_hi_through(UN["g0"] + 2)
            values_hi(7)
            decays(1)
            evac("g0", gates[:, 0, :])
            wait_evac(act, "z15")
            nc.scalar.activation(zs[:, :, :], zs[:, :, :], ACT.Silu).then_inc(zsilu, 1)
            evac("g1", gates[:, 1, :])
            for b in range(2, 16):
                decays(b)
                evac(f"g{b}", gates[:, b, :])
                square_y(b - 2)
                if b >= 3:
                    gated_hi(b - 3)
            split_hi_through(UN["ao0"] + 2)
            square_y(14)
            gated_hi(13)
            square_y(15)
            wait_evac(act, "g15")
            nc.scalar.activation(gates[:, 8:16, :], gates[:, 8:16, :], ACT.Sigmoid).then_inc(gsig, 1)
            gated_hi(14)
            gated_hi(15)
            nc.scalar.activation(gates[:, 0:8, :], gates[:, 0:8, :], ACT.Sigmoid).then_inc(gsig, 1)
            split_hi_through(UN["ao1"] + 2)
            act.wait_ge(mem_in, 32)
            norm_stats(1, memx, memn, between=UN["ao2"] + 2)
            act.wait_ge(gn_ms, 1)
            nc.scalar.activation(rs_bc, rs_bc, ACT.Sqrt).then_inc(gn_rstd, 1)
            split_hi_through(UN["ao3"] + 2)
            transposed_hi(u_hi)
            for b in range(8):
                split_hi_through(UN[f"so{b}"] + 2)
                if b >= 1:
                    act.wait_ge(mix_ready, b)
                    nc.scalar.activation(a_hi[:, b - 1, :], mix_tmp[:, (b - 1) % 2, :], ACT.Copy).then_inc(mix_hi, 1)
            act.wait_ge(mix_ready, 8)
            nc.scalar.activation(a_hi[:, 7, :], mix_tmp[:, 1, :], ACT.Copy).then_inc(mix_hi, 1)
            for b in range(8):
                evac(f"kx{b}", kxT[:, b, :])
            split_hi_through(UN["mo00"] + 2)

            norm_stats_by_tile("mo", 2, xn1)

            def mem_values(c):
                for i in range(NT):
                    n = STEP[f"vx{c}{i}"]
                    evac(f"vx{c}{i}", vx[:, i, 512 * c:512 * c + 512], src=bank[n % 2][:, :])

            mem_values(0)
            transposed_hi(a_hi)
            mem_values(1)
            for b in range(8):
                evac(f"qx{b}", qxT[:, b, :], scale=(D // X_HEADS) ** -0.5)
            for h in range(X_HEADS):
                for i in range(NT):
                    n = NT * h + i
                    act.wait_ge(xmx_ready, n + 1)
                    if h >= 2:
                        act.wait_ge(xpt_ready, h - 1)
                    nc.scalar.activation(pX[:, 2 * (h % 2) + i, 0:256], bank[4 + i][:, 0:256], ACT.Exp,
                                         bias=st[:, 104 + n:105 + n],
                                         accum_out=st[:, 112 + n:113 + n]).then_inc(xexp_done, 1)
                if h >= 1:
                    for c in range(2):
                        act.wait_ge(xo_ready, 2 * (h - 1) + c + 1)
                        nc.scalar.activation(a_hi[:, 2 * (h - 1) + c, :], bank[6 + c][:, 0:SEQ], ACT.Copy)\
                            .then_inc(xo_evac, 1)
            for c in range(2):
                act.wait_ge(xo_ready, 2 * (X_HEADS - 1) + c + 1)
                nc.scalar.activation(a_hi[:, 2 * (X_HEADS - 1) + c, :], bank[6 + c][:, 0:SEQ], ACT.Copy)\
                    .then_inc(xo_evac, 1)
            split_hi_through(UN["xo00"] + 2)
            norm_stats_by_tile("xo", 3, xn2)
            act.wait_ge(rexp_in, 1)
            nc.scalar.activation(rt[:, 80:88], rt[:, 80:88], ACT.Exp).then_inc(rexp_done, 1)
            act.wait_ge(rexp_in, 2)
            nc.scalar.activation(rt[:, 96:98], rt[:, 96:98], ACT.Exp).then_inc(rexp_done, 1)
            act.wait_ge(xpt_ready, X_HEADS)
            act.dma_start(gain_f, norm_final.rearrange("(o d) -> o d", o=1).to_broadcast([P, D]))\
                .then_inc(gainf_in, 16)

            act.wait_ge(route_ready, 1)
            n_iter = act.value_load(n_it[0:1, 0:1], min_val=PAIRS, max_val=PAIRS * MAX_PASSES)
            with act.Fori(0, n_iter) as i:
                act.wait_ge(up_used, 2 * i + 2)
                nc.scalar.activation(hs, bank[4][:, :], ACT.Silu).then_inc(m_silu, 1)
                act.wait_ge(down_used, 2 * i + 2)
                nc.scalar.activation(yj[:, 0:512], bank[2][:, :], ACT.Copy).then_inc(m_y0, 1)
            warm_sqrt()
            for i in range(NT):
                act.wait_ge(moe_done, i + 1)
                for c in range(2):
                    last = nc.scalar.activation(junk[:, 2 * i + c, :], acc_bank[i][c][:, :], ACT.Square,
                                                accum_out=st[:, 128 + 2 * i + c:129 + 2 * i + c])
                last.then_inc(f_ssq, 1)
            for i in range(NT):
                act.wait_ge(f_ms, i + 1)
                nc.scalar.activation(st[:, 136 + i:137 + i], st[:, 136 + i:137 + i], ACT.Sqrt).then_inc(f_rstd, 1)

        @block.vector
        def _(dve):
            chain = [0]

            def link(ins):
                chain[0] += 1
                ins.then_inc(dve_chain, 1)
                dve.wait_ge(dve_chain, chain[0])

            tt, ts_, stt = nc.vector.tensor_tensor, nc.vector.tensor_scalar, nc.vector.scalar_tensor_tensor
            group, split, split_groups = [0], [0], [0]

            def split_lo_through(n):
                while split[0] <= min(n, len(units) - 1):
                    m = split[0]
                    split[0] += 1
                    if m in LOW_ON_POOL:
                        continue
                    w = unit_len(m)
                    dve.wait_ge(hi_done, m + 1)
                    tt(lo_w[:, m % RING, 0:w], raw_w[:, m % RING, 0:w], hi_w[:, m % HI_RING, 0:w].bitcast(F32),
                       ALU.subtract).then_inc(lo_done, 1)

            def inverse_mean(dst, half0, half1):
                link(ts_(dst, half0, half1, 1.0 / D, ALU.add, ALU.mult))
                link(ts_(dst, dst, EPS, None, ALU.add))
                return nc.vector.reciprocal(dst, dst)

            def norm_rows(n, src, dst):
                dve.wait_ge(ssq_done, n + 1)
                c = 4 * n
                link(ts_(st[:, c + 2:c + 4], st[:, c:c + 2], 1.0 / D, EPS, ALU.mult, ALU.add))
                nc.vector.reciprocal(st[:, c + 2:c + 4], st[:, c + 2:c + 4]).then_inc(ms_ready, 1)
                dve.wait_ge(rstd_done, n + 1)
                for i in range(NT):
                    ts_(dst[:, i, :], src[:, i, :], st[:, c + 2 + i:c + 3 + i], None, ALU.mult).then_inc(xn_ready, 1)

            def columns_of(i, gain, hiT, loT, tiles=1):
                def low(i, q, g):
                    dve.wait_ge(tr_hi, g + 1)
                    blk = (slice(None), slice(4 * q, 4 * q + 4), slice(P * i, P * i + P))
                    tt(loT[blk], tr_tmp[:, g % 2, :].rearrange("p (k t) -> p k t", k=4), hiT[blk].bitcast(F32),
                       ALU.subtract).then_inc(tr_evac, 1)

                before = None
                for ii in range(i, i + tiles):
                    for q in range(2):
                        g = group[0]
                        dve.wait_ge(tr_ready, g + 1)
                        if g >= 2:
                            dve.wait_ge(tr_evac, g - 1)
                        ps = bank[2 + g % 2][:, :].rearrange("p (k t) -> p k t", k=4)
                        gb = gain[:, 4 * q:4 * q + 4].unsqueeze(2).to_broadcast([P, 4, P])
                        tt(tr_tmp[:, g % 2, :].rearrange("p (k t) -> p k t", k=4), ps, gb, ALU.mult)\
                            .then_inc(tr_gain, 1)
                        if before is not None:
                            low(*before)
                        before = (ii, q, g)
                        group[0] += 1
                low(*before)

            def columns_f32(i, gain, dstT):
                for q in range(2):
                    g = group[0]
                    dve.wait_ge(tr_ready, g + 1)
                    tt(dstT[:, 4 * q:4 * q + 4, P * i:P * i + P],
                       bank[2 + g % 2][:, :].rearrange("p (k t) -> p k t", k=4),
                       gain[:, 4 * q:4 * q + 4].unsqueeze(2).to_broadcast([P, 4, P]), ALU.mult).then_inc(tr_evac, 1)
                    group[0] += 1

            dve.wait_ge(gmix_in, 16)
            norm_rows(0, xres, xn0)
            columns_of(0, g_mix, u_hi, u_lo, NT)
            split_lo_through(2)
            dve.wait_ge(consts, 1)
            dve.wait_ge(prm_in, 16 * N_PRM)

            dve.wait_ge(prm_tr, 1)
            nc.vector.tensor_copy(prm[:, 0:136], bank[4][:, 0:136]).then_inc(prm_ready, 1)
            nc.vector.tensor_copy(dskip, bank[5][:, 0:16]).then_inc(prm_ready, 1)

            wait_evac(dve, "tm1")
            r = st[:, 224:288].rearrange("p (i h) -> p i h", i=NT)
            e1 = st[:, 160:224].rearrange("p (i h) -> p i h", i=NT)
            e2 = st[:, 288:352].rearrange("p (i h) -> p i h", i=NT)
            z2 = st[:, 352:416].rearrange("p (i h) -> p i h", i=NT)
            hb = dtb.unsqueeze(1).to_broadcast([P, NT, SSM_HEADS])
            link(tt(r, small_tm[:, :, SM_DT - SM_V:SM_DT - SM_V + SSM_HEADS], hb, ALU.add))
            link(ts_(dt, r, 0.0, None, ALU.max))
            stt(e1, dt, -2.0, r, ALU.mult, ALU.add).then_inc(dt_exp_in, 1)
            dve.wait_ge(dt_exp_in, 1)
            dve.wait_ge(dt_exp, 1)
            link(ts_(e2, e1, 2.0, None, ALU.add))
            link(nc.vector.reciprocal(e2, e2))
            link(tt(e1, e1, e2, ALU.mult))
            link(tt(z2, e1, e1, ALU.mult))
            link(ts_(e2, z2, 1.0 / 19, None, ALU.mult))
            for k in (17, 15, 13, 11, 9, 7, 5, 3):
                link(stt(e2, e2, 1.0 / k, z2, ALU.add, ALU.mult))
            link(stt(e2, e2, 1.0, e1, ALU.add, ALU.mult))
            link(stt(dt, e2, 2.0, dt, ALU.mult, ALU.add))
            stt(dA, dt, -1.0, alog.unsqueeze(1).to_broadcast([P, NT, SSM_HEADS]), ALU.mult, ALU.mult)\
                .then_inc(dt_ready, 1)
            link(ts_(small_tm[:, :, SM_WI - SM_V:SM_WI - SM_V + 8], small_tm[:, :, SM_WI - SM_V:SM_WI - SM_V + 8],
                     IDX_HEADS ** -0.5 * HEAD ** -0.5, None, ALU.mult))

            for b in range(4):
                split_lo_through(UN["qi0"] + 2 + b // 2)
                dve.wait_ge(idx_relu, b + 1)
                for a in range(2):
                    h = 2 * b + a
                    for i, (lo, hi) in enumerate(((0, 128), (128, 384))):
                        w = hi - lo
                        src = rel[:, b % 2, 128 * a:128 * a + 128] if i == 0 else \
                            rel[:, b % 2, 256 + 256 * a:512 + 256 * a]
                        wi = small_tm[:, i, SM_WI - SM_V + h:SM_WI - SM_V + h + 1]
                        if h == 0:
                            link(ts_(isc[:, lo:hi], src, wi, None, ALU.mult))
                        else:
                            link(stt(isc[:, lo:hi], src, wi, isc[:, lo:hi], ALU.mult, ALU.add))
                nc.vector.tensor_copy(st[:, 472:473], st[:, 473:474]).then_inc(idx_used, 1)
            dve.wait_ge(consts, 2)
            link(stt(selm[:, :], caus[:, :], 0.0, isc[:, :], ALU.is_ge, ALU.mult))
            link(tt(isc[:, :], selm[:, :], caus[:, :], ALU.add))

            def topk_round(i):
                lo, hi = ((0, 128), (128, 384))[i]
                m8 = st[:, 416 + 8 * i:424 + 8 * i]
                link(nc.vector.max(out=m8, in_=isc[:, lo:hi]))
                link(nc.vector.match_replace(out=isc[:, lo:hi], in_to_replace=m8, in_values=isc[:, lo:hi],
                                             imm_value=TAKEN))

            def cb_out(g):
                dve.wait_ge(cb_ready, g + 1)
                ps = bank[4 + g % 2]
                tt(cbm[:, g, 0:128], ps[:, 0:128], tri[:, :], ALU.mult)
                nc.vector.tensor_copy(cbm[:, g, 128:256], ps[:, 128:256])
                tt(cbm[:, g, 256:384], ps[:, 256:384], tri[:, :], ALU.mult).then_inc(cb_done, 1)

            def decay_biases():
                dve.wait_ge(acs_ready, 1)
                ts_(bias3[:, 0, :], bank[6][:, 0:32], -1.0, None, ALU.mult)
                ts_(bias3[:, 2, :], bank[6][:, 32:64], -1.0, None, ALU.mult)
                nc.vector.tensor_copy(bias3[:, 1, :], bank[6][:, 64:96]).then_inc(acs_done, 1)
                dve.wait_ge(acs_done, 1)
                tt(bias3[:, 1, :], bias3[:, 1, :], bias3[:, 0, :], ALU.add).then_inc(acs_done, 1)

            dve.wait_ge(prm_ready, 2)
            for n in range(24):
                if n % 2 == 0:
                    split_lo_through(UN["bc0"] + n // 2 + 2)
                wait_evac(dve, STEP["bc0"] + n)
                if n >= 2:
                    dve.wait_ge(conv_silu, n - 1)
                rb, cbuf = raw[:, n % 3, :], cacc[:, n % 2, :]
                ch = n + 16 if n < 8 else n - 8
                link(ts_(cbuf, rb[:, 3:259], cw[:, 3, ch:ch + 1], cbias[:, ch:ch + 1], ALU.mult, ALU.add))
                for k in (2, 1):
                    link(stt(cbuf, rb[:, k:k + 256], cw[:, k, ch:ch + 1], cbuf, ALU.mult, ALU.add))
                stt(cbuf, rb[:, 0:256], cw[:, 0, ch:ch + 1], cbuf, ALU.mult, ALU.add).then_inc(conv_done, 1)
                if n >= 12:
                    topk_round(n % 2)
                if n == 15:
                    decay_biases()
                if n in (14, 15, 18, 19):
                    cb_out((14, 15, 18, 19).index(n))
            for j in range(4):
                split_lo_through(UN["q0"] + j + 2)
                if j < 2:
                    topk_round(0)
                    topk_round(1)
                if j == 1:
                    link(ts_(selm[:, :], isc[:, :], TAKEN, -1.0, ALU.is_equal, ALU.add))
                    stt(selm[:, :], selm[:, :], -NEG, caus[:, :], ALU.mult, ALU.add).then_inc(mask_ready, 1)
                for i in range(NT):
                    dve.wait_ge(xt_ready, 2 * j + i + 1)
                    tt(xdt[:, i, 512 * j:512 * j + 512].rearrange("p (h c) -> p h c", c=HEAD),
                       bank[2 + i][:, :].rearrange("p (h c) -> p h c", c=HEAD),
                       dt[:, i, 8 * j:8 * j + 8].unsqueeze(2).to_broadcast([P, 8, HEAD]), ALU.mult)\
                        .then_inc(xdt_done, 1)
            def softmax_in(b):
                dve.wait_ge(sc_ready, b + 1)
                c = 72 + 4 * (b % 2)
                for a in range(2):
                    dve.wait_ge(albi_ready, 2 * b + a + 1)
                    pb = prob[:, 2 * (b % 2) + a, :]
                    if b >= 2:
                        dve.wait_ge(pt_ready, 2 * (b - 1))
                    tt(pb[:, 0:128], bank[4][:, 128 * a:128 * a + 128], albi[:, a, 0:128], ALU.add)
                    tt(pb[:, 128:384], bank[5][:, 256 * a:256 * a + 256], albi[:, a, 128:384], ALU.add)\
                        .then_inc(sc_used, 1)
                dve.wait_ge(sc_used, 2 * b + 2)
                for a in range(2):
                    pb = prob[:, 2 * (b % 2) + a, :]
                    nc.vector.tensor_reduce(out=st[:, c + 2 * a:c + 2 * a + 1], in_=pb[:, 0:128], axis=AXX,
                                            op=ALU.max, negate=True)
                    last = nc.vector.tensor_reduce(out=st[:, c + 2 * a + 1:c + 2 * a + 2], in_=pb[:, 128:384],
                                                   axis=AXX, op=ALU.max, negate=True)
                last.then_inc(mx_ready, 1)

            def sums(b):
                c = 80 + 4 * (b % 2)
                dve.wait_ge(exp_done, b + 1)
                nc.vector.reciprocal(st[:, c + 16:c + 20], st[:, c:c + 4]).then_inc(rcp_ready, 1)

            def probs_out(b):
                for a in range(2):
                    dve.wait_ge(pt_ready, 2 * b + a + 1)
                    if b >= 1:
                        dve.wait_ge(pv_ready, b)
                    nc.vector.tensor_copy(probT[:, a, :], bank[2 + a][:, 0:384]).then_inc(pt_evac, 1)

            def values_lo(b):
                dve.wait_ge(pv_evac, b + 1)
                tt(a_lo[:, b, :], bank[6 + b % 2][:, 0:SEQ], a_hi[:, b, :].bitcast(F32), ALU.subtract)\
                    .then_inc(pv_lo, 1)

            softmax_in(0)
            for b in range(8):
                sums(b)
                if b + 1 < 8:
                    softmax_in(b + 1)
                split_lo_through(UN[f"z{b}"] + 2)
                if b >= 1:
                    values_lo(b - 1)
                probs_out(b)

            def y_out(b):
                dve.wait_ge(y_ready, b + 1)
                stt(ysT[:, b, :], ysT[:, b, :], dskip[:, b:b + 1], bank[6 + b % 2][:, 0:SEQ], ALU.mult, ALU.add)\
                    .then_inc(y_used, 1)

            def gated_lo(b):
                dve.wait_ge(y_hi_done, b + 1)
                dve.wait_ge(sq_ready, b + 1)
                stt(y_lo[:, b, :], ysT[:, b, :], sgain[:, b:b + 1], y_hi[:, b, :].bitcast(F32), ALU.mult, ALU.subtract)\
                    .then_inc(y_lo_done, 1)

            def exponents(b):
                dve.wait_ge(r_ready, b + 1)
                if b == 0:
                    dve.wait_ge(pt_ready, 16)
                if b >= 2:
                    dve.wait_ge(m_ready, 2 * (b - 1))
                for a in range(2):
                    h = 2 * b + a
                    sg = seg[:, 2 * (b % 2) + a, :]
                    rr = bank[4 + b % 2][:, 256 * a:256 * a + 256]
                    ts_(sg[:, 0:128], rr[:, 0:128], bias3[:, 0, h:h + 1], 0.0, ALU.add, ALU.min)
                    ts_(sg[:, 128:256], rr[:, 128:256], bias3[:, 1, h:h + 1], 0.0, ALU.add, ALU.min)
                    ts_(sg[:, 256:384], rr[:, 128:256], bias3[:, 2, h:h + 1], 0.0, ALU.add, ALU.min)\
                        .then_inc(seg_ready, 1)

            exponents(0)
            for b in range(16):
                if b + 1 < 16:
                    exponents(b + 1)
                if b == 0:
                    values_lo(7)
                if b % 2 == 0:
                    split_lo_through(UN[f"g{b // 2}"] + 2)
                if b >= 1:
                    y_out(b - 1)
                if b >= 4:
                    gated_lo(b - 4)
            y_out(15)
            split_lo_through(UN["ao0"] + 2)
            for b in range(12, 16):
                gated_lo(b)
            dve.wait_ge(gsig, 1)

            def att_gate(b):
                n = STEP[f"ao{b}"]
                if b % 2 == 0:
                    split_lo_through(UN[f"ao{b // 2}"] + 2)
                dve.wait_ge(proj_ready, n + 1)
                tt(gates[:, 8 + b, :], bank[n % 2][:, 0:SEQ], gates[:, 8 + b, :], ALU.mult).then_inc(evac_dve, 1)

            for b in range(8):
                att_gate(b)
                if b == 1:
                    dve.wait_ge(ssq_mm, 16)
                    link(ts_(rs_bc, bank[2][:, 0:SEQ], 1.0 / D_INNER, EPS, ALU.mult, ALU.add))
                    nc.vector.reciprocal(rs_bc, rs_bc).then_inc(gn_ms, 1)
                if b == 3:
                    norm_rows(1, memx, memn)
                if b == 5:
                    columns_of(0, g_mem, u_hi, m_lo)
                if b == 7:
                    columns_of(1, g_mem, u_hi, m_lo)
            dve.wait_ge(gn_rstd, 1)
            dve.wait_ge(gsig, 2)
            for b in range(8):
                n = STEP[f"so{b}"]
                split_lo_through(UN[f"so{b}"] + 2)
                link(tt(gates[:, b, :], gates[:, b, :], rs_bc, ALU.mult))
                dve.wait_ge(proj_ready, n + 1)
                if b == 0:
                    dve.wait_ge(pv_lo, 8)
                m = mix_tmp[:, b % 2, :]
                if b >= 2:
                    dve.wait_ge(mix_hi, b - 1)
                tt(m, bank[n % 2][:, 0:SEQ], gates[:, b, :], ALU.mult).then_inc(evac_dve, 1)
                wait_evac(dve, n)
                tt(m, m, gates[:, 8 + b, :], ALU.add).then_inc(mix_ready, 1)
                dve.wait_ge(mix_hi, b + 1)
                tt(a_lo[:, b, :], m, a_hi[:, b, :].bitcast(F32), ALU.subtract).then_inc(mix_lo, 1)

            def residual_and_norm(prefix, nn, dst, between=None):
                split_lo_through(UN[f"{prefix}00"] + 2)
                for c in range(2):
                    for i in range(NT):
                        n = STEP[f"{prefix}{c}{i}"]
                        dve.wait_ge(proj_ready, n + 1)
                        d = xres[:, i, 512 * c:512 * c + 512]
                        tt(d, bank[n % 2][:, :], d, ALU.add).then_inc(evac_dve, 1)
                        split_lo_through(UN[f"{prefix}00"] + 3 + 2 * c + i)
                        if between is not None and c == 1 and i == 1:
                            between()
                        if c == 1:
                            wait_evac(dve, n)
                            dve.wait_ge(ssq_done, 2 * nn - 1 + i)
                            r, k = st[:, 4 * nn + 2 + i:4 * nn + 3 + i], 140 + 4 * (nn - 2) + 2 * i
                            inverse_mean(r, st[:, k:k + 1], st[:, k + 1:k + 2]).then_inc(ms_ready, 1)
                            dve.wait_ge(rstd_done, 2 * nn - 1 + i)
                            ts_(dst[:, i, :], xres[:, i, :], r, None, ALU.mult).then_inc(xn_ready, 1)

            for j in range(4):
                split_lo_through(UN[f"kx{j}"] + 2)
            dve.wait_ge(x_in, 64)
            residual_and_norm("mo", 2, xn1)
            split_lo_through(UN["vx10"])
            columns_of(0, g_x, a_hi, a_lo, NT)
            split_lo_through(UN["qx0"])
            for j in range(4):
                split_lo_through(UN[f"qx{j}"] + 2)

            def cross_lo(h):
                for c in range(2):
                    b = 2 * h + c
                    dve.wait_ge(xo_evac, b + 1)
                    tt(a_lo[:, b, :], bank[6 + c][:, 0:SEQ], a_hi[:, b, :].bitcast(F32), ALU.subtract)\
                        .then_inc(xo_lo, 1)

            for h in range(X_HEADS):
                for i in range(NT):
                    n = NT * h + i
                    dve.wait_ge(xs_ready, n + 1)
                    nc.vector.tensor_reduce(out=st[:, 104 + n:105 + n], in_=bank[4 + i][:, 0:256], axis=AXX,
                                            op=ALU.max, negate=True).then_inc(xmx_ready, 1)
                for i in range(NT):
                    n = NT * h + i
                    dve.wait_ge(xexp_done, n + 1)
                    link(nc.vector.reciprocal(st[:, 120 + n:121 + n], st[:, 112 + n:113 + n]))
                    pb = pX[:, 2 * (h % 2) + i, 0:256]
                    ts_(pb, pb, st[:, 120 + n:121 + n], None, ALU.mult).then_inc(xpn_ready, 1)
                dve.wait_ge(xpt_ready, h + 1)
                if h >= 1:
                    dve.wait_ge(xo_ready, 2 * h)
                nc.vector.tensor_copy(pXT[:, 0, 0:256], bank[2][:, 0:256])
                nc.vector.tensor_copy(pXT[:, 1, 0:256], bank[2][:, 256:512]).then_inc(xpt_evac, 1)
                if h >= 1:
                    cross_lo(h - 1)
            cross_lo(X_HEADS - 1)
            residual_and_norm("xo", 3, xn2, lambda: columns_f32(0, g_moe, tT))
            columns_f32(1, g_moe, tT)

            iota_b = iota64[:, :].unsqueeze(1).to_broadcast([P, 2, CAP])

            def select(col):
                for i in range(NT):
                    pc = pos_all[:, i, bass.ds(col, 2)].unsqueeze(2).to_broadcast([P, 2, CAP])
                    last = tt(S[:, i, :, :], iota_b, pc, ALU.is_equal)
                last.then_inc(m_sel, 1)

            L = rt[:, 0:72].rearrange("p (i n) -> p i n", i=NT)
            dve.wait_ge(rl_ready, 1)
            link(tt(L, bank[4][:, 0:72].rearrange("p (i n) -> p i n", i=NT),
                    brt.unsqueeze(1).to_broadcast([P, NT, 36]), ALU.add))
            glog = L[:, :, 0:4]
            gmx = rt[:, 72:74]
            ge = rt[:, 80:88].rearrange("p (i n) -> p i n", i=NT)
            dexp = rt[:, 96:98]
            oh_g = rt[:, 88:96].rearrange("p (i n) -> p i n", i=NT)
            pg = rt[:, 74:76]
            v1, v2, tmp2 = rt[:, 76:78], rt[:, 78:80], rt[:, 98:100]
            em = rt[:, 104:168].rearrange("p (i n) -> p i n", i=NT)
            oh1 = rt[:, 168:232].rearrange("p (i n) -> p i n", i=NT)
            oh2 = rt[:, 232:296].rearrange("p (i n) -> p i n", i=NT)
            msk = rt[:, 296:360].rearrange("p (i n) -> p i n", i=NT)
            cmb = rt[:, 360:424].rearrange("p (i n) -> p i n", i=NT)
            pm = rt[:, 424:488].rearrange("p (i n) -> p i n", i=NT)

            def over(v, n):
                return v.unsqueeze(2).to_broadcast([P, NT, n])

            def first_max(dst, src, rev, n, vmax):
                link(nc.vector.tensor_reduce(out=vmax, in_=src, axis=AXX, op=ALU.max))
                link(tt(dst, src, over(vmax, n), ALU.is_equal))
                link(tt(dst, dst, rev.unsqueeze(1).to_broadcast([P, NT, n]), ALU.mult))
                link(nc.vector.tensor_reduce(out=tmp2, in_=dst, axis=AXX, op=ALU.max))
                link(tt(dst, dst, over(tmp2, n), ALU.is_equal))

            first_max(oh_g, glog, rev4, GROUPS, gmx)
            tt(ge, glog, over(gmx, GROUPS), ALU.subtract).then_inc(rexp_in, 1)
            link(ts_(oh2[:, :, 0:4], oh_g, -1.0, -NEG, ALU.add, ALU.mult))
            link(tt(em.rearrange("p i (g e) -> p i g e", g=GROUPS),
                    L[:, :, 4:36].rearrange("p i (g e) -> p i g e", g=GROUPS),
                    oh2[:, :, 0:4].unsqueeze(3).to_broadcast([P, NT, GROUPS, PER_GROUP]), ALU.add))
            first_max(oh1, em, rev32, EXPERTS, v1)
            link(stt(em, oh1, 3 * NEG, em, ALU.mult, ALU.add))
            first_max(oh2, em, rev32, EXPERTS, v2)
            tt(dexp, v2, v1, ALU.subtract).then_inc(rexp_in, 1)
            tt(msk, oh1, oh2, ALU.add).then_inc(rmask, 1)
            dve.wait_ge(rexp_done, 1)
            link(nc.vector.tensor_reduce(out=pg, in_=ge, axis=AXX, op=ALU.add))
            link(nc.vector.reciprocal(pg, pg))
            dve.wait_ge(rexp_done, 2)
            link(ts_(tmp2, dexp, 1.0, None, ALU.add))
            link(nc.vector.reciprocal(tmp2, tmp2))
            link(tt(v1, pg, tmp2, ALU.mult))
            link(tt(v2, v1, dexp, ALU.mult))
            link(tt(oh1, oh1, over(v1, EXPERTS), ALU.mult))
            link(tt(oh2, oh2, over(v2, EXPERTS), ALU.mult))
            link(tt(cmb, oh1, oh2, ALU.add))
            nc.vector.memset(pos_all[:, :, MAX_PASSES * EXPERTS:], -1000.0)
            nc.vector.memset(comb_all[:, :, MAX_PASSES * EXPERTS:], 0.0)
            for k in range(MAX_PASSES):
                last = nc.vector.tensor_copy(comb_all[:, :, EXPERTS * k:EXPERTS * k + EXPERTS], cmb)
            link(last)
            dve.wait_ge(rpos, 1)
            link(tt(pm, bank[5][:, 0:64].rearrange("p (i n) -> p i n", i=NT), msk, ALU.mult))
            link(ts_(pos_all[:, :, 0:EXPERTS], pm, -1.0, None, ALU.add))
            select(0)
            for k in range(1, MAX_PASSES):
                ts_(pos_all[:, :, EXPERTS * k:EXPERTS * k + EXPERTS], pm, -1.0 - CAP * k, None, ALU.add)
            link(nc.vector.tensor_reduce(out=rt[:, 500:501], in_=bank[5][:, 64:96], axis=AXX, op=ALU.max))
            link(ts_(rt[:, 501:502], rt[:, 500:501], CAP + 0.5, 1.0, ALU.is_gt, ALU.add))
            for k in range(2, MAX_PASSES):
                link(stt(rt[:, 501:502], rt[:, 500:501], CAP * k + 0.5, rt[:, 501:502], ALU.is_gt, ALU.add))
            ts_(n_it[:, 0:1], rt[:, 501:502], float(PAIRS), None, ALU.mult)
            ts_(n_it[:, 2:3], rt[:, 501:502], float(PAIRS // 2), None, ALU.mult)
            nc.vector.tensor_copy(n_it[:, 1:2], rt[:, 501:502]).then_inc(route_ready, 1)
            dve.wait_ge(route_ready, 1)

            def gathered_out(n):
                dve.wait_ge(m_gath, n)
                for q in range(2):
                    gb = g_moe[:, 4 * q:4 * q + 4].unsqueeze(2).to_broadcast([P, 4, P])
                    last = tt(xg[:, 4 * q:4 * q + 4, :], bank[2 + q][:, :].rearrange("p (k j) -> p k j", k=4), gb,
                              ALU.mult)
                last.then_inc(m_xg, 1)

            n_iter = dve.value_load(n_it[0:1, 0:1], min_val=PAIRS, max_val=PAIRS * MAX_PASSES)
            gathered_out(1)
            with dve.Fori(0, n_iter) as it:
                dve.wait_ge(m_sel, it + 1)
                for i in range(NT):
                    cc = comb_all[:, i, bass.ds(2 * it, 2)].unsqueeze(2).to_broadcast([P, 2, CAP])
                    last = tt(Sw[:, i, :, :], S[:, i, :, :], cc, ALU.mult)
                last.then_inc(m_sw, 1)
                dve.wait_ge(m_sw, it + 1)
                select(2 * it + 2)
                dve.wait_ge(m_silu, it + 1)
                tt(hh, hs, bank[5][:, :], ALU.mult).then_inc(m_h, 1)
                gathered_out(it + 2)
                dve.wait_ge(m_tr, it + 1)
                nc.vector.tensor_copy(hT[:, :, :], bank[4][:, :].rearrange("p (k j) -> p k j", k=4)).then_inc(m_ht, 1)
                nc.vector.tensor_copy(SwT[:, :, :], bank[5][:, 0:256].rearrange("p (i t) -> p i t", i=NT))\
                    .then_inc(m_st, 1)
                dve.wait_ge(down_used, 2 * it + 2)
                nc.vector.tensor_copy(yj[:, 512:1024], bank[3][:, :]).then_inc(m_y1, 1)

            for i in range(NT):
                dve.wait_ge(f_ssq, i + 1)
                inverse_mean(st[:, 136 + i:137 + i], st[:, 128 + 2 * i:129 + 2 * i], st[:, 129 + 2 * i:130 + 2 * i])\
                    .then_inc(f_ms, 1)
            dve.wait_ge(gainf_in, 16)
            for i in range(NT):
                dve.wait_ge(f_rstd, i + 1)
                for c in range(2):
                    last = stt(outb[:, i, 512 * c:512 * c + 512], acc_bank[i][c][:, :], st[:, 136 + i:137 + i],
                               gain_f[:, 512 * c:512 * c + 512], ALU.mult, ALU.mult)
                last.then_inc(f_out, 1)

        @block.tensor
        def _(pe):
            mm, tp = nc.tensor.matmul, nc.tensor.transpose
            group = [0]

            def use_unit(name):
                wait_low(pe, UN[name])
                return parts(name)

            def product(dst, left, right, first, last):
                mm(dst, left[0], right[0], start=first, stop=False)
                mm(dst, left[0], right[1], start=False, stop=False)
                return mm(dst, left[1], right[0], start=False, stop=last)

            u_parts, m_parts, a_parts, y_parts = (u_hi, u_lo), (u_hi, m_lo), (a_hi, a_lo), (y_hi, y_lo)

            def transposes_of(xn, i, split=True):
                pe.wait_ge(xn_ready, group[0] // 2 + 1)
                for q in range(2):
                    g = group[0]
                    if g >= 2:
                        pe.wait_ge(tr_gain if split else tr_evac, g - 1)
                    for k in range(4):
                        last = tp(bank[2 + g % 2][:, P * k:P * k + P], xn[:, i, 4 * q + k::KT], ident[:, :])
                    last.then_inc(tr_ready, 1)
                    group[0] += 1

            def transposes(xn):
                for i in range(NT):
                    transposes_of(xn, i)

            def bank_of(name):
                n = STEP[name]
                if n >= 2:
                    wait_evac(pe, n - 2)
                return bank[n % 2]

            def fm_step(name, w, c0, act_parts, nk=KT):
                b = bank_of(name)
                for k in range(nk):
                    last = product(b[:, 0:SEQ], [x[:, k, c0:c0 + P] for x in w], [x[:, k, :] for x in act_parts],
                                   k == 0, k == nk - 1)
                last.then_inc(proj_ready, 1)

            def tm_steps(prefix, c, act_parts, sem=None, halves=None):
                banks = {}
                for half in range(2):
                    w = use_unit(f"{prefix}{c}{half}")
                    if sem is not None:
                        pe.wait_ge(sem, halves[half])
                    for i in range(NT):
                        if half == 0:
                            banks[i] = bank_of(f"{prefix}{c}{i}")
                        for k in range(4):
                            last = product(banks[i][:, :], [x[:, 4 * half + k, P * i:P * i + P] for x in act_parts],
                                           [x[:, k, :] for x in w], half == 0 and k == 0, half == 1 and k == 3)
                        if half == 1:
                            last.then_inc(proj_ready, 1)

            pe.wait_ge(ident_ready, 1)
            transposes(xn0)
            pe.wait_ge(consts, 1)
            pe.wait_ge(tr_evac, 4)
            w = use_unit("kk")
            fm_step("k", w, 0, u_parts)
            fm_step("ki", w, P, u_parts)
            w = use_unit("tm")
            for i in range(NT):
                b = bank_of(f"tm{i}")
                for k in range(KT):
                    last = product(b[:, 0:TM_W], [x[:, k, P * i:P * i + P] for x in u_parts],
                                   [x[:, k, :] for x in w], k == 0, k == KT - 1)
                last.then_inc(proj_ready, 1)

            pe.wait_ge(prm_in, 16 * N_PRM)
            for k in range(CONV_K):
                tp(bank[4][:, 24 * k:24 * k + 24], cwrow[:, k::CONV_K], ident[0:24, 0:24])
            tp(bank[4][:, 96:136], prow[:, :], ident[0:40, 0:40])
            mm(bank[5][:, 0:16], sel2[:, :], drow[:, :], start=True, stop=True).then_inc(prm_tr, 1)

            def indexer(b):
                wait_evac(pe, f"qi{b}")
                if b == 0:
                    pe.wait_ge(prm_ready, 2)
                else:
                    pe.wait_ge(idx_relu, b)
                mm(bank[4][:, 0:256].rearrange("p (a s) -> p a s", a=2), qiT[:, b, 0:P], kiz[:, :, 0:P],
                   start=True, stop=True)
                mm(bank[5][:, :].rearrange("p (a s) -> p a s", a=2), qiT[:, b, P:SEQ], kiz[:, :, :],
                   start=True, stop=True).then_inc(idx_ready, 1)

            for b in range(4):
                if b % 2 == 0:
                    w = use_unit(f"qi{b // 2}")
                fm_step(f"qi{b}", w, P * (b % 2), u_parts)
                if b >= 1:
                    indexer(b - 1)
            for b in range(8):
                if b % 2 == 0:
                    w = use_unit(f"bc{b // 2}")
                fm_step(f"bc{b}", w, P * (b % 2), u_parts)
                if b == 0:
                    indexer(3)
            for b in range(16):
                if b % 2 == 0:
                    w = use_unit(f"xs{b // 2}")
                fm_step(f"xs{b}", w, P * (b % 2), u_parts)
                if b == 3:
                    pe.wait_ge(dt_ready, 1)
                    mm(bank[6][:, 0:32], tri[:, :], dA[:, 0, :], start=True, stop=True)
                    mm(bank[6][:, 32:64], tri[:, :], dA[:, 1, :], start=True, stop=True)
                    mm(bank[6][:, 64:96], ones[:, :], dA[:, 0, :], start=True, stop=True).then_inc(acs_ready, 1)
                if b in (5, 9):
                    pe.wait_ge(conv_silu, 8)
                    pe.wait_ge(idx_relu, 4)
                    for g in ((0, 1) if b == 5 else (2, 3)):
                        if g >= 2:
                            pe.wait_ge(cb_done, g - 1)
                        mm(bank[4 + g % 2][:, 0:256], bc[:, g, 0:P], bc[:, 4 + g, :], start=True, stop=True)
                        mm(bank[4 + g % 2][:, 256:384], bc[:, g, P:SEQ], bc[:, 4 + g, P:SEQ], start=True,
                           stop=True).then_inc(cb_ready, 1)
            for b in range(8):
                if b % 2 == 0:
                    w = use_unit(f"q{b // 2}")
                fm_step(f"q{b}", w, P * (b % 2), u_parts)
                i, q = b % 2, b // 2
                pe.wait_ge(conv_silu, 8 + 4 * (q + 1))
                if b >= 2:
                    pe.wait_ge(xdt_done, b - 1)
                for c in range(4):
                    last = tp(bank[2 + i][:, P * c:P * c + P], ysT[:, 4 * q + c, P * i:P * i + P], ident[:, :])
                last.then_inc(xt_ready, 1)

            def scores(b):
                wait_evac(pe, f"q{b}")
                if b == 0:
                    pe.wait_ge(cb_done, N_GROUPS)
                else:
                    pe.wait_ge(sc_used, 2 * b)
                mm(bank[4][:, 0:256].rearrange("p (a s) -> p a s", a=2), qT[:, b, 0:P], kz[:, :, 0:P],
                   start=True, stop=True)
                mm(bank[5][:, :].rearrange("p (a s) -> p a s", a=2), qT[:, b, P:SEQ], kz[:, :, :],
                   start=True, stop=True).then_inc(sc_ready, 1)

            def prob_transposes(b):
                for a in range(2):
                    pe.wait_ge((pn_ready, pn_odd)[a], b + 1)
                    if b == 0:
                        pe.wait_ge(xdt_done, 8)
                    else:
                        pe.wait_ge(pt_evac, 2 * (b - 1) + a + 1)
                    pb = prob[:, 2 * (b % 2) + a, :]
                    for c in range(3):
                        last = tp(bank[2 + a][:, P * c:P * c + P], pb[:, P * c:P * c + P], ident[:, :])
                    last.then_inc(pt_ready, 1)

            def weighted_sum(dst, left0, left1, right):
                mm(dst[:, 0:256], left0, right[:, 0:256], start=True, stop=False, skip_group_check=True)
                return mm(dst[:, 128:256], left1, right[:, 256:384], start=False, stop=True, skip_group_check=True)

            def values(b):
                pe.wait_ge(pt_evac, 2 * b + 2)
                if b >= 2:
                    pe.wait_ge(pv_lo, b - 1)
                if b == 0:
                    pe.wait_ge(acs_done, 2)
                for a in range(2):
                    last = weighted_sum(bank[6 + b % 2][64 * a:64 * a + 64, :], small_tm[:, 0, 0:HEAD],
                                        small_tm[:, 1, 0:HEAD], probT[:, a, :])
                last.then_inc(pv_ready, 1)

            scores(0)
            for b in range(8):
                w = use_unit(f"z{b}")
                fm_step(f"z{2 * b}", w, 0, u_parts)
                if b == 0:
                    scores(1)
                if b >= 1:
                    values(b - 1)
                fm_step(f"z{2 * b + 1}", w, P, u_parts)
                if b + 2 < 8:
                    scores(b + 2)
                prob_transposes(b)

            def cumsum_rows(b):
                if b < 2:
                    pe.wait_ge(sc_used, 16)
                else:
                    pe.wait_ge(seg_ready, 2 * (b - 1))
                for a in range(2):
                    for i in range(NT):
                        left = dA[:, i, 2 * b + a:2 * b + a + 1].to_broadcast([P, P])
                        last = mm(bank[4 + b % 2][:, 256 * a + P * i:256 * a + P * i + P], left, tri[:, :],
                                  start=True, stop=True)
                last.then_inc(r_ready, 1)

            def sum_squares(b):
                pe.wait_ge(sq_ready, b + 1)
                mm(bank[2][:, 0:SEQ], ones[:, :], ysq[:, b % 2, :], start=(b == 0), stop=(b == 15))\
                    .then_inc(ssq_mm, 1)

            cumsum_rows(0)
            pe.wait_ge(xdt_done, 8)
            for b in range(16):
                if b + 1 < 16:
                    cumsum_rows(b + 1)
                if b % 2 == 0:
                    w = use_unit(f"g{b // 2}")
                fm_step(f"g{b}", w, P * (b % 2), u_parts)
                if b == 0:
                    values(7)
                pe.wait_ge(m_ready, 2 * b + 2)
                if b >= 2:
                    pe.wait_ge(y_used, b - 1)
                else:
                    pe.wait_ge(pv_lo, 7 + b)
                for a in range(2):
                    h = 2 * b + a
                    last = weighted_sum(bank[6 + b % 2][64 * a:64 * a + 64, :], xdt[:, 0, HEAD * h:HEAD * h + HEAD],
                                        xdt[:, 1, HEAD * h:HEAD * h + HEAD], mdec[:, 2 * ((b + 1) % 2) + a, :])
                last.then_inc(y_ready, 1)
                if b >= 3:
                    sum_squares(b - 3)
            sum_squares(13)

            for b in range(8):
                if b % 2 == 0:
                    w = use_unit(f"ao{b // 2}")
                fm_step(f"ao{b}", w, P * (b % 2), a_parts)
                if b < 2:
                    sum_squares(14 + b)
                if b == 4:
                    pe.wait_ge(gn_ms, 1)
                    transposes_of(memn, 0)
                if b == 6:
                    transposes_of(memn, 1)
            pe.wait_ge(y_lo_done, 16)
            for b in range(8):
                w = use_unit(f"so{b}")
                fm_step(f"so{b}", w, 0, y_parts, 16)
            pe.wait_ge(tr_evac, 8)
            for b in range(8):
                if b % 2 == 0:
                    w = use_unit(f"kx{b // 2}")
                fm_step(f"kx{b}", w, P * (b % 2), m_parts)
            for c in range(2):
                tm_steps("mo", c, a_parts, mix_lo, (4, 8))
            tm_steps("vx", 0, m_parts)
            transposes(xn1)
            tm_steps("vx", 1, m_parts)

            pe.wait_ge(tr_evac, 12)
            for b in range(8):
                if b % 2 == 0:
                    w = use_unit(f"qx{b // 2}")
                fm_step(f"qx{b}", w, P * (b % 2), a_parts)
            wait_evac(pe, "qx7")

            def x_scores(h):
                for i in range(NT):
                    if h == 0:
                        pe.wait_ge(seg_ready, 32)
                    else:
                        pe.wait_ge(xexp_done, NT * (h - 1) + i + 1)
                    for c in range(2):
                        last = mm(bank[4 + i][:, 0:256], qxT[:, 2 * h + c, P * i:P * i + P], kxT[:, 2 * h + c, :],
                                  start=(c == 0), stop=(c == 1))
                    last.then_inc(xs_ready, 1)

            x_scores(0)
            for h in range(X_HEADS):
                if h + 1 < X_HEADS:
                    x_scores(h + 1)
                pe.wait_ge(xpn_ready, NT * (h + 1))
                if h >= 1:
                    pe.wait_ge(xpt_evac, h)
                for m in range(2):
                    for i in range(NT):
                        last = tp(bank[2][:, 256 * m + P * i:256 * m + P * i + P],
                                  pX[:, 2 * (h % 2) + i, P * m:P * m + P], ident[:, :])
                last.then_inc(xpt_ready, 1)
                pe.wait_ge(xpt_evac, h + 1)
                for c in range(2):
                    if h == 0:
                        pe.wait_ge(y_used, 16)
                    else:
                        pe.wait_ge(xo_lo, 2 * (h - 1) + c + 1)
                    for m in range(2):
                        f0 = 256 * h + P * c
                        last = mm(bank[6 + c][:, 0:SEQ], vx[:, m, f0:f0 + P], pXT[:, m, 0:256],
                                  start=(m == 0), stop=(m == 1))
                    last.then_inc(xo_ready, 1)
            for c in range(2):
                tm_steps("xo", c, a_parts, xo_lo, (4, 8))

            pe.wait_ge(xexp_done, 8)
            for i in range(NT):
                transposes_of(xn2, i, split=False)
                pe.wait_ge(tr_evac, 14 + 2 * i)
                for k in range(KT):
                    last = mm(bank[4][:, 36 * i:36 * i + 36], tT[:, k, P * i:P * i + P], wr[:, k, :],
                              start=(k == 0), stop=(k == KT - 1))
            last.then_inc(rl_ready, 1)
            wait_evac(pe, "xo11")
            def residual_sum(i, c):
                return mm(acc_bank[i][c][:, :], ident[:, :], xres[:, i, 512 * c:512 * c + 512], start=True,
                          stop=False, skip_group_check=True)

            for i, c in ((0, 0), (0, 1), (1, 0)):
                residual_sum(i, c)
            pe.wait_ge(rmask, 1)
            m_t = rt[:, 296:360].rearrange("p (i n) -> p i n", i=NT)
            mm(bank[5][:, 0:32], tri[:, :], m_t[:, 0, :], start=True, stop=True)
            mm(bank[5][:, 32:64], ones[:, :], m_t[:, 0, :], start=True, stop=False)
            mm(bank[5][:, 32:64], tri[:, :], m_t[:, 1, :], start=False, stop=True)
            mm(bank[5][:, 64:96], ones[:, :], m_t[:, 0, :], start=True, stop=False)
            mm(bank[5][:, 64:96], ones[:, :], m_t[:, 1, :], start=False, stop=True).then_inc(rpos, 1)
            residual_sum(1, 1).then_inc(residual_in, 1)

            def gather():
                for k in range(KT):
                    for i in range(NT):
                        last = mm(bank[2 + k // 4][:, P * (k % 4):P * (k % 4) + P], xn2[:, i, k::KT],
                                  S[:, i, :, :], start=(i == 0), stop=(i == NT - 1))
                last.then_inc(m_gath, 1)

            def first_layer(ps, slot, turns, used):
                for h in range(2):
                    for a in range(2):
                        pe.wait_ge(moe_landed[slot + a][h], 16 * turns)
                    for k in range(KT // 2 * h, KT // 2 * h + KT // 2):
                        for a in range(2):
                            w = moe_slot[slot + a][h][:, :].rearrange("p (t n) -> p t n", t=KT // 2)
                            last = mm(ps[64 * a:64 * a + 64, :], xg[:, k, CAP * a:CAP * a + CAP],
                                      w[:, k % (KT // 2), :], start=(k == 0), stop=(k == KT - 1))
                    last.then_inc(used, 1)

            def transposes_and_down(it):
                pe.wait_ge(m_h, it + 1)
                for k in range(4):
                    tp(bank[4][:, P * k:P * k + P], hh[:, k::4], ident[:, :])
                pe.wait_ge(m_sw, it + 1)
                for i in range(NT):
                    last = tp(bank[5][:, P * i:P * i + P], Sw[:, i, :, :], ident[:, :])
                last.then_inc(m_tr, 1)
                pe.wait_ge(m_xg, it + 2)
                pe.wait_ge(m_ht, it + 1)
                for h in range(2):
                    for a in range(2):
                        pe.wait_ge(moe_landed[DOWN + a][h], 16 * it + 16)
                    for c in range(2):
                        for k in (2 * h, 2 * h + 1):
                            for a in range(2):
                                w = moe_slot[DOWN + a][h][:, :].rearrange("p (t n) -> p t n", t=2)
                                last = mm(bank[2 + c][64 * a:64 * a + 64, :], hT[:, k, CAP * a:CAP * a + CAP],
                                          w[:, k % 2, 512 * c:512 * c + 512], start=(k == 0), stop=(k == 3))
                    last.then_inc(down_used, 1)

            def scatter(n, done=None):
                pe.wait_ge(m_y0, n)
                pe.wait_ge(m_y1, n)
                pe.wait_ge(m_st, n)
                for i in range(NT):
                    for c in range(2):
                        last = mm(acc_bank[i][c][:, :], SwT[:, i, :], yj[:, 512 * c:512 * c + 512],
                                  start=False, stop=False, skip_group_check=True)
                    if done is not None:
                        last.then_inc(done, 1)

            def pair_of_experts(it, j, odd):
                pe.wait_ge(m_st, it)
                pe.wait_ge(m_xg, it + 1)
                first_layer(bank[4], GATE[odd], j + 1, gate_used)
                scatter(it)
                first_layer(bank[5], UP, it + 1, up_used)
                pe.wait_ge(m_sel, it + 2)
                gather()
                transposes_and_down(it)

            pe.wait_ge(m_sel, 1)
            gather()
            pe.wait_ge(m_xg, 1)
            first_layer(bank[4], GATE[0], 1, gate_used)
            first_layer(bank[5], UP, 1, up_used)
            pe.wait_ge(m_sel, 2)
            gather()
            transposes_and_down(0)
            pair_of_experts(1, 0, 1)
            pe.wait_ge(route_ready, 1)
            n_iter = pe.value_load(n_it[0:1, 0:1], min_val=PAIRS, max_val=PAIRS * MAX_PASSES)
            n_twice = pe.value_load(n_it[0:1, 2:3], min_val=PAIRS // 2, max_val=PAIRS // 2 * MAX_PASSES)
            with pe.Fori(1, n_twice) as j:
                for odd in range(2):
                    pair_of_experts(2 * j + odd, j, odd)
            scatter(n_iter, moe_done)


_INS = ["x", "mem", "norm_mix", "w_in", "conv_w", "conv_b", "dt_bias", "a_log", "d_skip", "ssm_norm",
        "w_ssm_out", "w_att_out", "w_mix_out", "norm_x", "norm_mem", "w_xq", "w_xkv", "w_xo", "norm_moe",
        "w_rg", "b_rg", "w_re", "b_re", "w_e_gate", "w_e_up", "w_e_down", "norm_final"]
_OUTS = [((1, 256, 1024), "float32")]


def kernel(**inputs):
    import numpy as _np
    import concourse.bacc as _bacc
    from concourse import mybir as _mybir
    from concourse.bass_utils import run_bass_kernel_spmd as _run

    nc = _bacc.Bacc("TRN2", target_bir_lowering=False, num_devices=1)
    arrays, args = {}, []
    for name in _INS:
        a = _np.ascontiguousarray(inputs[name])
        arrays[f"in_{name}_dram"] = a
        args.append(nc.dram_tensor(f"in_{name}_dram", a.shape, _mybir.dt.from_np(a.dtype), kind="ExternalInput").ap())
    for i, (shape, dtype) in enumerate(_OUTS):
        dt = _mybir.dt.from_np(_np.dtype(dtype))
        args.append(nc.dram_tensor(f"out_{i}_dram", shape, dt, kind="ExternalOutput").ap())
    hybrid_block(nc, *args)
    r = _run(nc, [arrays], core_ids=[0])
    return r.results[0]["out_0_dram"]
```
